# Optimizing a Trainium2 kernel written in Bass

```python
import jax, jax.numpy as jnp
from jax import lax
import numpy as np

D_MODEL = 1024
BATCH = 1
SEQ = 512
DEPTH = 2

GRID_W = 64
CTX_LEN = 256
HEAD_DIM = 64
ROPE_BASE = 10000.0
EPS = 1e-6
NEG = -1e30
A_Q_HEADS = D_MODEL // (2 * HEAD_DIM)
A_KV_HEADS = 2
WINDOW = 128
BLOCK = 128
B_DV = 128
B_DK = 64
B_HEADS = D_MODEL // (2 * B_DV)
GATE_RANK = 16
GATE_TAU = 16.0
GLA_CHUNK = 64
C_HEADS = D_MODEL // HEAD_DIM
NA_ROWS = 8
NA_COLS = 16
NA_QCOLS = 16
NA_KCOLS = 32
D_FF = -(-8 * D_MODEL // (3 * 256)) * 256

A_Q = A_Q_HEADS * HEAD_DIM
A_KV = A_KV_HEADS * HEAD_DIM
B_QK = B_HEADS * B_DK
B_V = B_HEADS * B_DV
AB_SIZES = (A_Q, A_KV, A_KV, B_QK, B_QK, B_V, B_V, GATE_RANK, GATE_RANK)
AB_SPLITS = [int(s) for s in np.cumsum(AB_SIZES)[:-1]]
AB_IN = int(sum(AB_SIZES))
AB_OUT = A_Q + B_V
N_EVEN = (DEPTH + 1) // 2
N_ODD = DEPTH // 2

kernel_name = "hybrid_window_gla_natten_dit_block"

def rms_norm(x, g):
    xf = x.astype(jnp.float32)
    y = xf * lax.rsqrt(jnp.mean(xf * xf, axis=-1, keepdims=True) + EPS)
    return (y * g.astype(jnp.float32)).astype(x.dtype)

def to_heads(t, n):
    b, s, _ = t.shape
    return t.reshape(b, s, n, -1).transpose(0, 2, 1, 3)

def from_heads(t):
    b, n, s, d = t.shape
    return t.transpose(0, 2, 1, 3).reshape(b, s, n * d)

def axial_angles(T):
    nf = HEAD_DIM // 4
    inv = ROPE_BASE ** (-jnp.arange(nf, dtype=jnp.float32) / nf)
    t = jnp.arange(T)
    row = (t // GRID_W).astype(jnp.float32)
    col = (t % GRID_W).astype(jnp.float32)
    return row[:, None] * inv[None, :], col[:, None] * inv[None, :]

def rope_2d(t, ang_r, ang_c):
    half = t.shape[-1] // 2
    def rot(u, ang):
        u1, u2 = jnp.split(u, 2, axis=-1)
        cos = jnp.cos(ang).astype(u.dtype)
        sin = jnp.sin(ang).astype(u.dtype)
        return jnp.concatenate([u1 * cos - u2 * sin, u2 * cos + u1 * sin], axis=-1)
    return jnp.concatenate([rot(t[..., :half], ang_r), rot(t[..., half:], ang_c)], axis=-1)

def window_attention(q, k, v, qc, kc, vc, sink, need_ctx):
    b, hq, T, dh = q.shape
    hkv = k.shape[1]
    g = hq // hkv
    nb = T // BLOCK
    scale = dh ** -0.5
    qb = q.reshape(b, hkv, g, nb, BLOCK, dh)

    def band(t):
        tp = jnp.pad(t, ((0, 0), (0, 0), (BLOCK, BLOCK), (0, 0))).reshape(b, hkv, nb + 2, BLOCK, dh)
        return jnp.concatenate([tp[:, :, :-2], tp[:, :, 1:-1], tp[:, :, 2:]], axis=3)

    kb, vb = band(k), band(v)
    s_loc = jnp.einsum('bhgnqd,bhnkd->bhgnqk', qb, kb).astype(jnp.float32) * scale
    qpos = jnp.arange(nb)[:, None] * BLOCK + jnp.arange(BLOCK)[None, :]
    kpos = (jnp.arange(nb)[:, None] - 1) * BLOCK + jnp.arange(3 * BLOCK)[None, :]
    valid = ((jnp.abs(qpos[:, :, None] - kpos[:, None, :]) <= WINDOW)
             & (kpos >= 0)[:, None, :] & (kpos < T)[:, None, :])
    s_loc = jnp.where(valid, s_loc, NEG)
    s_ctx = jnp.einsum('bhgnqd,bhld->bhgnql', qb, kc).astype(jnp.float32) * scale
    sink_f = sink.astype(jnp.float32).reshape(1, hkv, g, 1, 1, 1)
    sink_l = jnp.broadcast_to(sink_f, s_loc.shape[:-1] + (1,))
    p = jax.nn.softmax(jnp.concatenate([s_loc, s_ctx, sink_l], axis=-1), axis=-1)
    nk = 3 * BLOCK
    L = kc.shape[2]
    o = (jnp.einsum('bhgnqk,bhnkd->bhgnqd', p[..., :nk].astype(v.dtype), vb)
         + jnp.einsum('bhgnql,bhld->bhgnqd', p[..., nk:nk + L].astype(v.dtype), vc))
    o = o.reshape(b, hq, T, dh)
    oc = None
    if need_ctx:
        qcb = qc.reshape(b, hkv, g, L, dh)
        sc = jnp.einsum('bhgqd,bhkd->bhgqk', qcb, kc).astype(jnp.float32) * scale
        sink_c = jnp.broadcast_to(sink.astype(jnp.float32).reshape(1, hkv, g, 1, 1), sc.shape[:-1] + (1,))
        pc = jax.nn.softmax(jnp.concatenate([sc, sink_c], axis=-1), axis=-1)
        oc = jnp.einsum('bhgqk,bhkd->bhgqd', pc[..., :L].astype(vc.dtype), vc).reshape(b, hq, L, dh)
    return o, oc

def gla_chunked(q, k, v, log_a, s0):
    b, h, T, dk = q.shape
    dv = v.shape[-1]
    n = T // GLA_CHUNK
    r = lambda t: t.reshape(b, h, n, GLA_CHUNK, t.shape[-1])
    q, k, v, la = r(q), r(k), r(v), r(log_a)
    cum = jnp.cumsum(la, axis=3)
    cum_last = cum[:, :, :, -1:, :]
    qg = q * jnp.exp(cum)
    kg = k * jnp.exp(-cum)
    kd = k * jnp.exp(cum_last - cum)
    causal = jnp.tril(jnp.ones((GLA_CHUNK, GLA_CHUNK), dtype=bool))
    att = jnp.where(causal, jnp.einsum('bhncd,bhnsd->bhncs', qg, kg), 0.0)
    o = jnp.einsum('bhncs,bhnsv->bhncv', att, v)
    ds = jnp.einsum('bhncd,bhncv->bhndv', kd, v)
    decay = jnp.exp(cum_last[:, :, :, 0, :])

    def step(s, inp):
        dcy, d = inp
        return dcy[..., None] * s + d, s

    s_fin, s_in = lax.scan(step, s0, (jnp.moveaxis(decay, 2, 0), jnp.moveaxis(ds, 2, 0)))
    s_in = jnp.moveaxis(s_in, 0, 2)
    o = o + jnp.einsum('bhncd,bhndv->bhncv', qg, s_in)
    return o.reshape(b, h, T, dv), s_fin

def gla_final_state(k, v, log_a):
    cum = jnp.cumsum(log_a, axis=2)
    kd = k * jnp.exp(cum[:, :, -1:, :] - cum)
    return jnp.einsum('bhtd,bhtv->bhdv', kd, v)

def bidir_gla(q, k, v, lf, lb, qc, kc, vc, lfc, lbc, need_ctx):
    flip = lambda t: t[:, :, ::-1]
    b, h, _, dk = q.shape
    dv = v.shape[-1]
    oc = None
    if need_ctx:
        zero = jnp.zeros((b, h, dk, dv), jnp.float32)
        oc_f, sc_f = gla_chunked(qc, kc, vc, lfc, zero)
        oc_b, sc_b = gla_chunked(flip(qc), flip(kc), flip(vc), flip(lbc), zero)
        oc = oc_f + flip(oc_b)
    else:
        sc_f = gla_final_state(kc, vc, lfc)
        sc_b = gla_final_state(flip(kc), flip(vc), flip(lbc))
    o_f, _ = gla_chunked(q, k, v, lf, sc_f)
    o_b, _ = gla_chunked(flip(q), flip(k), flip(v), flip(lb), sc_b)
    return o_f + flip(o_b), oc

def parallel_window_gla(hl, hc, w_in, w_out, sink, gf_w, gf_b, gb_w, gb_b, norm_g, ang_r, ang_c, need_ctx):
    def project(h):
        aq, ak, av, bq, bk, bv, bo, rf, rb = jnp.split(h @ w_in, AB_SPLITS, axis=-1)
        log_f = jax.nn.log_sigmoid((rf @ gf_w + gf_b).astype(jnp.float32)) / GATE_TAU
        log_b = jax.nn.log_sigmoid((rb @ gb_w + gb_b).astype(jnp.float32)) / GATE_TAU
        a = (to_heads(aq, A_Q_HEADS), to_heads(ak, A_KV_HEADS), to_heads(av, A_KV_HEADS))
        g = (to_heads(bq, B_HEADS).astype(jnp.float32) * B_DK ** -0.5,
             to_heads(bk, B_HEADS).astype(jnp.float32),
             to_heads(bv, B_HEADS).astype(jnp.float32),
             to_heads(log_f, B_HEADS), to_heads(log_b, B_HEADS))
        return a, g, bo

    (aq, ak, av), (bq, bk, bv, lf, lb), bo = project(hl)
    (aqc, akc, avc), (bqc, bkc, bvc, lfc, lbc), boc = project(hc)
    aq = rope_2d(aq, ang_r, ang_c)
    ak = rope_2d(ak, ang_r, ang_c)
    oa, oac = window_attention(aq, ak, av, aqc, akc, avc, sink, need_ctx)
    ob, obc = bidir_gla(bq, bk, bv, lf, lb, bqc, bkc, bvc, lfc, lbc, need_ctx)

    def gla_out(o, og):
        o = o * lax.rsqrt(jnp.mean(o * o, axis=-1, keepdims=True) + EPS)
        o = o * norm_g.astype(jnp.float32).reshape(B_HEADS, 1, B_DV)
        return from_heads(o).astype(og.dtype) * jax.nn.silu(og)

    yl = jnp.concatenate([from_heads(oa), gla_out(ob, bo)], axis=-1) @ w_out
    yc = None
    if need_ctx:
        yc = jnp.concatenate([from_heads(oac), gla_out(obc, boc)], axis=-1) @ w_out
    return yl, yc

def neighbourhood_attention(q, k, v, kc, vc, rel_bias):
    b, h, T, dh = q.shape
    rows = T // GRID_W
    kh = min(NA_ROWS, rows)
    scale = dh ** -0.5
    n_seg = GRID_W // NA_QCOLS
    kg = k.reshape(b, h, rows, GRID_W, dh)
    vg = v.reshape(b, h, rows, GRID_W, dh)
    qcol = np.arange(GRID_W).reshape(n_seg, NA_QCOLS)
    cs = np.clip(qcol - NA_COLS // 2, 0, GRID_W - NA_COLS)
    seg_start = np.clip(np.arange(n_seg) * NA_QCOLS - NA_COLS // 2, 0, GRID_W - NA_KCOLS)
    keycol = seg_start[:, None] + np.arange(NA_KCOLS)[None, :]
    col_ok = (keycol[:, None, :] >= cs[:, :, None]) & (keycol[:, None, :] < cs[:, :, None] + NA_COLS)
    col_off = np.clip(keycol[:, None, :] - qcol[:, :, None] + NA_COLS - 1, 0, 2 * NA_COLS - 2)
    bias_cols = rel_bias.astype(jnp.float32)[:, :, col_off]
    col_ok = jnp.asarray(col_ok)[:, :, None, :]

    def row_block(args):
        r, q_row = args
        rs = jnp.clip(r - kh // 2, 0, rows - kh)
        k_seg = lax.dynamic_slice_in_dim(kg, rs, kh, axis=2)[:, :, :, keycol]
        v_seg = lax.dynamic_slice_in_dim(vg, rs, kh, axis=2)[:, :, :, keycol]
        q_seg = q_row.reshape(b, h, n_seg, NA_QCOLS, dh)
        s = jnp.einsum('bhjqd,bhrjkd->bhjqrk', q_seg, k_seg).astype(jnp.float32) * scale
        row_off = rs + jnp.arange(kh) - r + NA_ROWS - 1
        bias = bias_cols[:, row_off].transpose(0, 2, 3, 1, 4)
        s = jnp.where(col_ok, s + bias[None], NEG)
        s_loc = s.reshape(b, h, n_seg, NA_QCOLS, kh * NA_KCOLS)
        s_ctx = jnp.einsum('bhjqd,bhld->bhjql', q_seg, kc).astype(jnp.float32) * scale
        p = jax.nn.softmax(jnp.concatenate([s_loc, s_ctx], axis=-1), axis=-1)
        nloc = kh * NA_KCOLS
        p_loc = p[..., :nloc].reshape(b, h, n_seg, NA_QCOLS, kh, NA_KCOLS).astype(v.dtype)
        o = (jnp.einsum('bhjqrk,bhrjkd->bhjqd', p_loc, v_seg)
             + jnp.einsum('bhjql,bhld->bhjqd', p[..., nloc:].astype(vc.dtype), vc))
        return o.reshape(b, h, GRID_W, dh)

    q_rows = jnp.moveaxis(q.reshape(b, h, rows, GRID_W, dh), 2, 0)
    out = lax.map(row_block, (jnp.arange(rows), q_rows))
    return jnp.moveaxis(out, 0, 2).reshape(b, h, T, dh)

def neighbourhood_mixer(hl, hc, w_in, w_out, rel_bias, need_ctx):
    q, k, v = [to_heads(t, C_HEADS) for t in jnp.split(hl @ w_in, 3, axis=-1)]
    qc, kc, vc = [to_heads(t, C_HEADS) for t in jnp.split(hc @ w_in, 3, axis=-1)]
    yl = from_heads(neighbourhood_attention(q, k, v, kc, vc, rel_bias)) @ w_out
    yc = None
    if need_ctx:
        sc = jnp.einsum('bhqd,bhkd->bhqk', qc, kc).astype(jnp.float32) * HEAD_DIM ** -0.5
        pc = jax.nn.softmax(sc, axis=-1).astype(vc.dtype)
        yc = from_heads(jnp.einsum('bhqk,bhkd->bhqd', pc, vc)) @ w_out
    return yl, yc

def swiglu(h, w_in, w_out):
    g, u = jnp.split(h @ w_in, 2, axis=-1)
    return (jax.nn.silu(g) * u) @ w_out

def setup_inputs(seed: int = 0) -> dict:
    key = jax.random.key(seed)
    ks = jax.random.split(key, 24)
    f32 = jnp.float32
    nrm = lambda k, shape, fan_in: jax.random.normal(k, shape, f32) * fan_in ** -0.5
    gain = lambda k, shape: 1.0 + 0.02 * jax.random.normal(k, shape, f32)
    return {
        "x": jax.random.normal(ks[0], (BATCH, SEQ, D_MODEL), f32),
        "c": jax.random.normal(ks[1], (BATCH, D_MODEL), f32),
        "ctx": jax.random.normal(ks[2], (BATCH, CTX_LEN, D_MODEL), f32),
        "c_ctx": jax.random.normal(ks[3], (D_MODEL,), f32),
        "w_mod": 0.5 * nrm(ks[4], (DEPTH, D_MODEL, 6 * D_MODEL), D_MODEL),
        "b_mod": 0.02 * jax.random.normal(ks[5], (DEPTH, 6 * D_MODEL), f32),
        "g_mix_pre": gain(ks[6], (DEPTH, D_MODEL)),
        "g_mix_post": gain(ks[7], (DEPTH, D_MODEL)),
        "g_ffn_pre": gain(ks[8], (DEPTH, D_MODEL)),
        "g_ffn_post": gain(ks[9], (DEPTH, D_MODEL)),
        "w_ffn_in": nrm(ks[10], (DEPTH, D_MODEL, 2 * D_FF), D_MODEL),
        "w_ffn_out": nrm(ks[11], (DEPTH, D_FF, D_MODEL), D_FF),
        "ab_w_in": nrm(ks[12], (N_EVEN, D_MODEL, AB_IN), D_MODEL),
        "ab_w_out": nrm(ks[13], (N_EVEN, AB_OUT, D_MODEL), AB_OUT),
        "a_sink": jax.random.normal(ks[14], (N_EVEN, A_Q_HEADS), f32),
        "gla_gate_f_w": nrm(ks[15], (N_EVEN, GATE_RANK, B_QK), GATE_RANK),
        "gla_gate_f_b": 0.1 * jax.random.normal(ks[16], (N_EVEN, B_QK), f32),
        "gla_gate_b_w": nrm(ks[17], (N_EVEN, GATE_RANK, B_QK), GATE_RANK),
        "gla_gate_b_b": 0.1 * jax.random.normal(ks[18], (N_EVEN, B_QK), f32),
        "gla_norm_g": gain(ks[19], (N_EVEN, B_V)),
        "na_w_in": nrm(ks[20], (N_ODD, D_MODEL, 3 * D_MODEL), D_MODEL),
        "na_w_out": nrm(ks[21], (N_ODD, D_MODEL, D_MODEL), D_MODEL),
        "na_rel_bias": 0.1 * jax.random.normal(ks[22], (N_ODD, C_HEADS, 2 * NA_ROWS - 1, 2 * NA_COLS - 1), f32),
    }

def reference(x, c, ctx, c_ctx, w_mod, b_mod, g_mix_pre, g_mix_post, g_ffn_pre, g_ffn_post,
              w_ffn_in, w_ffn_out, ab_w_in, ab_w_out, a_sink, gla_gate_f_w, gla_gate_f_b,
              gla_gate_b_w, gla_gate_b_b, gla_norm_g, na_w_in, na_w_out, na_rel_bias):
    T = x.shape[1]
    ang_r, ang_c = axial_angles(T)
    xl, xc = x, ctx
    for i in range(DEPTH):
        need_ctx = i < DEPTH - 1
        ml = (jax.nn.silu(c) @ w_mod[i] + b_mod[i])[:, None, :]
        mc = jax.nn.silu(c_ctx) @ w_mod[i] + b_mod[i]
        sh1, sc1, gt1, sh2, sc2, gt2 = jnp.split(ml, 6, axis=-1)
        csh1, csc1, cgt1, csh2, csc2, cgt2 = jnp.split(mc, 6, axis=-1)
        hl = rms_norm(xl, g_mix_pre[i]) * (1.0 + sc1) + sh1
        hc = rms_norm(xc, g_mix_pre[i]) * (1.0 + csc1) + csh1
        if i % 2 == 0:
            j = i // 2
            yl, yc = parallel_window_gla(hl, hc, ab_w_in[j], ab_w_out[j], a_sink[j],
                                         gla_gate_f_w[j], gla_gate_f_b[j], gla_gate_b_w[j], gla_gate_b_b[j],
                                         gla_norm_g[j], ang_r, ang_c, need_ctx)
        else:
            j = i // 2
            yl, yc = neighbourhood_mixer(hl, hc, na_w_in[j], na_w_out[j], na_rel_bias[j], need_ctx)
        xl = xl + gt1 * rms_norm(yl, g_mix_post[i])
        fl = swiglu(rms_norm(xl, g_ffn_pre[i]) * (1.0 + sc2) + sh2, w_ffn_in[i], w_ffn_out[i])
        xl = xl + gt2 * rms_norm(fl, g_ffn_post[i])
        if need_ctx:
            xc = xc + cgt1 * rms_norm(yc, g_mix_post[i])
            fc = swiglu(rms_norm(xc, g_ffn_pre[i]) * (1.0 + csc2) + csh2, w_ffn_in[i], w_ffn_out[i])
            xc = xc + cgt2 * rms_norm(fc, g_ffn_post[i])
    return xl


_drawn_inputs = setup_inputs


def setup_inputs(seed=0):
    import zlib

    import numpy as np

    out = dict(_drawn_inputs(seed))
    spreads = {}
    factors = {'g_mix_pre': 4.401,
     'g_mix_post': 7.03,
     'g_ffn_pre': 5.18,
     'g_ffn_post': 7.042,
     'a_sink': 64.0,
     'gla_gate_f_b': 5.285,
     'gla_gate_b_b': 6.475,
     'gla_norm_g': 8.0,
     'na_rel_bias': 8.0}
    for name, (base, spread) in spreads.items():
        noise = np.random.default_rng([zlib.crc32(name.encode()), seed]).standard_normal(out[name].shape)
        drawn = base * np.exp(spread * noise) if base else spread * noise
        out[name] = __import__('jax').numpy.asarray(drawn.astype(out[name].dtype))
    for name, factor in factors.items():
        out[name] = (out[name] * factor).astype(out[name].dtype)
    return out
```

```python
from contextlib import ExitStack

import numpy as np

import concourse.bass as bass
from concourse import mybir

F32, F32R, BF16 = mybir.dt.float32, mybir.dt.float32r, mybir.dt.bfloat16
ALU, ACT = mybir.AluOpType, mybir.ActivationFunctionType
AX = mybir.AxisListType.X

P = 128
D = 1024
KT = D // P
SEQ, CTX = 512, 256
LT, CT = SEQ // P, CTX // P
NT = LT + CT
TOK = SEQ + CTX
DFF = 2816
FT = DFF // P
FH = FT // 2
AQ, AKV, BQK, BV, RANK = 512, 128, 256, 512, 16
C_AQ, C_AK, C_AV = 0, AQ, AQ + AKV
C_BQ = C_AV + AKV
C_BK = C_BQ + BQK
C_BV = C_BK + BQK
C_BO = C_BV + BV
AB_IN = C_BO + BV + 2 * RANK
CH = 64
GRID = 64
EPS = 1e-6
NEG = -1e30
SCALE = 0.125
RAW, RING = 3, 2
BIAS_ROW = 31
BIAS_HEAD = 15 * BIAS_ROW
BIAS_PAD = 16
BIAS_RUN = 7 * BIAS_ROW + 48
L_TILES, C_TILES = list(range(LT)), list(range(LT, NT))
UNIT = 1024


def constants():
    nf = 16
    inv = (10000.0 ** (-np.arange(nf, dtype=np.float32) / nf)).astype(np.float32)
    t = np.arange(SEQ)
    ang = [(t // GRID).astype(np.float32)[None] * inv[:, None], (t % GRID).astype(np.float32)[None] * inv[:, None]]
    cos, sin = np.zeros((P, SEQ), np.float32), np.zeros((P, SEQ), np.float32)
    for p in range(P):
        a = ang[(p % 64) // 32][p % 16]
        cos[p] = np.cos(a)
        sin[p] = np.sin(a) * (-1.0 if p % 32 < 16 else 1.0)
    q, k = np.arange(P)[:, None], np.arange(P)[None]
    window = np.concatenate([np.where(k >= q, 0.0, NEG), np.where(k <= q, 0.0, NEG)], 1).astype(np.float32)
    col = lambda i: 8 * (i // 64) + i % 8
    near = np.full((P, LT, 3 * P), NEG, np.float32)
    for tile in range(LT):
        qc = 16 * tile + col(np.arange(P))
        cs = np.clip(qc - 8, 0, GRID - 16)[:, None]
        for d in range(3):
            kc = (16 * (tile + d - 1) + col(np.arange(P)))[None]
            near[:, tile, d * P:(d + 1) * P] = np.where((kc >= cs) & (kc < cs + 16), 0.0, NEG)
    same = (q // CH) == (k // CH)
    tri = np.stack([same & (q <= k), same & (q >= k)], 1).astype(np.float32)
    return {"k_ident": np.eye(P, dtype=np.float32), "k_cos": cos, "k_sin": sin, "k_window": window,
            "k_near": near.reshape(P, LT * 3 * P), "k_tri": tri.reshape(P, 2 * P)}


def weight_units(a):
    units = []
    start = {}

    def begin(name):
        start[name] = len(units)

    def fm(w, parts):
        src = w.rearrange("(k p) n -> p k n", p=P)
        units.append((False, [("fm", at, width, src[:, :, c:c + width]) for at, c, width in parts]))

    def tm(w, k, parts):
        units.append((False, [("tm", at, width, w[k * P:(k + 1) * P, c:c + width]) for at, c, width in parts]))

    def mod(block):
        begin(("mod", block))
        l, i = divmod(block, 6)
        for k in range(KT):
            units.append((True, [("tm", 0, D, a["w_mod"][l, k * P:(k + 1) * P, i * D:(i + 1) * D])]))

    def ffn_in(name, l, js):
        begin(name)
        for j in js:
            fm(a["w_ffn_in"][l], [(0, j * P, P)])
            fm(a["w_ffn_in"][l], [(0, DFF + j * P, P)])

    def rows(name, w, ks):
        begin(name)
        for k in ks:
            tm(w, k, [(0, 0, D)])

    mod(0), mod(1)
    w = a["ab_w_in"][0]
    begin("v0")
    for k in range(KT):
        tm(w, k, [(0, C_AV, AKV), (AKV, C_BV, BV)])
    begin("in0")
    for j in range(4):
        fm(w, [(0, C_AQ + j * P, P)])
    for j in range(2):
        fm(w, [(0, C_AK + 64 * j, 64), (64, C_AK + 64 * j, 64)])
    for c, n in ((C_BQ, 2), (C_BK, 2), (C_BO, 4)):
        for j in range(n):
            fm(w, [(0, c + j * P, P)])
    fm(w, [(0, AB_IN - P, P)])
    for b in range(2, 6):
        mod(b)
    rows("out0L", a["ab_w_out"][0], range(KT))
    rows("out0C", a["ab_w_out"][0], range(KT))
    for half in range(2):
        ffn_in(("fi0L", half), 0, range(FH * half, FH * half + FH))
        rows(("fo0L", half), a["w_ffn_out"][0], range(FH * half, FH * half + FH))
    ffn_in("fi0C", 0, range(FT))
    rows("fo0C", a["w_ffn_out"][0], range(FT))
    for b in range(6, 12):
        mod(b)
    w = a["na_w_in"][0]
    begin("qk1")
    for j in range(16):
        fm(w, [(0, j * P, P)])
    begin("v1L")
    for k in range(KT):
        tm(w, k, [(0, 2 * D, D)])
    begin("v1C")
    for k in range(KT):
        tm(w, k, [(0, 2 * D, D)])
    rows("out1L", a["na_w_out"][0], range(KT))
    for half in range(2):
        ffn_in(("fi1L", half), 1, range(FH * half, FH * half + FH))
        rows(("fo1L", half), a["w_ffn_out"][1], range(FH * half, FH * half + FH))
    return units, start


def attention_steps(layer):
    if layer == 0:
        return [(t, 0, h) for t in range(NT) for h in range(8)]
    return [(t, g, h) for g in range(2) for t in range(LT) for h in range(8)]


def local_tiles(t):
    return [u for u in (t - 1, t, t + 1) if 0 <= u < LT] if t < LT else []


def build(nc, a, out):
    units, start = weight_units(a)
    split_no, direct_no, n_split, n_direct = [], [], 0, 0
    for direct, _ in units:
        split_no.append(n_split)
        direct_no.append(n_direct)
        n_split += not direct
        n_direct += direct
    run_end = [0] * n_split
    last = None
    for u in range(len(units) - 1, -1, -1):
        if units[u][0]:
            last = None
        else:
            last = split_no[u] if last is None else last
            run_end[split_no[u]] = last
    landed_value, count = [], [0] * RAW
    for u, (_, parts) in enumerate(units):
        count[u % RAW] += 16 * len(parts)
        landed_value.append(count[u % RAW])
    unit_of_split = [u for u, x in enumerate(units) if not x[0]]

    def sp(name):
        return split_no[start[name]]

    with ExitStack() as ctx:
        def sb(name, shape, dt=F32, scope=ctx):
            return scope.enter_context(nc.sbuf_tensor(name, shape, dt))

        x_res = sb("x_res", [P, NT, D])
        h_hi = sb("h_hi", [P, KT, TOK], F32R)
        h_lo = sb("h_lo", [P, KT, TOK], F32R)
        w_raw = sb("w_raw", [P, RAW, UNIT])
        w_hi = sb("w_hi", [P, RING, UNIT], F32R)
        w_lo = sb("w_lo", [P, RING, UNIT], F32R)
        with ExitStack() as early:
            state = sb("state", [P, 12, 4, P], scope=early)
        gate_b = sb("gate_b", [P, 2, D])
        xs = sb("xs", [P, 2, D])
        full = sb("full", [P, KT, P])
        post_t = sb("post_t", [P, D])
        ident = sb("ident", [P, P])
        ident_b = sb("ident_b", [P, P], BF16)
        window_b = sb("window_b", [P, 2 * P], BF16)
        near_b = sb("near_b", [P, LT, 3 * P], BF16)
        tri = sb("tri", [P, 2, P])
        junk = sb("junk", [P, D], BF16)
        mod_rows = sb("mod_rows", [2, D])
        bias_col = sb("bias_col", [P, 96])
        par_col = sb("par_col", [P, 84])
        c_col = sb("c_col", [P, KT, 2])
        mod_col = sb("mod_col", [P, 12, 2, KT])
        pre_a = sb("pre_a", [P, 4, 2, KT])
        gate_col = sb("gate_col", [P, 4, 2, KT])
        half_neg = sb("half_neg", [P, 8])
        one_col = sb("one_col", [P, 1])
        sink = sb("sink", [P, 8])
        nsink = sb("nsink", [P, 8])
        negm = sb("negm", [P, 2, 8])
        rowsum = sb("rowsum", [P, 2, 8])
        sm = sb("sm", [P, 4, 8])
        raw_max = sb("raw_max", [P, 2])
        ssq_pre, ms_pre, rs_pre = (sb(n, [P, 24]) for n in ("ssq_pre", "ms_pre", "rs_pre"))
        ssq_post, ms_post, rs_post = (sb(n, [P, 24]) for n in ("ssq_post", "ms_post", "rs_post"))
        gla_ssq, gla_ms, gla_rs = (sb(n, [P, NT, 4]) for n in ("gla_ssq", "gla_ms", "gla_rs"))
        decay = sb("decay", [P, 4, 2 * NT])

        with ExitStack() as s0:
            par_rows = sb("par_rows", [P, 2, P], scope=s0)
            mask_in = sb("mask_in", [P, 2 * P + LT * 3 * P], scope=s0)
            sb("fence0", [P, 64], scope=s0)
        with ExitStack() as s1:
            b_q = sb("b_q", [P, 2, TOK], scope=s1)
            b_k = sb("b_k", [P, 2, TOK], scope=s1)
            b_v = sb("b_v", [P, NT, BV], scope=s1)
            b_o = sb("b_o", [P, 4, TOK], scope=s1)
            r_t = sb("r_t", [33, TOK], scope=s1)
            gw = sb("gw", [33, 2 * BQK], scope=s1)
            with ExitStack() as s2:
                cos = sb("cos", [P, SEQ], scope=s2)
                sin = sb("sin", [P, SEQ], scope=s2)
                rope_t = sb("rope_t", [P, 2, SEQ], scope=s2)
                a_q = sb("a_q", [P, 4, TOK], scope=s2)
                a_k = sb("a_k", [P, 2, TOK], scope=s2)
                a_v = sb("a_v", [P, NT, AKV], scope=s2)
                prob0 = sb("prob0", [P, 2, 5 * P], scope=s2)
                prob0_t = sb("prob0_t", [P, 2, 5 * P], scope=s2)
            with ExitStack() as s2:
                with ExitStack() as s3:
                    la = sb("la", [P, NT, 2 * BQK], scope=s3)
                kg_t = sb("kg_t", [P, NT, 2 * BQK], scope=s2)
                qg = sb("qg", [P, 4, TOK], scope=s2)
                kg = sb("kg", [P, 4, TOK], scope=s2)
                att_m = sb("att_m", [P, 2, 4 * P], scope=s2)
        with ExitStack() as s1:
            hid_hi = sb("hid_hi", [P, FH * SEQ], F32R, scope=s1)
            hid_lo = sb("hid_lo", [P, FH * SEQ], F32R, scope=s1)
            y_half = sb("y_half", [P, LT, D], scope=s1)
            silu_g = sb("silu_g", [P, 2, SEQ], scope=s1)
            hid_f = sb("hid_f", [P, 2, SEQ], scope=s1)
        with ExitStack() as s1:
            c_q = sb("c_q", [P, KT, SEQ], scope=s1)
            c_k = sb("c_k", [P, KT, TOK], scope=s1)
            c_v = sb("c_v", [P, NT, D], scope=s1)
            rel = sb("rel", [P, 8, BIAS_RUN], scope=s1)
            prob1 = sb("prob1", [P, 2, 5 * P], scope=s1)
            prob1_t = sb("prob1_t", [P, 2, 5 * P], scope=s1)

        PS = ctx.enter_context(nc.psum_tensor("ps", [P, 8, 512], F32))

        def ps(bank, lo, hi, p0=0, p1=P):
            return PS[p0:p1].rearrange("p b n -> p (b n)")[:, bank * 512 + lo:bank * 512 + hi]

        def sem(name):
            return ctx.enter_context(nc.semaphore(name))

        landed = [sem(f"w_landed{i}") for i in range(RAW)]
        (consts_in, par_in, x_in, gw_zero, gw_in, rel_in, stored) = map(sem, (
            "consts_in", "par_in", "x_in", "gw_zero", "gw_in", "rel_in", "stored"))
        (w_hi_done, w_lo_done, w_used, w_direct, tm_done) = map(sem, (
            "w_hi_done", "w_lo_done", "w_used", "w_direct", "tm_done"))
        (small_done, par_turned, par_done, c_done) = map(sem, ("small_done", "par_turned", "par_done", "c_done"))
        (mod_copied, mod_turned, mod_done, mod_der) = map(sem, ("mod_copied", "mod_turned", "mod_done", "mod_der"))
        (gb_ready, gb_done) = map(sem, ("gb_ready", "gb_done"))
        (pre_ssq, pre_ms, pre_rs, pre_xs, pre_tr, pre_full, pre_hi, pre_lo) = map(sem, (
            "pre_ssq", "pre_ms", "pre_rs", "pre_xs", "pre_tr", "pre_full", "pre_hi", "pre_lo"))
        (post_y, post_ssq, post_ms, post_rs, post_n, post_x) = map(sem, (
            "post_y", "post_ssq", "post_ms", "post_rs", "post_n", "post_x"))
        (v_act, v_dve, fe_act, fe_dve, rope_m, rope_done, bo_done, fe1_act) = map(sem, (
            "v_act", "v_dve", "fe_act", "fe_dve", "rope_m", "rope_done", "bo_done", "fe1_act"))
        (ff_silu, ff_full, ff_hi, ff_lo, half_done) = map(sem, ("ff_silu", "ff_full", "ff_hi", "ff_lo", "half_done"))
        (at_s, at_r, at_m, at_p, at_t, at_e, at_o) = map(sem, (
            "at_s", "at_r", "at_m", "at_p", "at_t", "at_e", "at_o"))
        (at_shift, at_sink, at_den, at_rinv, at_on, at_f, at_hi, at_lo) = map(sem, (
            "at_shift", "at_sink", "at_den", "at_rinv", "at_on", "at_f", "at_hi", "at_lo"))
        (gl_z, gl_abs, gl_exp, gl_ln, gl_la, gl_cum, gl_eq, gl_ek, gl_dec, gl_q, gl_k, gl_kt, gl_ktc) = map(sem, (
            "gl_z", "gl_abs", "gl_exp", "gl_ln", "gl_la", "gl_cum", "gl_eq", "gl_ek", "gl_dec", "gl_q", "gl_k",
            "gl_kt", "gl_ktc"))
        (gl_ds, gl_u, gl_s, gl_att, gl_msk, gl_o, gl_ssq, gl_ms, gl_rs, gl_on, gl_f, gl_full, gl_hi, gl_lo) = map(
            sem, ("gl_ds", "gl_u", "gl_s", "gl_att", "gl_msk", "gl_o", "gl_ssq", "gl_ms", "gl_rs", "gl_on", "gl_f",
                  "gl_full", "gl_hi", "gl_lo"))

        TM = [("v0", 6), ("out0L", 4), ("out0C", 2), (("fo0L", 0), 4), (("fo0L", 1), 4), ("fo0C", 2), ("v1L", 4),
              ("v1C", 2), ("out1L", 4), (("fo1L", 0), 4), (("fo1L", 1), 4)]
        tm_base, n = {}, 0
        for name, tiles in TM:
            tm_base[name] = (n, tiles)
            n += tiles - 1
        PRE = {"mix0": 0, "ffn0L": 6, "ffn0C": 10, "mix1": 12, "ffn1L": 18}
        POST = {"out0L": 0, "out0C": 4, "fo0L": 6, "fo0C": 10, "out1L": 12, "fo1L": 16}
        FI = {("fi0L", 0): 0, ("fi0L", 1): FH, "fi0C": 2 * FH, ("fi1L", 0): 4 * FH, ("fi1L", 1): 5 * FH}
        n_groups = {0: NT, 1: 2 * LT}
        STEPS = {0: attention_steps(0), 1: attention_steps(1)}
        STEP0 = {0: 0, 1: len(STEPS[0])}
        GROUP0 = {0: 0, 1: n_groups[0]}
        f_order = [8, 9, 10, 11, 0, 1, 2, 3, 4, 5, 6, 7]
        b_order = [11, 10, 9, 8, 7, 6, 5, 4, 3, 2, 1, 0]

        def wait_tm(eng, name, i, k_units):
            base, tiles = tm_base[name]
            if i == tiles - 1:
                eng.wait_ge(w_used, sp(name) + k_units)
            else:
                eng.wait_ge(tm_done, base + i + 1)

        def bcast(ap, n):
            return bass.AP(ap.tensor, ap.offset, [list(x) for x in ap.ap] + [[0, n]])

        def group_out(layer, t, g, f):
            if layer == 0:
                return lambda h: h[:, 4 * g + f, t * P:(t + 1) * P], lambda x: x
            return (lambda h: h[:, 4 * g + f, 0:SEQ].rearrange("p (r b c) -> p b r c", b=8, c=8)[:, 2 * t:2 * t + 2],
                    lambda x: x.rearrange("p (b r c) -> p b r c", b=2, c=8))

        def grid_order(h, k, t):
            return h[:, k, 0:SEQ].rearrange("p (b r c) -> p r b c", b=8, c=8)[:, 2 * t:2 * t + 2]

        def rel_load(g, part=0):
            b, r = divmod(part, 8)
            p = 64 * b + 8 * r
            first = BIAS_PAD + (8 * g + 7) * BIAS_HEAD + (7 - r) * BIAS_ROW - 1 - 8 * b
            first = 2 * BIAS_PAD + 16 * BIAS_HEAD - 1 - (first + BIAS_RUN - 1)
            return rel[p:p + 8], bass.AP(a["rel_rev"].tensor, first, [[1, 8], [BIAS_HEAD, 8], [1, BIAS_RUN]])

        gb_base, gb_after = [0, 2, 4, 5], [0, 6, 12, 16]
        gb_need = {"out0L": (1, 2), "out0C": (1, 2), "fo0L": (3, 4), "fo0C": (3, 4), "out1L": (5, 5), "fo1L": (6, 6)}
        tm_name = {"out0L": "out0L", "out0C": "out0C", "fo0C": "fo0C", "out1L": "out1L"}
        n_y = {"fo0L": 0, "fo1L": LT}

        def s_cols(layer, a):
            t = STEPS[layer][a][0]
            return (len(local_tiles(t)) + CT) * P

        block = ctx.enter_context(nc.Block())

        @block.sync
        def _(sync):
            for dst, src in ((ident[:], a["k_ident"]), (tri[:].rearrange("p a n -> p (a n)"), a["k_tri"]),
                             (mask_in[:, 0:2 * P], a["k_window"]), (mask_in[:, 2 * P:], a["k_near"]),
                             (cos[:], a["k_cos"]), (sin[:], a["k_sin"])):
                sync.dma_start(dst, src).then_inc(consts_in, 16)
            sync.dma_start(par_rows[0:96, 0, :], a["b_mod"].rearrange("l (r n) -> (l r) n", n=P)).then_inc(par_in, 16)
            at = 0
            for name in ("g_mix_pre", "g_mix_post", "g_ffn_pre", "g_ffn_post", "gla_norm_g"):
                src = a[name].rearrange("l (r n) -> (l r) n", n=P)
                n = src.shape[0]
                sync.dma_start(par_rows[at:at + n, 1, :], src).then_inc(par_in, 16)
                at += n
            for src in (a["c"].rearrange("b (r n) -> (b r) n", n=P), a["c_ctx"].rearrange("(r n) -> r n", n=P)):
                sync.dma_start(par_rows[at:at + KT, 1, :], src).then_inc(par_in, 16)
                at += KT
            sync.dma_start(sink[:], a["a_sink"].partition_broadcast(P)).then_inc(par_in, 16)
            sync.dma_start(x_res[:, 0:LT, :], a["x"][0].rearrange("(t p) d -> p t d", p=P)).then_inc(x_in, 16)
            sync.dma_start(x_res[:, LT:NT, :], a["ctx"][0].rearrange("(t p) d -> p t d", p=P)).then_inc(x_in, 16)
            for u, (direct, parts) in enumerate(units):
                if u >= RAW:
                    v = u - RAW
                    if units[v][0]:
                        sync.wait_ge(w_direct, direct_no[v] + 1)
                    else:
                        sync.wait_ge(w_hi_done, split_no[v] + 1)
                        sync.wait_ge(w_lo_done, split_no[v] + 1)
                for kind, at, width, src in parts:
                    dst = w_raw[:, u % RAW, :]
                    if kind == "fm":
                        dst = dst.rearrange("p (k n) -> p k n", k=KT)
                        dst = dst[:, :, at:at + width]
                    else:
                        dst = dst[:, at:at + width]
                    sync.dma_start(dst, src).then_inc(landed[u % RAW], 16)
            for t in L_TILES:
                sync.wait_ge(post_x, POST["fo1L"] + t + 1)
                sync.dma_start(out[0, t * P:(t + 1) * P, :], x_res[:, t, :]).then_inc(stored, 16)
            sync.wait_ge(stored, 16 * LT)

        @block.gpsimd
        def _(pool):
            pool.memset(half_neg[:], -0.5).then_inc(small_done, 1)
            pool.memset(one_col[:], 1.0).then_inc(small_done, 1)
            pool.wait_ge(small_done, 2)
            fed = [0]

            def feed(s, name):
                while fed[0] <= min(s, run_end[sp(name)]):
                    u = fed[0]
                    raw = unit_of_split[u]
                    width = sum(w for _, _, w, _ in units[raw][1]) * (KT if units[raw][1][0][0] == "fm" else 1)
                    pool.wait_ge(w_hi_done, u + 1)
                    if u >= RING:
                        pool.wait_ge(w_used, u - RING + 1)
                    pool.tensor_tensor(w_lo[:, u % RING, 0:width], w_raw[:, raw % RAW, 0:width],
                                       w_hi[:, u % RING, 0:width].bitcast(F32), ALU.subtract).then_inc(w_lo_done, 1)
                    fed[0] += 1

            def root(ssq, m, r, width, n_done, s_ssq, s_ms, s_rs, sums=1):
                pool.wait_ge(s_ssq, sums * (n_done + 1))
                pool.tensor_scalar(m, ssq, 1.0 / width, EPS, ALU.mult, ALU.add).then_inc(s_ms, 1)
                pool.wait_ge(s_ms, n_done + 1)
                pool.tensor_tensor(r, m, half_neg[:, 0:m.shape[1]], ALU.pow).then_inc(s_rs, 1)

            def pre(name, i):
                n = PRE[name] + i
                root(ssq_pre[:, n:n + 1], ms_pre[:, n:n + 1], rs_pre[:, n:n + 1], D, n, pre_ssq, pre_ms, pre_rs)

            def post(name, i):
                n = POST[name] + i
                root(ssq_post[:, n:n + 1], ms_post[:, n:n + 1], rs_post[:, n:n + 1], D, n,
                     post_ssq, post_ms, post_rs)

            for i in range(NT):
                pre("mix0", i)
            feed(sp("in0") + 14, "v0")
            for t in range(NT):
                root(gla_ssq[:, t, :], gla_ms[:, t, :], gla_rs[:, t, :], P, t, gl_ssq, gl_ms, gl_rs, 4)
            feed(sp("out0C") + 1, "out0L")
            for i in range(LT):
                post("out0L", i)
                feed(sp("out0C") + i, "out0L")
            for i in range(LT):
                pre("ffn0L", i)
                feed(sp("out0C") + 4 + i, "out0L")
            feed(sp(("fi0L", 0)) + 1, "out0L")
            for i in range(CT):
                post("out0C", i)
            for i in range(CT):
                pre("ffn0C", i)
            feed(sp("fi0C") + 1, "out0L")
            for j in range(2 * LT):
                feed(sp("fi0C") + 2 * j + 3, "out0L")
                post("fo0L", j) if j < LT else pre("mix1", j - LT)
            feed(sp("fo0C") + FT - 1, "out0L")
            for i in range(CT):
                post("fo0C", i)
            for i in range(CT):
                pre("mix1", LT + i)
            feed(sp("out1L") + 7, "qk1")
            feed(sp(("fi1L", 0)) + 1, "qk1")
            for i in range(LT):
                post("out1L", i)
            for i in range(LT):
                pre("ffn1L", i)
            feed(sp(("fo1L", 1)) + FH - 1, "qk1")
            for i in range(LT):
                post("fo1L", i)

        @block.scalar
        def _(act):
            fed = [0]
            junk_written = []

            def square(src, ssq, done, value):
                if junk_written:
                    act.wait_ge(*junk_written.pop())
                act.activation(junk[:, 0:src.shape[1]], src, ACT.Square, accum_out=ssq).then_inc(done, 1)
                junk_written.append((done, value))

            def feed(s, name):
                while fed[0] <= min(s, run_end[sp(name)]):
                    u = fed[0]
                    raw = unit_of_split[u]
                    width = sum(w for _, _, w, _ in units[raw][1]) * (KT if units[raw][1][0][0] == "fm" else 1)
                    act.wait_ge(landed[raw % RAW], landed_value[raw])
                    if u >= RING:
                        act.wait_ge(w_used, u - RING + 1)
                    act.activation(w_hi[:, u % RING, 0:width], w_raw[:, raw % RAW, 0:width],
                                   ACT.Copy).then_inc(w_hi_done, 1)
                    fed[0] += 1

            def pre_square(name, i, tiles, ready):
                n = PRE[name] + i
                act.wait_ge(*ready)
                square(x_res[:, tiles[i], :], ssq_pre[:, n:n + 1], pre_ssq, n + 1)

            def pre_high(name, i, tiles):
                n, t = PRE[name] + i, tiles[i]
                act.wait_ge(pre_full, n + 1)
                if name == "mix1" and t < LT:
                    for k in range(KT):
                        last = act.activation(grid_order(h_hi, k, t), full[:, k, :].rearrange(
                            "p (r b c) -> p r b c", b=8, c=8), ACT.Copy)
                else:
                    last = act.activation(h_hi[:, :, t * P:(t + 1) * P], full[:], ACT.Copy)
                last.then_inc(pre_hi, 1)

            def post_square(name, i, k_units=None):
                n = POST[name] + i
                if k_units is None:
                    act.wait_ge(post_y, n_y[name] + i + 1)
                    src = y_half[:, i, :]
                else:
                    wait_tm(act, tm_name[name], i, k_units)
                    src = ps(2 * i, 0, D)
                square(src, ssq_post[:, n:n + 1], post_ssq, n + 1)

            def gate_rows(b, n_lc):
                for lc in range(n_lc):
                    act.wait_ge(gb_ready, gb_base[b] + lc + 1)
                    if gb_after[b]:
                        act.wait_ge(post_n, gb_after[b])
                    act.activation(gate_b[:, lc, :], ps(4 + 2 * lc, 0, D), ACT.Copy).then_inc(gb_done, 1)

            def ffn_in(name, n_js, width, run, hooks=None):
                s, f0 = sp(name), FI[name]
                for j in range(n_js):
                    f = f0 + j
                    feed(s + 2 * j + 1, run)
                    act.wait_ge(w_used, s + 2 * j + 1)
                    if f >= 2:
                        act.wait_ge(ff_full, f - 1)
                    act.activation(silu_g[:, f % 2, 0:width], ps(2 * (f % 2), 0, width), ACT.Silu)\
                        .then_inc(ff_silu, 1)
                    feed(s + 2 * j + 2, run)
                    act.wait_ge(ff_full, f + 1)
                    act.activation(hid_hi[:, j * width:(j + 1) * width], hid_f[:, f % 2, 0:width], ACT.Copy)\
                        .then_inc(ff_hi, 1)
                    feed(s + 2 * j + 3, run)
                    if hooks and j in hooks:
                        hooks[j]()

            def attention(layer):
                steps, a0, g0 = STEPS[layer], STEP0[layer], GROUP0[layer]
                prob = (prob0, prob1)[layer]

                def softmax(i):
                    a, n = a0 + i, s_cols(layer, i)
                    g, h = g0 + i // 8, steps[i][2]
                    act.wait_ge(at_m, a + 1)
                    if a >= 2:
                        act.wait_ge(at_t, a - 1)
                    act.activation(prob[:, i % 2, 0:n], ps(2 * (i % 2), 0, n), ACT.Exp, bias=negm[:, g % 2, h:h + 1],
                                   scale=SCALE if layer == 0 else 1.0,
                                   accum_out=rowsum[:, g % 2, h:h + 1]).then_inc(at_p, 1)

                def high(gi):
                    t, grp, _ = steps[8 * gi]
                    act.wait_ge(at_f, g0 + gi + 1)
                    for f in range(4):
                        dst, order = group_out(layer, t, grp, f)
                        last = act.activation(dst(h_hi), order(ps(7, f * P, (f + 1) * P)), ACT.Copy)
                    last.then_inc(at_hi, 1)

                softmax(0)
                for i in range(len(steps)):
                    if i + 1 < len(steps):
                        softmax(i + 1)
                    if layer == 1 and i + 1 == len(steps) // 2 - 1:
                        for part in range(16):
                            act.dma_start(*rel_load(1, part)).then_inc(rel_in, 16)
                    if i % 8 == 7 and layer == 0:
                        act.wait_ge(at_shift, i // 8 + 1)
                        act.activation(sm[:, 1, :], sm[:, 0, :], ACT.Exp).then_inc(at_sink, 1)
                    if i % 8 == 0 and i:
                        high(i // 8 - 1)
                high(len(steps) // 8 - 1)

            act.wait_ge(gw_zero, 1)
            act.dma_start(gw[0:RANK, 0:BQK], a["gla_gate_f_w"][0]).then_inc(gw_in, 16)
            act.dma_start(gw[RANK:2 * RANK, BQK:], a["gla_gate_b_w"][0]).then_inc(gw_in, 16)
            act.dma_start(gw[2 * RANK:, 0:BQK], a["gla_gate_f_b"]).then_inc(gw_in, 16)
            act.dma_start(gw[2 * RANK:, BQK:], a["gla_gate_b_b"]).then_inc(gw_in, 16)
            act.wait_ge(par_done, 2)
            act.activation(c_col[:], par_col[:, 68:84].rearrange("p (v k) -> p k v", v=2), ACT.Silu)\
                .then_inc(c_done, 1)
            act.wait_ge(x_in, 32)
            act.wait_ge(consts_in, 16 * 6)
            for i in range(NT):
                pre_square("mix0", i, range(NT), (x_in, 32))
            feed(sp("v0") + 1, "v0")
            for i in range(NT):
                pre_high("mix0", i, range(NT))
            feed(sp("in0") + 1, "v0")
            for t in range(NT):
                wait_tm(act, "v0", t, KT)
                act.activation(b_v[:, t, :], ps(t, 0, BV), ACT.Copy).then_inc(v_act, 1)
            for i in range(15):
                s = sp("in0") + i
                feed(s + 1, "v0")
                act.wait_ge(w_used, s + 1)
                bl, bc = 2 * (i % 2), 2 * (i % 2) + 1
                lat, con = ps(bl, 0, SEQ), ps(bc, 0, CTX)
                if i < 6:
                    dst = a_q[:, i] if i < 4 else a_k[:, i - 4]
                    act.activation(dst[:, SEQ:], con, ACT.Copy).then_inc(fe_act, 1)
                    continue
                if i < 8:
                    dst, fn, scale = b_q[:, i - 6], ACT.Copy, SCALE
                elif i < 10:
                    dst, fn, scale = b_k[:, i - 8], ACT.Copy, 1.0
                elif i < 14:
                    dst, fn, scale = b_o[:, i - 10], ACT.Silu, 1.0
                else:
                    dst, fn, scale = r_t[0:32], ACT.Copy, 1.0
                    lat, con = ps(bl, 0, SEQ, 96, P), ps(bc, 0, CTX, 96, P)
                act.activation(dst[:, 0:SEQ], lat, fn, scale=scale)
                act.activation(dst[:, SEQ:], con, fn, scale=scale).then_inc(fe_act, 1)
            attention(0)

            for t in range(NT):
                act.wait_ge(gl_z, t + 1)
                if t == 0:
                    act.wait_ge(at_lo, n_groups[0])
                act.activation(la[:, t, :], ps(t, 0, 512), ACT.Abs).then_inc(gl_abs, 1)
                act.wait_ge(gl_abs, t + 1)
                act.activation(la[:, t, :], la[:, t, :], ACT.Exp, scale=-1.0).then_inc(gl_exp, 1)
            for t in range(NT):
                act.wait_ge(gl_exp, t + 1)
                act.activation(la[:, t, :], la[:, t, :], ACT.Ln, bias=one_col[:]).then_inc(gl_ln, 1)
            for t in range(NT):
                act.wait_ge(gl_cum, t + 1)
                src = ps(6 + t % 2, 0, 512).rearrange("p (m n) -> p m n", m=4)
                act.activation(qg[:, :, t * P:(t + 1) * P], src, ACT.Exp, scale=1.0 / 16).then_inc(gl_eq, 1)
                act.activation(kg[:, :, t * P:(t + 1) * P], src, ACT.Exp, scale=-1.0 / 16).then_inc(gl_ek, 1)

            def gla_high(t):
                act.wait_ge(gl_full, t + 1)
                act.activation(h_hi[:, 4:8, t * P:(t + 1) * P],
                               b_q[:].rearrange("p a n -> p (a n)")[:, 0:512].rearrange("p (h n) -> p h n", h=4),
                               ACT.Copy).then_inc(gl_hi, 1)

            for t in range(NT):
                act.wait_ge(gl_o, t + 1)
                for h in range(4):
                    square(ps(4 + h % 2, (h // 2) * P, (h // 2 + 1) * P), gla_ssq[:, t, h:h + 1], gl_ssq, 4 * t + h + 1)
                if t:
                    gla_high(t - 1)
            gla_high(NT - 1)

            gate_rows(0, 2)
            feed(sp("out0C") + 1, "out0L")
            for i in range(LT):
                post_square("out0L", i, KT)
                feed(sp("out0C") + i, "out0L")
            for i in range(LT):
                pre_square("ffn0L", i, L_TILES, (post_x, POST["out0L"] + i + 1))
                feed(sp("out0C") + 4 + i, "out0L")
            feed(sp(("fi0L", 0)) + 1, "out0L")
            for i in range(CT):
                post_square("out0C", i, KT)
            for i in range(CT):
                pre_square("ffn0C", i, C_TILES, (post_x, POST["out0C"] + i + 1))
            for i in range(LT):
                pre_high("ffn0L", i, L_TILES)
            ffn_in(("fi0L", 0), FH, SEQ, "out0L",
                   {2: lambda: [pre_high("ffn0C", i, C_TILES) for i in range(CT)], 4: lambda: gate_rows(1, 2)})
            feed(sp(("fi0L", 1)) + 1, "out0L")
            ffn_in(("fi0L", 1), FH, SEQ, "out0L")
            feed(sp("fi0C") + 1, "out0L")
            hooks = {j: (lambda i=j: post_square("fo0L", i)) for j in range(LT)}
            hooks |= {LT + j: (lambda i=j: pre_square("mix1", i, L_TILES, (post_x, POST["fo0L"] + i + 1)))
                      for j in range(LT)}
            ffn_in("fi0C", FT, CTX, "out0L", hooks)
            feed(sp("fo0C") + FT - 1, "out0L")
            for i in range(CT):
                post_square("fo0C", i, FT)
            for i in range(CT):
                pre_square("mix1", LT + i, range(NT), (post_x, POST["fo0C"] + i + 1))

            gate_rows(2, 1)
            feed(sp("qk1") + 1, "qk1")
            for i in range(NT):
                pre_high("mix1", i, range(NT))
            for i in range(16):
                s = sp("qk1") + i
                feed(s + 1, "qk1")
                act.wait_ge(w_used, s + 1)
                bank = 2 * (i % 2)
                if i == 0:
                    act.dma_start(*rel_load(0)).then_inc(rel_in, 16)
                    for other in range(1, 16):
                        act.dma_start(*rel_load(0, other)).then_inc(rel_in, 16)
                if i < KT:
                    act.activation(c_q[:, i, :], ps(bank, 0, SEQ), ACT.Copy, scale=SCALE).then_inc(fe1_act, 1)
                else:
                    act.activation(c_k[:, i - KT, 0:SEQ], ps(bank, 0, SEQ), ACT.Copy)
                    act.activation(c_k[:, i - KT, SEQ:], ps(bank + 1, 0, CTX), ACT.Copy).then_inc(fe1_act, 1)
            for name, tiles in (("v1L", L_TILES), ("v1C", C_TILES)):
                feed(sp(name) + KT + 1, "qk1")
                for i, t in enumerate(tiles):
                    wait_tm(act, name, i, KT)
                    act.activation(c_v[:, t, :], ps(2 * i, 0, D), ACT.Copy).then_inc(v_act, 1)
            attention(1)
            feed(sp("out1L") + 7, "qk1")
            feed(sp(("fi1L", 0)) + 1, "qk1")
            for i in range(LT):
                post_square("out1L", i, KT)
            for i in range(LT):
                pre_square("ffn1L", i, L_TILES, (post_x, POST["out1L"] + i + 1))
            for i in range(LT):
                pre_high("ffn1L", i, L_TILES)
            ffn_in(("fi1L", 0), FH, SEQ, "qk1", {4: lambda: gate_rows(3, 1)})
            feed(sp(("fi1L", 1)) + 1, "qk1")
            ffn_in(("fi1L", 1), FH, SEQ, "qk1")
            feed(sp(("fo1L", 1)) + FH - 1, "qk1")
            for i in range(LT):
                post_square("fo1L", i)

        @block.vector
        def _(dve):
            def pre_scale(name, i, tiles):
                n = PRE[name] + i
                dve.wait_ge(pre_rs, n + 1)
                if n >= 2:
                    dve.wait_ge(pre_tr, n - 1)
                dve.tensor_scalar(xs[:, n % 2, :], x_res[:, tiles[i], :], rs_pre[:, n:n + 1], None,
                                  ALU.mult).then_inc(pre_xs, 1)

            def pre_modulate(name, i, tiles, b, j):
                n = PRE[name] + i
                lc = int(tiles[i] >= LT)
                dve.wait_ge(pre_tr, n + 1)
                if n:
                    dve.wait_ge(pre_lo, n)
                dve.wait_ge(mod_der, 2 * j + 1 if j % 2 == 0 else 2 * j + 1)
                dve.wait_ge(mod_done, b + 1)
                for k in range(KT):
                    last = dve.tensor_scalar(full[:, k, :], ps(4 + 2 * (n % 2), k * P, (k + 1) * P),
                                             pre_a[:, j, lc, k:k + 1], mod_col[:, b, lc, k:k + 1], ALU.mult, ALU.add)
                last.then_inc(pre_full, 1)

            def pre_low(name, i, tiles):
                n, t = PRE[name] + i, tiles[i]
                dve.wait_ge(pre_hi, n + 1)
                if name == "mix1" and t < LT:
                    for k in range(KT):
                        last = dve.tensor_tensor(
                            grid_order(h_lo, k, t), full[:, k, :].rearrange("p (r b c) -> p r b c", b=8, c=8),
                            grid_order(h_hi, k, t).bitcast(F32), ALU.subtract)
                else:
                    cols = slice(t * P, (t + 1) * P)
                    last = dve.tensor_tensor(h_lo[:, :, cols], full[:], h_hi[:, :, cols].bitcast(F32), ALU.subtract)
                last.then_inc(pre_lo, 1)

            def pre_rest(name, tiles, b, j, scaled=0):
                for i in range(scaled, min(2, len(tiles))):
                    pre_scale(name, i, tiles)
                for i in range(len(tiles)):
                    pre_modulate(name, i, tiles, b, j)
                    if 2 <= i + 2 < len(tiles):
                        pre_scale(name, i + 2, tiles)
                    pre_low(name, i, tiles)

            def post_norm(name, i, t, k_units=None):
                n, lc = POST[name] + i, int(t >= LT)
                src = ps(2 * i, 0, D) if k_units else y_half[:, i, :]
                dve.wait_ge(post_rs, n + 1)
                dve.wait_ge(gb_done, gb_need[name][lc])
                if n:
                    dve.wait_ge(post_x, n)
                dve.scalar_tensor_tensor(post_t[:], src, rs_post[:, n:n + 1], gate_b[:, lc, :], ALU.mult,
                                         ALU.mult).then_inc(post_n, 1)
                dve.wait_ge(post_n, n + 1)
                dve.tensor_tensor(x_res[:, t, :], x_res[:, t, :], post_t[:], ALU.add).then_inc(post_x, 1)

            def take_half(name, k_units):
                for i in range(LT):
                    wait_tm(dve, name, i, k_units)
                    dve.tensor_copy(y_half[:, i, :], ps(2 * i, 0, D)).then_inc(half_done, 1)

            def add_half(name, short, k_units):
                for i in range(LT):
                    wait_tm(dve, name, i, k_units)
                    dve.wait_ge(half_done, LT * (1 + (short == "fo1L")))
                    dve.tensor_tensor(y_half[:, i, :], y_half[:, i, :], ps(2 * i, 0, D), ALU.add).then_inc(post_y, 1)

            def modulation(b):
                l, i = divmod(b, 6)
                dve.wait_ge(w_direct, KT * (b + 1))
                if b:
                    dve.wait_ge(mod_turned, b)
                dve.tensor_copy(mod_rows[:], ps(4, 0, D, 0, 2)).then_inc(mod_copied, 1)
                dve.wait_ge(mod_turned, b + 1)
                bias = bias_col[:, b * KT:(b + 1) * KT]
                bias = bass.AP(bias.tensor, bias.offset, [list(bias.ap[0]), [0, 2], [1, KT]])
                dve.tensor_tensor(mod_col[:, b], ps(6, 0, 2 * KT).rearrange("p (k v) -> p v k", v=2), bias,
                                  ALU.add).then_inc(mod_done, 1)
                if i in (0, 3):
                    return
                which = {1: 0, 2: 0, 4: 1, 5: 1}[i]
                gain = {1: 0, 2: 16, 4: 32, 5: 48}[i] + l * KT
                gain = par_col[:, gain:gain + KT]
                gain = bass.AP(gain.tensor, gain.offset, [list(gain.ap[0]), [0, 2], [1, KT]])
                dve.wait_ge(mod_done, b + 1)
                if i in (1, 4):
                    dve.scalar_tensor_tensor(pre_a[:, 2 * l + which], mod_col[:, b], 1.0, gain, ALU.add,
                                             ALU.mult).then_inc(mod_der, 1)
                else:
                    dve.tensor_tensor(gate_col[:, 2 * l + which], mod_col[:, b], gain, ALU.mult).then_inc(mod_der, 1)

            def ffn_in(name, n_js, width, hooks=None):
                s, f0 = sp(name), FI[name]
                for j in range(n_js):
                    f = f0 + j
                    dve.wait_ge(w_used, s + 2 * j + 2)
                    dve.wait_ge(ff_silu, f + 1)
                    if f >= 2:
                        dve.wait_ge(ff_lo, f - 1)
                    dve.tensor_tensor(hid_f[:, f % 2, 0:width], silu_g[:, f % 2, 0:width],
                                      ps(2 * (f % 2) + 1, 0, width), ALU.mult).then_inc(ff_full, 1)
                    dve.wait_ge(ff_hi, f + 1)
                    dve.tensor_tensor(hid_lo[:, j * width:(j + 1) * width], hid_f[:, f % 2, 0:width],
                                      hid_hi[:, j * width:(j + 1) * width].bitcast(F32), ALU.subtract)\
                        .then_inc(ff_lo, 1)
                    if hooks and j in hooks:
                        hooks[j]()

            def attention(layer):
                steps, a0, g0 = STEPS[layer], STEP0[layer], GROUP0[layer]
                prob_t = (prob0_t, prob1_t)[layer]

                def maximum(i):
                    a, n = a0 + i, s_cols(layer, i)
                    g, h = g0 + i // 8, steps[i][2]
                    dve.wait_ge(at_s, a + 1)
                    if a >= 2:
                        dve.wait_ge(at_m, a - 1)
                    dve.tensor_reduce(raw_max[:, a % 2:a % 2 + 1], ps(2 * (i % 2), 0, n), AX, ALU.max)\
                        .then_inc(at_r, 1)
                    dve.wait_ge(at_r, a + 1)
                    if layer == 0:
                        dve.tensor_scalar(negm[:, g % 2, h:h + 1], raw_max[:, a % 2:a % 2 + 1], -SCALE,
                                          nsink[:, h:h + 1], ALU.mult, ALU.min).then_inc(at_m, 1)
                    else:
                        dve.tensor_scalar(negm[:, g % 2, h:h + 1], raw_max[:, a % 2:a % 2 + 1], -1.0, None,
                                          ALU.mult).then_inc(at_m, 1)

                def evacuate(i):
                    a, n = a0 + i, s_cols(layer, i)
                    dve.wait_ge(at_t, a + 1)
                    if a >= 2:
                        dve.wait_ge(at_o, a - 1)
                    dve.tensor_copy(prob_t[:, i % 2, 0:n], ps(4, 0, n)).then_inc(at_e, 1)

                def group_end(gi):
                    g = g0 + gi
                    dve.wait_ge(at_o, a0 + 8 * gi + 8)
                    den = rowsum[:, g % 2, :]
                    if layer == 0:
                        dve.tensor_tensor(sm[:, 0, :], negm[:, g % 2, :], sink[:], ALU.add).then_inc(at_shift, 1)
                        dve.wait_ge(at_sink, g + 1)
                        dve.tensor_tensor(sm[:, 2, :], den, sm[:, 1, :], ALU.add).then_inc(at_den, 1)
                        dve.wait_ge(at_den, g + 1)
                        den = sm[:, 2, :]
                    if g:
                        dve.wait_ge(at_on, g)
                    dve.reciprocal(sm[:, 3, :], den).then_inc(at_rinv, 1)
                    dve.wait_ge(at_rinv, g + 1)
                    if g >= 2:
                        dve.wait_ge(at_f, g - 1)
                    dve.tensor_tensor(full[:, 4 * (g % 2):4 * (g % 2) + 4, :].rearrange(
                        "p a n -> p (a n)").rearrange("p (h d) -> p h d", h=8),
                        ps(6, 0, 512).rearrange("p (h d) -> p h d", h=8), bcast(sm[:, 3, :], 64),
                        ALU.mult).then_inc(at_on, 1)

                def low(gi):
                    t, grp, _ = steps[8 * gi]
                    dve.wait_ge(at_hi, g0 + gi + 1)
                    for f in range(4):
                        dst, order = group_out(layer, t, grp, f)
                        last = dve.tensor_tensor(dst(h_lo), order(ps(7, f * P, (f + 1) * P)),
                                                 dst(h_hi).bitcast(F32), ALU.subtract)
                    last.then_inc(at_lo, 1)

                maximum(0)
                for i in range(len(steps)):
                    if i + 1 < len(steps):
                        maximum(i + 1)
                    evacuate(i)
                    if i % 8 == 0 and i:
                        low(i // 8 - 1)
                    if i % 8 == 7:
                        group_end(i // 8)
                low(len(steps) // 8 - 1)

            dve.memset(r_t[32:33, :], 1.0)
            dve.memset(gw[:], 0.0).then_inc(gw_zero, 1)
            dve.wait_ge(consts_in, 16 * 6)
            dve.tensor_copy(ident_b[:], ident[:])
            dve.tensor_copy(window_b[:], mask_in[:, 0:2 * P])
            dve.tensor_copy(near_b[:].rearrange("p t n -> p (t n)"), mask_in[:, 2 * P:]).then_inc(par_done, 1)
            dve.wait_ge(par_in, 16 * 9)
            dve.tensor_scalar(nsink[:], sink[:], -1.0, None, ALU.mult)
            dve.wait_ge(par_turned, 2)
            dve.tensor_copy(bias_col[:], ps(6, 0, 96))
            dve.tensor_copy(par_col[:], ps(7, 0, 84)).then_inc(par_done, 1)
            dve.wait_ge(par_done, 2)
            modulation(0)
            modulation(1)
            pre_rest("mix0", range(NT), 0, 0)
            wait_tm(dve, "v0", NT - 1, KT)
            for t in range(NT):
                dve.tensor_copy(a_v[:, t, :], ps(6, t * P, (t + 1) * P)).then_inc(v_dve, 1)
            for i in range(14):
                s = sp("in0") + i
                if i < 6:
                    dst = (a_q[:, i] if i < 4 else a_k[:, i - 4])[:, 0:SEQ]
                    lat = ps(2 * (i % 2), 0, SEQ)
                    dve.wait_ge(w_used, s + 1)
                    if i:
                        dve.wait_ge(rope_done, i)
                    dve.tensor_tensor(rope_t[:, 0], lat, cos[:], ALU.mult)
                    dve.stream_shuffle(rope_t[:, 1], lat, [(q + 16) % 32 for q in range(32)]).then_inc(fe_dve, 1)
                    dve.wait_ge(fe_dve, i + 1)
                    dve.tensor_tensor(rope_t[:, 1], rope_t[:, 1], sin[:], ALU.mult).then_inc(rope_m, 1)
                    dve.wait_ge(rope_m, i + 1)
                    dve.tensor_tensor(dst, rope_t[:, 0], rope_t[:, 1], ALU.add).then_inc(rope_done, 1)
                elif i >= 10:
                    dve.wait_ge(fe_act, i + 1)
                    dve.tensor_scalar(b_o[:, i - 10], b_o[:, i - 10], par_col[:, 64 + i - 10:65 + i - 10], None,
                                      ALU.mult).then_inc(bo_done, 1)
            for b in range(2, 6):
                modulation(b)
            attention(0)

            for t in range(NT):
                dve.wait_ge(gl_ln, t + 1)
                dve.scalar_tensor_tensor(la[:, t, :], ps(t, 0, 512), 0.0, la[:, t, :], ALU.min,
                                         ALU.subtract).then_inc(gl_la, 1)
            for t in range(NT):
                cols = slice(t * P, (t + 1) * P)
                dve.wait_ge(gl_eq, t + 1)
                dve.tensor_copy(decay[:, 0:2, 2 * t:2 * t + 2], qg[:, 0:2, t * P + CH - 1:(t + 1) * P:CH])
                dve.tensor_copy(decay[:, 2:4, 2 * t:2 * t + 2], qg[:, 2:4, t * P:(t + 1) * P:CH]).then_inc(gl_dec, 1)
                dve.wait_ge(gl_dec, t + 1)
                for d in range(2):
                    last = dve.tensor_tensor(qg[:, 2 * d:2 * d + 2, cols], qg[:, 2 * d:2 * d + 2, cols],
                                             b_q[:, :, cols], ALU.mult)
                last.then_inc(gl_q, 1)
                dve.wait_ge(gl_ek, t + 1)
                for d in range(2):
                    last = dve.tensor_tensor(kg[:, 2 * d:2 * d + 2, cols], kg[:, 2 * d:2 * d + 2, cols],
                                             b_k[:, :, cols], ALU.mult)
                last.then_inc(gl_k, 1)
            for t in range(NT):
                dve.wait_ge(gl_kt, t + 1)
                if t == 0:
                    dve.wait_ge(gl_cum, NT)
                dve.tensor_copy(kg_t[:, t, :], ps(t % 2, 0, 512)).then_inc(gl_ktc, 1)
            dve.memset(state[:, 0], 0.0).then_inc(gl_s, 1)
            dve.wait_ge(gl_dec, NT)
            for i in range(2 * NT - 1):
                dve.wait_ge(gl_ds, i + 1)
                dve.wait_ge(gl_s, 2 * i + 1)
                for d in range(2):
                    m = slice(2 * d, 2 * d + 2)
                    last = dve.tensor_tensor(state[:, i + 1, m], state[:, i, m], ps(2 + 2 * d + i % 2, 0, 256).rearrange(
                        "p (m n) -> p m n", m=2), ALU.add)
                last.then_inc(gl_u, 1)
                dve.wait_ge(gl_u, i + 1)
                for d, chunk in enumerate((f_order[i], b_order[i])):
                    dve.tensor_tensor(state[:, i + 1, 2 * d:2 * d + 2], state[:, i + 1, 2 * d:2 * d + 2],
                                      bcast(decay[:, 2 * d:2 * d + 2, chunk], P), ALU.mult).then_inc(gl_s, 1)
            fg = b_q[:].rearrange("p a n -> p (a n)")[:, 0:512]
            on = b_k[:].rearrange("p a n -> p (a n)")[:, 0:512]

            def gla_mask(t):
                dve.wait_ge(gl_att, t + 1)
                if t:
                    dve.wait_ge(gl_o, t)
                for d in range(2):
                    m = tri[:, d]
                    m = bass.AP(m.tensor, m.offset, [list(m.ap[0]), [0, 2], [1, P]])
                    for b in range(2):
                        last = dve.tensor_tensor(
                            att_m[:, d].rearrange("p (a b n) -> p b a n", a=2, b=2)[:, b],
                            ps(2 * d + b, 0, 256).rearrange("p (h n) -> p h n", h=2), m, ALU.mult)
                last.then_inc(gl_msk, 1)

            gla_mask(0)
            for t in range(NT):
                dve.wait_ge(gl_rs, t + 1)
                if t:
                    dve.wait_ge(gl_f, t)
                for b in range(2):
                    last = dve.tensor_tensor(on.rearrange("p (a b n) -> p b a n", a=2, b=2)[:, b],
                                             ps(4 + b, 0, 256).rearrange("p (h n) -> p h n", h=2),
                                             bcast(gla_rs[:, t, b:4:2], P), ALU.mult)
                last.then_inc(gl_on, 1)
                if t + 1 < NT:
                    gla_mask(t + 1)
                dve.wait_ge(gl_f, t + 1)
                cols = slice(t * P, (t + 1) * P)
                if t:
                    dve.wait_ge(gl_lo, t)
                dve.tensor_tensor(fg.rearrange("p (h n) -> p h n", h=4),
                                  ps(6 + t % 2, 0, 512).rearrange("p (h n) -> p h n", h=4), b_o[:, :, cols],
                                  ALU.mult).then_inc(gl_full, 1)
                dve.wait_ge(gl_hi, t + 1)
                dve.tensor_tensor(h_lo[:, 4:8, cols], fg.rearrange("p (h n) -> p h n", h=4),
                                  h_hi[:, 4:8, cols].bitcast(F32), ALU.subtract).then_inc(gl_lo, 1)

            for i in range(LT):
                post_norm("out0L", i, i, KT)
            pre_scale("ffn0L", 0, L_TILES)
            pre_scale("ffn0L", 1, L_TILES)
            for i in range(CT):
                post_norm("out0C", i, LT + i, KT)
            pre_rest("ffn0L", L_TILES, 3, 1, scaled=2)
            for i in range(CT):
                pre_scale("ffn0C", i, C_TILES)
            ffn_in(("fi0L", 0), FH, SEQ, {2: lambda: pre_rest("ffn0C", C_TILES, 3, 1, scaled=2)})
            take_half(("fo0L", 0), FH)
            ffn_in(("fi0L", 1), FH, SEQ)
            add_half(("fo0L", 1), "fo0L", FH)
            hooks = {j: (lambda i=j: post_norm("fo0L", i, i)) for j in range(LT)}
            ffn_in("fi0C", FT, CTX, hooks)
            for i in range(CT):
                post_norm("fo0C", i, LT + i, FT)
            for b in range(6, 12):
                modulation(b)
            pre_rest("mix1", range(NT), 6, 2)
            attention(1)
            for i in range(LT):
                post_norm("out1L", i, i, KT)
            pre_rest("ffn1L", L_TILES, 9, 3)
            ffn_in(("fi1L", 0), FH, SEQ)
            take_half(("fo1L", 0), FH)
            ffn_in(("fi1L", 1), FH, SEQ)
            add_half(("fo1L", 1), "fo1L", FH)
            for i in range(LT):
                post_norm("fo1L", i, i)

        @block.tensor
        def _(pe):
            readers = {}

            def claim(*banks):
                for b in banks:
                    for s, v in readers.pop(b, ()):
                        pe.wait_ge(s, v)

            def read_by(banks, *who):
                for b in banks:
                    readers[b] = who

            def split_ready(s):
                pe.wait_ge(w_lo_done, s + 1)

            def product3(s, sta, mov, outs, first, last, done=None):
                order = [("hi", "hi"), ("hi", "lo"), ("lo", "hi")]
                for n, (x, y) in enumerate(order):
                    for o in outs:
                        mm = pe.matmul(o[0], sta(x, o), mov(y, o), start=first and n == 0, stop=last and n == 2)
                return mm

            def fm_unit(s, outs):
                split_ready(s)
                w = {"hi": w_hi[:, s % RING], "lo": w_lo[:, s % RING]}
                h = {"hi": h_hi, "lo": h_lo}
                for k in range(KT):
                    mm = product3(s, lambda x, o: w[x][:, k * P:(k + 1) * P],
                                  lambda y, o: h[y][:, k, o[1]:o[1] + o[2]], outs, k == 0, k == KT - 1)
                mm.then_inc(w_used, 1)

            def tm_product(name, n_units, act, tiles, where, ready=None):
                s0 = sp(name)
                for k in range(n_units):
                    s = s0 + k
                    if ready:
                        ready(k)
                    split_ready(s)
                    w = {"hi": w_hi[:, s % RING], "lo": w_lo[:, s % RING]}
                    for i, t in enumerate(tiles):
                        for x, y in (("hi", "hi"), ("hi", "lo"), ("lo", "hi")):
                            for o, c, n in where(i):
                                mm = pe.matmul(o, act(x, k, t), w[y][:, c:c + n],
                                               start=k == 0 and (x, y) == ("hi", "hi") and first_in_bank(name, i, c),
                                               stop=k == n_units - 1 and x == "lo", skip_group_check=True)
                        if k == n_units - 1 and i < len(tiles) - 1:
                            mm.then_inc(tm_done, 1)
                    mm.then_inc(w_used, 1)

            def first_in_bank(name, i, c):
                return not (name == "v0" and c == 0 and i not in (0, 4))

            def h_act(x, k, t):
                return (h_hi if x == "hi" else h_lo)[:, k, t * P:(t + 1) * P]

            def two_halves(i):
                return [(ps(2 * i + n, 0, 512), 512 * n, 512) for n in range(2)]

            def modulation(b):
                claim(4, 5)
                u0 = start[("mod", b)]
                for k in range(KT):
                    pe.wait_ge(landed[(u0 + k) % RAW], landed_value[u0 + k])
                    for n in range(2):
                        mm = pe.matmul(ps(4 + n, 0, 512, 0, 2), c_col[:, k, :],
                                       w_raw[:, (u0 + k) % RAW, n * 512:(n + 1) * 512], start=k == 0, stop=k == KT - 1)
                    mm.then_inc(w_direct, 1)
                read_by((4, 5), (mod_copied, b + 1))
                claim(6)
                pe.wait_ge(mod_copied, b + 1)
                for k in range(KT):
                    mm = pe.transpose(ps(6, 2 * k, 2 * k + 2), mod_rows[:, k * P:(k + 1) * P], ident[0:2, 0:2])
                mm.then_inc(mod_turned, 1)
                read_by((6,), (mod_done, b + 1))

            def pre_turn(name, tiles):
                for i in range(len(tiles)):
                    n = PRE[name] + i
                    b = 4 + 2 * (n % 2)
                    claim(b, b + 1)
                    pe.wait_ge(pre_xs, n + 1)
                    for k in range(KT):
                        mm = pe.transpose(ps(b, k * P, (k + 1) * P), xs[:, n % 2, k * P:(k + 1) * P], ident[:])
                    mm.then_inc(pre_tr, 1)
                    read_by((b, b + 1), (pre_full, n + 1))

            def gate_rows(j, n_lc):
                pe.wait_ge(mod_der, 2 * j + 2)
                for lc in range(n_lc):
                    claim(4 + 2 * lc, 5 + 2 * lc)
                    for k in range(KT):
                        col = gate_col[:, j, lc, k:k + 1]
                        mm = pe.matmul(ps(4 + 2 * lc, k * P, (k + 1) * P),
                                       bass.AP(col.tensor, col.offset, [list(col.ap[0]), [0, P]]), ident[:],
                                       start=True, stop=True)
                    mm.then_inc(gb_ready, 1)
                    read_by((4 + 2 * lc, 5 + 2 * lc), (gb_done, gb_base[j] + lc + 1))

            def ffn_in(name, n_js, col0, width, hooks=None):
                s, f0 = sp(name), FI[name]
                for j in range(n_js):
                    f = f0 + j
                    for up in range(2):
                        bank = 2 * (f % 2) + up
                        claim(bank)
                        fm_unit(s + 2 * j + up, [(ps(bank, 0, width), col0, width)])
                        read_by((bank,), (ff_full, f + 1) if up else (ff_silu, f + 1))
                    if hooks and j in hooks:
                        hooks[j]()

            def ffn_out(name, fi, n_units, tiles, width, base):
                f0 = FI[fi]
                hid = {"hi": hid_hi, "lo": hid_lo}
                tm_product(name, n_units,
                           lambda x, k, t: hid[x][:, k * width + (t - base) * P:k * width + (t - base + 1) * P],
                           tiles, two_halves, ready=lambda k: pe.wait_ge(ff_lo, f0 + k + 1))

            def attention(layer):
                steps, a0, g0 = STEPS[layer], STEP0[layer], GROUP0[layer]
                prob, prob_t = ((prob0, prob0_t), (prob1, prob1_t))[layer]

                def scores(i):
                    t, grp, h = steps[i]
                    sb_ = 2 * (i % 2)
                    claim(sb_, sb_ + 1)
                    if layer == 1 and i == len(steps) // 2:
                        pe.wait_ge(rel_in, 16 * 32)
                    head = 8 * grp + h
                    rows = slice(64 * (h % 2), 64 * (h % 2) + 64)
                    if layer == 0:
                        q, kk = a_q[rows, h // 2, t * P:(t + 1) * P], a_k[rows, h // 4]
                    else:
                        q, kk = c_q[rows, head // 2, t * P:(t + 1) * P], c_k[rows, head // 2]
                    near, n = local_tiles(t), 0
                    if near:
                        n = len(near) * P
                        pe.matmul(ps(sb_, 0, n), q, kk[:, near[0] * P:near[0] * P + n], start=True, stop=False,
                                  skip_group_check=True)
                        if layer == 0:
                            for at, u in enumerate(near):
                                if u != t:
                                    side = int(u > t)
                                    pe.matmul(ps(sb_, at * P, (at + 1) * P), ident_b[:],
                                              window_b[:, side * P:(side + 1) * P], start=False, stop=False,
                                              skip_group_check=True)
                        else:
                            d0 = near[0] - t + 1
                            run = rel[:, 7 - h, BIAS_RUN - 1 - 16 * d0:BIAS_RUN - 16 * d0]
                            run = bass.AP(run.tensor, run.offset,
                                          [list(run.ap[0]), [-8, 2 * len(near)], [-BIAS_ROW, 8], [-1, 8]])
                            pe.matmul(ps(sb_, 0, n), ident[:], run, start=False, stop=False, skip_group_check=True)
                            pe.matmul(ps(sb_, 0, n), ident_b[:], near_b[:, t, d0 * P:d0 * P + n], start=False,
                                      stop=False, skip_group_check=True)
                    left, at = CTX, 0
                    while left:
                        m = min(left, 512 - n % 512)
                        mm = pe.matmul(ps(sb_, n, n + m), q, kk[:, SEQ + at:SEQ + at + m],
                                       start=n % 512 == 0, stop=left == m, skip_group_check=True)
                        n, at, left = n + m, at + m, left - m
                    mm.then_inc(at_s, 1)
                    read_by((sb_, sb_ + 1), (at_p, a0 + i + 1))

                def turn(i):
                    a = a0 + i
                    pe.wait_ge(at_p, a + 1)
                    claim(4, 5)
                    for j in range(s_cols(layer, i) // P):
                        mm = pe.transpose(ps(4, j * P, (j + 1) * P), prob[:, i % 2, j * P:(j + 1) * P], ident[:])
                    mm.then_inc(at_t, 1)
                    read_by((4, 5), (at_e, a + 1))

                def values(i):
                    t, grp, h = steps[i]
                    if h == 0:
                        claim(6)
                    pe.wait_ge(at_e, a0 + i + 1)
                    keys = local_tiles(t) + C_TILES
                    for j, u in enumerate(keys):
                        v = a_v[:, u, 64 * (h // 4):64 * (h // 4) + 64] if layer == 0 else \
                            c_v[:, u, (8 * grp + h) * 64:(8 * grp + h + 1) * 64]
                        mm = pe.matmul(ps(6, h * 64, h * 64 + 64), prob_t[:, i % 2, j * P:(j + 1) * P], v,
                                       start=h == 0 and j == 0, stop=j == len(keys) - 1, skip_group_check=True)
                    mm.then_inc(at_o, 1)
                    if h == 7:
                        read_by((6,), (at_on, g0 + i // 8 + 1))

                def turn_group(gi):
                    g = g0 + gi
                    pe.wait_ge(at_on, g + 1)
                    claim(7)
                    for f in range(4):
                        mm = pe.transpose(ps(7, f * P, (f + 1) * P), full[:, 4 * (g % 2) + f, :], ident[:])
                    mm.then_inc(at_f, 1)
                    read_by((7,), (at_lo, g + 1))

                scores(0)
                scores(1)
                turn(0)
                for i in range(len(steps)):
                    if i + 2 < len(steps):
                        scores(i + 2)
                    if i + 1 < len(steps):
                        turn(i + 1)
                    if i % 8 == 0 and i:
                        turn_group(i // 8 - 1)
                    values(i)
                turn_group(len(steps) // 8 - 1)

            pe.wait_ge(par_in, 16 * 9)
            pe.wait_ge(consts_in, 16 * 6)
            pe.transpose(ps(6, 0, 96), par_rows[0:96, 0, :], ident[0:96, 0:96]).then_inc(par_turned, 1)
            pe.transpose(ps(7, 0, 84), par_rows[0:84, 1, :], ident[0:84, 0:84]).then_inc(par_turned, 1)
            read_by((6, 7), (par_done, 2))
            pe.wait_ge(c_done, 1)
            modulation(0)
            modulation(1)
            pre_turn("mix0", range(NT))
            pe.wait_ge(pre_lo, NT)
            claim(*range(8))
            tm_product("v0", KT, h_act, range(NT),
                       lambda i: [(ps(6, i * P, (i + 1) * P), 0, AKV), (ps(i, 0, BV), AKV, BV)])
            for t in range(NT):
                read_by((t,), (v_act, t + 1))
            read_by((6, 7), (v_dve, NT))
            for i in range(15):
                bl = 2 * (i % 2)
                claim(bl, bl + 1)
                fm_unit(sp("in0") + i, [(ps(bl, 0, SEQ), 0, SEQ), (ps(bl + 1, 0, CTX), SEQ, CTX)])
                read_by((bl, bl + 1), (fe_act, i + 1), *([(fe_dve, i + 1)] if i < 6 else []))
            for b in range(2, 6):
                modulation(b)
            pe.wait_ge(rope_done, 6)
            pe.wait_ge(fe_act, 15)
            claim(*range(8))
            attention(0)

            pe.wait_ge(gw_in, 64)
            claim(*range(8))
            for t in range(NT):
                pe.matmul(ps(t, 0, 512), r_t[:, t * P:(t + 1) * P], gw[:], start=True, stop=True).then_inc(gl_z, 1)
                read_by((t,), (gl_la, t + 1))
            for t in range(NT):
                claim(6 + t % 2)
                pe.wait_ge(gl_la, t + 1)
                for m in range(4):
                    mm = pe.matmul(ps(6 + t % 2, m * P, (m + 1) * P), la[:, t, m * P:(m + 1) * P], tri[:, m // 2],
                                   start=True, stop=True)
                mm.then_inc(gl_cum, 1)
                read_by((6 + t % 2,), (gl_ek, t + 1))
            for t in range(NT):
                claim(t % 2)
                pe.wait_ge(gl_k, t + 1)
                for m in range(4):
                    mm = pe.transpose(ps(t % 2, m * P, (m + 1) * P), kg[:, m, t * P:(t + 1) * P], ident[:])
                mm.then_inc(gl_kt, 1)
                read_by((t % 2,), (gl_ktc, t + 1))
            pe.wait_ge(gl_ktc, NT)
            for i in range(2 * NT - 1):
                claim(2 + i % 2, 4 + i % 2)
                for m in range(4):
                    bank = 2 + 2 * (m // 2) + i % 2
                    chunk = (f_order, b_order)[m // 2][i]
                    t, rows = chunk // 2, slice(64 * (chunk % 2), 64 * (chunk % 2) + 64)
                    for hh in range(2):
                        head = 2 * (m % 2) + hh
                        mm = pe.matmul(ps(bank, (m % 2) * P, (m % 2 + 1) * P, 64 * hh, 64 * hh + 64),
                                       kg_t[rows, t, m * P + 64 * hh:m * P + 64 * hh + 64],
                                       b_v[rows, t, head * P:(head + 1) * P], start=True, stop=True)
                mm.then_inc(gl_ds, 1)
                read_by((2 + i % 2, 4 + i % 2), (gl_u, i + 1))
            pe.wait_ge(gl_q, NT)

            def gla_scores(t):
                claim(0, 1, 2, 3)
                cols = slice(t * P, (t + 1) * P)
                for d in range(2):
                    for h in range(4):
                        m, rows = 2 * d + h // 2, slice(64 * (h % 2), 64 * (h % 2) + 64)
                        mm = pe.matmul(ps(2 * d + h % 2, (h // 2) * P, (h // 2 + 1) * P), kg[rows, m, cols],
                                       qg[rows, m, cols], start=True, stop=True)
                mm.then_inc(gl_att, 1)
                read_by((0, 1, 2, 3), (gl_msk, t + 1))

            def gla_turn(t):
                bank = 6 + t % 2
                claim(bank)
                pe.wait_ge(gl_on, t + 1)
                on = b_k[:].rearrange("p a n -> p (a n)")
                for h in range(4):
                    mm = pe.transpose(ps(bank, h * P, (h + 1) * P), on[:, h * P:(h + 1) * P], ident[:])
                mm.then_inc(gl_f, 1)
                read_by((bank,), (gl_full, t + 1))

            gla_scores(0)
            pe.wait_ge(gl_s, 1 + 2 * (2 * NT - 1))
            for t in range(NT):
                claim(4, 5)
                pe.wait_ge(gl_msk, t + 1)
                for d in range(2):
                    for h in range(4):
                        pe.matmul(ps(4 + h % 2, (h // 2) * P, (h // 2 + 1) * P), att_m[:, d, h * P:(h + 1) * P],
                                  b_v[:, t, h * P:(h + 1) * P], start=d == 0 and h < 2, stop=False,
                                  skip_group_check=True)
                for d in range(2):
                    for half in range(2):
                        chunk = 2 * t + half
                        i = (f_order, b_order)[d].index(chunk)
                        for h in range(4):
                            m, rows = 2 * d + h // 2, slice(64 * (h % 2), 64 * (h % 2) + 64)
                            mm = pe.matmul(ps(4 + h % 2, (h // 2) * P, (h // 2 + 1) * P, 64 * half, 64 * half + 64),
                                           qg[rows, m, chunk * CH:(chunk + 1) * CH], state[rows, i, m, :],
                                           start=False, stop=d == 1, skip_group_check=True)
                mm.then_inc(gl_o, 1)
                read_by((4, 5), (gl_on, t + 1))
                if t + 1 < NT:
                    gla_scores(t + 1)
                gla_turn(t)

            gate_rows(0, 2)
            claim(*range(8))
            pe.wait_ge(gl_lo, NT)
            pe.wait_ge(at_lo, NT)
            tm_product("out0L", KT, h_act, L_TILES, two_halves)
            for i in range(LT):
                read_by((2 * i, 2 * i + 1), (post_n, POST["out0L"] + i + 1))
            claim(0, 1, 2, 3)
            tm_product("out0C", KT, h_act, C_TILES, two_halves)
            for i in range(CT):
                read_by((2 * i, 2 * i + 1), (post_n, POST["out0C"] + i + 1))
            pre_turn("ffn0L", L_TILES)
            pe.wait_ge(pre_lo, PRE["ffn0L"] + LT)
            ffn_in(("fi0L", 0), FH, 0, SEQ, {2: lambda: pre_turn("ffn0C", C_TILES), 4: lambda: gate_rows(1, 2)})
            claim(*range(8))
            ffn_out(("fo0L", 0), ("fi0L", 0), FH, L_TILES, SEQ, 0)
            for i in range(LT):
                read_by((2 * i, 2 * i + 1), (half_done, i + 1))
            ffn_in(("fi0L", 1), FH, 0, SEQ)
            claim(*range(8))
            ffn_out(("fo0L", 1), ("fi0L", 1), FH, L_TILES, SEQ, 0)
            for i in range(LT):
                read_by((2 * i, 2 * i + 1), (post_y, i + 1))
            ffn_in("fi0C", FT, SEQ, CTX)
            claim(0, 1, 2, 3)
            ffn_out("fo0C", "fi0C", FT, C_TILES, CTX, LT)
            for i in range(CT):
                read_by((2 * i, 2 * i + 1), (post_n, POST["fo0C"] + i + 1))
            for b in range(6, 12):
                modulation(b)

            gate_rows(2, 1)
            pre_turn("mix1", range(NT))
            pe.wait_ge(pre_lo, PRE["mix1"] + NT)
            for i in range(16):
                bank = 2 * (i % 2)
                claim(bank, bank + 1)
                outs = [(ps(bank, 0, SEQ), 0, SEQ)] + ([(ps(bank + 1, 0, CTX), SEQ, CTX)] if i >= KT else [])
                fm_unit(sp("qk1") + i, outs)
                read_by((bank, bank + 1), (fe1_act, i + 1))
            claim(*range(8))
            tm_product("v1L", KT, h_act, L_TILES, two_halves)
            for i in range(LT):
                read_by((2 * i, 2 * i + 1), (v_act, NT + i + 1))
            claim(0, 1, 2, 3)
            tm_product("v1C", KT, h_act, C_TILES, two_halves)
            for i in range(CT):
                read_by((2 * i, 2 * i + 1), (v_act, NT + LT + i + 1))
            pe.wait_ge(fe1_act, 16)
            pe.wait_ge(rel_in, 16 * 16)
            claim(*range(8))
            attention(1)
            claim(*range(8))
            pe.wait_ge(at_lo, n_groups[0] + n_groups[1])
            tm_product("out1L", KT, h_act, L_TILES, two_halves)
            for i in range(LT):
                read_by((2 * i, 2 * i + 1), (post_n, POST["out1L"] + i + 1))
            pre_turn("ffn1L", L_TILES)
            pe.wait_ge(pre_lo, PRE["ffn1L"] + LT)
            ffn_in(("fi1L", 0), FH, 0, SEQ, {4: lambda: gate_rows(3, 1)})
            claim(*range(8))
            ffn_out(("fo1L", 0), ("fi1L", 0), FH, L_TILES, SEQ, 0)
            for i in range(LT):
                read_by((2 * i, 2 * i + 1), (half_done, LT + i + 1))
            ffn_in(("fi1L", 1), FH, 0, SEQ)
            claim(*range(8))
            ffn_out(("fo1L", 1), ("fi1L", 1), FH, L_TILES, SEQ, 0)


INPUTS = ["x", "c", "ctx", "c_ctx", "w_mod", "b_mod", "g_mix_pre", "g_mix_post", "g_ffn_pre", "g_ffn_post", "w_ffn_in",
          "w_ffn_out", "ab_w_in", "ab_w_out", "a_sink", "gla_gate_f_w", "gla_gate_f_b", "gla_gate_b_w",
          "gla_gate_b_b", "gla_norm_g", "na_w_in", "na_w_out"]


def kernel(**inputs):
    import concourse.bacc as bacc
    from concourse.bass_utils import run_bass_kernel_spmd

    nc = bacc.Bacc("TRN2", target_bir_lowering=False, num_devices=1, dynamic_dma_scratch_size=1024)
    arrays = {name: np.ascontiguousarray(inputs[name]) for name in INPUTS}
    arrays["rel_rev"] = np.ascontiguousarray(np.pad(np.asarray(inputs["na_rel_bias"]).reshape(-1), BIAS_PAD)[::-1])
    arrays |= constants()
    handles = {name: nc.dram_tensor(f"in_{name}", v.shape, mybir.dt.from_np(v.dtype), kind="ExternalInput").ap()
               for name, v in arrays.items()}
    out = nc.dram_tensor("out_y", (1, SEQ, D), F32, kind="ExternalOutput").ap()
    build(nc, handles, out)
    r = run_bass_kernel_spmd(nc, [{f"in_{name}": v for name, v in arrays.items()}], core_ids=[0])
    return r.results[0]["out_y"]
```

```python
from contextlib import ExitStack

import numpy as np

import concourse.bass as bass
from concourse import mybir

F32, F32R, BF16 = mybir.dt.float32, mybir.dt.float32r, mybir.dt.bfloat16
ALU, ACT = mybir.AluOpType, mybir.ActivationFunctionType
AX = mybir.AxisListType.X

P = 128
D = 1024
KT = D // P
SEQ, CTX = 512, 256
LT, CT = SEQ // P, CTX // P
NT = LT + CT
TOK = SEQ + CTX
DFF = 2816
FT = DFF // P
FH = FT // 2
AQ, AKV, BQK, BV, RANK = 512, 128, 256, 512, 16
C_AQ, C_AK, C_AV = 0, AQ, AQ + AKV
C_BQ = C_AV + AKV
C_BK = C_BQ + BQK
C_BV = C_BK + BQK
C_BO = C_BV + BV
AB_IN = C_BO + BV + 2 * RANK
CH = 64
GRID = 64
EPS = 1e-6
NEG = -1e30
SCALE = 0.125
RAW, RING, ACC = 3, 3, 2
BIAS_ROW = 31
BIAS_HEAD = 15 * BIAS_ROW
BIAS_PAD = 16
BIAS_RUN = 7 * BIAS_ROW + 48
L_TILES, C_TILES = list(range(LT)), list(range(LT, NT))
UNIT = 1024


def constants():
    nf = 16
    inv = (10000.0 ** (-np.arange(nf, dtype=np.float32) / nf)).astype(np.float32)
    t = np.arange(SEQ)
    ang = [(t // GRID).astype(np.float32)[None] * inv[:, None], (t % GRID).astype(np.float32)[None] * inv[:, None]]
    cos, sin = np.zeros((P, SEQ), np.float32), np.zeros((P, SEQ), np.float32)
    for p in range(P):
        a = ang[(p % 64) // 32][p % 16]
        cos[p] = np.cos(a)
        sin[p] = np.sin(a) * (-1.0 if p % 32 < 16 else 1.0)
    q, k = np.arange(P)[:, None], np.arange(P)[None]
    window = np.concatenate([np.where(k >= q, 0.0, NEG), np.where(k <= q, 0.0, NEG)], 1).astype(np.float32)
    col = lambda i: 8 * (i // 64) + i % 8
    near = np.full((P, LT, 3 * P), NEG, np.float32)
    for tile in range(LT):
        qc = 16 * tile + col(np.arange(P))
        cs = np.clip(qc - 8, 0, GRID - 16)[:, None]
        for d in range(3):
            kc = (16 * (tile + d - 1) + col(np.arange(P)))[None]
            near[:, tile, d * P:(d + 1) * P] = np.where((kc >= cs) & (kc < cs + 16), 0.0, NEG)
    same = (q // CH) == (k // CH)
    tri = np.stack([same & (q <= k), same & (q >= k)], 1).astype(np.float32)
    return {"k_ident": np.eye(P, dtype=np.float32), "k_cos": cos, "k_sin": sin, "k_window": window,
            "k_near": near.reshape(P, LT * 3 * P), "k_tri": tri.reshape(P, 2 * P)}


def weight_units(a):
    units = []
    start = {}
    w_mod = [(block, k) for block in range(2, 12) for k in range(KT)]

    def begin(name):
        start[name] = len(units)

    def modulations(n):
        for block, k in w_mod[:n]:
            l, i = divmod(block, 6)
            units.append(("acc", [("tm", 0, D, a["w_mod"][l, k * P:(k + 1) * P, i * D:(i + 1) * D])]))
        del w_mod[:n]

    def fm(w, parts):
        src = w.rearrange("(k p) n -> p k n", p=P)
        units.append(("split", [("fm", at, width, src[:, :, c:c + width]) for at, c, width in parts]))

    def tm(w, k, parts):
        units.append(("split", [("tm", at, width, w[k * P:(k + 1) * P, c:c + width]) for at, c, width in parts]))

    def ffn_in(name, l, js, n_mod=0):
        begin(name)
        for n, j in enumerate(js):
            fm(a["w_ffn_in"][l], [(0, j * P, P)])
            modulations(n_mod if n > 1 else 0)
            fm(a["w_ffn_in"][l], [(0, DFF + j * P, P)])
            modulations(n_mod if n else 0)

    def rows(name, w, ks, n_mod=0):
        begin(name)
        for n, k in enumerate(ks):
            tm(w, k, [(0, 0, D)])
            modulations(int(n < n_mod))

    for block in range(2):
        begin(("mod", block))
        for k in range(KT):
            units.append(("direct", [("tm", 0, D, a["w_mod"][0, k * P:(k + 1) * P, block * D:(block + 1) * D])]))
    w = a["ab_w_in"][0]
    begin("v0")
    for k in range(KT):
        tm(w, k, [(0, C_AV, AKV), (AKV, C_BV, BV)])
        modulations(int(k >= 2) + int(k >= 6))
    begin("in0")
    parts = [[(0, C_AQ + j * P, P)] for j in range(4)]
    parts += [[(0, C_AK + 64 * j, 64), (64, C_AK + 64 * j, 64)] for j in range(2)]
    parts += [[(0, c + j * P, P)] for c, n in ((C_BQ, 2), (C_BK, 2), (C_BO, 4)) for j in range(n)]
    parts += [[(0, AB_IN - P, P)]]
    for i, part in enumerate(parts):
        fm(w, part)
        modulations(1 if i < 6 else 2)
    rows("out0L", a["ab_w_out"][0], range(KT))
    rows("out0C", a["ab_w_out"][0], range(KT))
    for half in range(2):
        ffn_in(("fi0L", half), 0, range(FH * half, FH * half + FH), 1)
        rows(("fo0L", half), a["w_ffn_out"][0], range(FH * half, FH * half + FH), 5)
    ffn_in("fi0C", 0, range(FT))
    rows("fo0C", a["w_ffn_out"][0], range(FT))
    w = a["na_w_in"][0]
    begin("qk1")
    for j in range(16):
        fm(w, [(0, j * P, P)])
    begin("v1L")
    for k in range(KT):
        tm(w, k, [(0, 2 * D, D)])
    begin("v1C")
    for k in range(KT):
        tm(w, k, [(0, 2 * D, D)])
    rows("out1L", a["na_w_out"][0], range(KT))
    for half in range(2):
        ffn_in(("fi1L", half), 1, range(FH * half, FH * half + FH))
        rows(("fo1L", half), a["w_ffn_out"][1], range(FH * half, FH * half + FH))
    return units, start


def attention_steps(layer):
    if layer == 0:
        return [(t, 0, h) for t in range(NT) for h in range(8)]
    return [(t, g, h) for g in range(2) for t in range(LT) for h in range(8)]


def local_tiles(t):
    return [u for u in (t - 1, t, t + 1) if 0 <= u < LT] if t < LT else []


def build(nc, a, out):
    units, start = weight_units(a)
    kind_no, n_kind = [], {"split": 0, "direct": 0, "acc": 0}
    for kind, _ in units:
        kind_no.append(n_kind[kind])
        n_kind[kind] += 1
    acc_unit = [u for u, x in enumerate(units) if x[0] == "acc"]
    acc_after = [sum(x[0] == "split" for x in units[:u]) for u in acc_unit]
    ring_no, in_ring, landed_value, count = [], ([], []), [], {}
    for u, (kind, parts) in enumerate(units):
        acc = kind == "acc"
        n = len(in_ring[acc])
        slot = (acc, n % (ACC if acc else RAW))
        count[slot] = count.get(slot, 0) + 16 * len(parts)
        ring_no.append(n)
        in_ring[acc].append(u)
        landed_value.append(count[slot])
    unit_of_split = [u for u, x in enumerate(units) if x[0] == "split"]

    def sp(name):
        return kind_no[start[name]]

    by_dve = [False] * n_kind["split"]
    for name, n in (("fi0C", 2 * FT), ("fo0C", FT), ("v1C", KT)):
        for u in range(sp(name), sp(name) + n):
            by_dve[u] = True
    low_no = [sum(x == by_dve[u] for x in by_dve[:u]) for u in range(len(by_dve))]

    with ExitStack() as ctx:
        def sb(name, shape, dt=F32, scope=ctx):
            return scope.enter_context(nc.sbuf_tensor(name, shape, dt))

        x_res = sb("x_res", [P, NT, D])
        h_hi = sb("h_hi", [P, KT, TOK], F32R)
        h_lo = sb("h_lo", [P, KT, TOK], F32R)
        w_raw = sb("w_raw", [P, RAW, UNIT])
        w_hi = sb("w_hi", [P, RING, UNIT], F32R)
        w_lo = sb("w_lo", [P, RING, UNIT], F32R)
        with ExitStack() as early:
            state = sb("state", [P, 11, 4, P], scope=early)
        with ExitStack() as early:
            sb("before", [P, 2 * D], scope=early)
            bias_m = sb("bias_m", [P, 2, 3 * P], scope=early)
        gate_b = sb("gate_b", [P, 2, D])
        xs = sb("xs", [P, 2, D])
        full = sb("full", [P, KT, P])
        junk = sb("junk", [P, D], BF16)
        ident = sb("ident", [P, P])
        ident_b = sb("ident_b", [P, P], BF16)
        window_b = sb("window_b", [P, 2 * P], BF16)
        near_b = sb("near_b", [P, LT, 3 * P], BF16)
        tri = sb("tri", [P, 2, P])
        bias_col = sb("bias_col", [P, 96])
        par_col = sb("par_col", [P, 84])
        c_col = sb("c_col", [P, KT, 2])
        mod_col = sb("mod_col", [P, 12, 2, KT])
        pre_a = sb("pre_a", [P, 4, 2, KT])
        gate_col = sb("gate_col", [P, 4, 2, KT])
        half_neg = sb("half_neg", [P, 8])
        one_col = sb("one_col", [P, 1])
        sink = sb("sink", [P, 8])
        nsink = sb("nsink", [P, 8])
        negm = sb("negm", [P, 2, 8])
        rowsum = sb("rowsum", [P, 2, 8])
        sm = sb("sm", [P, 4, 8])
        raw_max = sb("raw_max", [P, 2])
        ctx_max = sb("ctx_max", [P, 2])
        ssq_pre, ms_pre, rs_pre = (sb(n, [P, 24]) for n in ("ssq_pre", "ms_pre", "rs_pre"))
        ssq_post, ms_post, rs_post = (sb(n, [P, 24]) for n in ("ssq_post", "ms_post", "rs_post"))
        gla_ssq, gla_ms, gla_rs = (sb(n, [P, NT, 4]) for n in ("gla_ssq", "gla_ms", "gla_rs"))
        decay = sb("decay", [P, 4, 2 * NT])

        with ExitStack() as s0:
            par_rows = sb("par_rows", [P, 2, P], scope=s0)
            mask_in = sb("mask_in", [P, 2 * P + LT * 3 * P], scope=s0)
            sb("fence0", [P, 64], scope=s0)
        with ExitStack() as s1:
            b_q = sb("b_q", [P, 2, TOK], scope=s1)
            b_k = sb("b_k", [P, 2, TOK], scope=s1)
            b_v = sb("b_v", [P, NT, BV], scope=s1)
            b_o = sb("b_o", [P, 4, TOK], scope=s1)
            r_t = sb("r_t", [33, TOK], scope=s1)
            gw = sb("gw", [33, 2 * BQK], scope=s1)
            with ExitStack() as s2:
                cos = sb("cos", [P, SEQ], scope=s2)
                sin = sb("sin", [P, SEQ], scope=s2)
                rope_t = sb("rope_t", [P, 2, SEQ], scope=s2)
                a_q = sb("a_q", [P, 4, TOK], scope=s2)
                a_k = sb("a_k", [P, 2, TOK], scope=s2)
                a_v = sb("a_v", [P, NT, AKV], scope=s2)
                prob0 = sb("prob0", [P, 2, 5 * P], scope=s2)
                prob0_t = sb("prob0_t", [P, 2, 5 * P], scope=s2)
            with ExitStack() as s2:
                with ExitStack() as s3:
                    la = sb("la", [P, NT, 2 * BQK], scope=s3)
                kg_t = sb("kg_t", [P, NT, 2 * BQK], scope=s2)
                qg = sb("qg", [P, 4, TOK], scope=s2)
                kg = sb("kg", [P, 4, TOK], scope=s2)
                att_m = sb("att_m", [P, 2, 4 * P], scope=s2)
        with ExitStack() as s1:
            hid_hi = sb("hid_hi", [P, FH * SEQ], F32R, scope=s1)
            hid_lo = sb("hid_lo", [P, FH * SEQ], F32R, scope=s1)
            y_half = sb("y_half", [P, LT, D], scope=s1)
            silu_g = sb("silu_g", [P, 2, SEQ], scope=s1)
            hid_f = sb("hid_f", [P, 2, SEQ], scope=s1)
            mod_acc = sb("mod_acc", [P, 2, D], scope=s1)
            mod_raw = sb("mod_raw", [P, ACC, UNIT], scope=s1)
        with ExitStack() as s1:
            c_q = sb("c_q", [P, KT, SEQ], scope=s1)
            c_k = sb("c_k", [P, KT, TOK], scope=s1)
            c_v = sb("c_v", [P, NT, D], scope=s1)
            rel = sb("rel", [P, 8, BIAS_RUN], scope=s1)
            prob1 = sb("prob1", [P, 2, 5 * P], scope=s1)
            prob1_t = sb("prob1_t", [P, 2, 5 * P], scope=s1)

        PS = ctx.enter_context(nc.psum_tensor("ps", [P, 8, 512], F32))

        def ps(bank, lo, hi, p0=0, p1=P):
            return PS[p0:p1].rearrange("p b n -> p (b n)")[:, bank * 512 + lo:bank * 512 + hi]

        def sem(name):
            return ctx.enter_context(nc.semaphore(name))

        landed = [sem(f"w_landed{i}") for i in range(RAW)]
        acc_landed = [sem(f"acc_landed{i}") for i in range(ACC)]
        (consts_in, par_in, x_in, gw_zero, gw_in, rel_in, stored) = map(sem, (
            "consts_in", "par_in", "x_in", "gw_zero", "gw_in", "rel_in", "stored"))
        w_lo_dve, w_acc = sem("w_lo_dve"), sem("w_acc")
        (w_hi_done, w_lo_done, w_used, w_direct, tm_done) = map(sem, (
            "w_hi_done", "w_lo_done", "w_used", "w_direct", "tm_done"))
        (small_done, par_turned, par_done, c_done) = map(sem, ("small_done", "par_turned", "par_done", "c_done"))
        (mod_copied, mod_turned, mod_done, mod_der) = map(sem, ("mod_copied", "mod_turned", "mod_done", "mod_der"))
        (gb_ready, gb_done) = map(sem, ("gb_ready", "gb_done"))
        (pre_ssq, pre_ms, pre_rs, pre_xs, pre_tr, pre_full, pre_hi, pre_lo) = map(sem, (
            "pre_ssq", "pre_ms", "pre_rs", "pre_xs", "pre_tr", "pre_full", "pre_hi", "pre_lo"))
        (post_y, post_ssq, post_ms, post_rs, post_n, post_x) = map(sem, (
            "post_y", "post_ssq", "post_ms", "post_rs", "post_n", "post_x"))
        (v_act, v_dve, fe_act, fe_dve, rope_m, rope_done, bo_done, fe1_act) = map(sem, (
            "v_act", "v_dve", "fe_act", "fe_dve", "rope_m", "rope_done", "bo_done", "fe1_act"))
        (ff_silu, ff_full, ff_hi, ff_lo, half_done) = map(sem, ("ff_silu", "ff_full", "ff_hi", "ff_lo", "half_done"))
        at_c, at_b = sem("at_c"), sem("at_b")
        (at_s, at_r, at_m, at_p, at_t, at_e, at_o) = map(sem, (
            "at_s", "at_r", "at_m", "at_p", "at_t", "at_e", "at_o"))
        (at_shift, at_sink, at_den, at_rinv, at_on, at_f, at_hi, at_lo) = map(sem, (
            "at_shift", "at_sink", "at_den", "at_rinv", "at_on", "at_f", "at_hi", "at_lo"))
        (gl_z, gl_abs, gl_exp, gl_ln, gl_la, gl_cum, gl_eq, gl_ek, gl_dec, gl_q, gl_k, gl_kt, gl_ktc) = map(sem, (
            "gl_z", "gl_abs", "gl_exp", "gl_ln", "gl_la", "gl_cum", "gl_eq", "gl_ek", "gl_dec", "gl_q", "gl_k",
            "gl_kt", "gl_ktc"))
        (gl_ds, gl_u, gl_s, gl_att, gl_msk, gl_o, gl_ssq, gl_ms, gl_rs, gl_on, gl_f, gl_full, gl_hi, gl_lo) = map(
            sem, ("gl_ds", "gl_u", "gl_s", "gl_att", "gl_msk", "gl_o", "gl_ssq", "gl_ms", "gl_rs", "gl_on", "gl_f",
                  "gl_full", "gl_hi", "gl_lo"))

        TM = [("v0", 6), ("out0L", 4), ("out0C", 2), (("fo0L", 0), 4), (("fo0L", 1), 4), ("fo0C", 2), ("v1L", 4),
              ("v1C", 2), ("out1L", 4), (("fo1L", 0), 4), (("fo1L", 1), 4)]
        tm_base, n = {}, 0
        for name, tiles in TM:
            tm_base[name] = (n, tiles)
            n += tiles - 1
        PRE = {"mix0": 0, "ffn0L": 6, "ffn0C": 10, "mix1": 12, "ffn1L": 18}
        POST = {"out0L": 0, "out0C": 4, "fo0L": 6, "fo0C": 10, "out1L": 12, "fo1L": 16}
        FI = {("fi0L", 0): 0, ("fi0L", 1): FH, "fi0C": 2 * FH, ("fi1L", 0): 4 * FH, ("fi1L", 1): 5 * FH}
        n_groups = {0: NT, 1: 2 * LT}
        STEPS = {0: attention_steps(0), 1: attention_steps(1)}
        STEP0 = {0: 0, 1: len(STEPS[0])}
        GROUP0 = {0: 0, 1: n_groups[0]}
        f_order = [8, 9, 10, 11, 0, 1, 2, 3, 4, 5, 6, 7]
        b_order = [11, 10, 9, 8, 7, 6, 5, 4, 3, 2, 1, 0]

        def wait_tm(eng, name, i, k_units):
            base, tiles = tm_base[name]
            if i == tiles - 1:
                eng.wait_ge(w_used, sp(name) + k_units)
            else:
                eng.wait_ge(tm_done, base + i + 1)

        def qk_bank(i):
            return 6 + i if i < 2 else 2 * (i % 2)

        def low_ready(s):
            return (w_lo_dve if by_dve[s] else w_lo_done), low_no[s] + 1

        def acc_slot(n):
            if n < 4 * KT:
                return (prob0, prob0_t)[n % ACC][:].rearrange("p a n -> p (a n)")[:, 0:UNIT]
            return mod_raw[:, n % ACC, :]

        def low_part(eng, u):
            raw = unit_of_split[u]
            width = sum(w for _, _, w, _ in units[raw][1]) * (KT if units[raw][1][0][0] == "fm" else 1)
            eng.wait_ge(w_hi_done, u + 1)
            if u >= RING:
                eng.wait_ge(w_used, u - RING + 1)
            eng.tensor_tensor(w_lo[:, u % RING, 0:width], w_raw[:, ring_no[raw] % RAW, 0:width],
                              w_hi[:, u % RING, 0:width].bitcast(F32), ALU.subtract).then_inc(low_ready(u)[0], 1)

        def bcast(ap, n):
            return bass.AP(ap.tensor, ap.offset, [list(x) for x in ap.ap] + [[0, n]])

        def group_out(layer, t, g, f):
            if layer == 0:
                return lambda h: h[:, 4 * g + f, t * P:(t + 1) * P], lambda x: x
            return (lambda h: h[:, 4 * g + f, 0:SEQ].rearrange("p (r b c) -> p b r c", b=8, c=8)[:, 2 * t:2 * t + 2],
                    lambda x: x.rearrange("p (b r c) -> p b r c", b=2, c=8))

        def grid_order(h, k, t):
            return h[:, k, 0:SEQ].rearrange("p (b r c) -> p r b c", b=8, c=8)[:, 2 * t:2 * t + 2]

        def rel_load(g, part=0):
            b, r = divmod(part, 8)
            p = 64 * b + 8 * r
            first = BIAS_PAD + (8 * g + 7) * BIAS_HEAD + (7 - r) * BIAS_ROW - 1 - 8 * b
            first = 2 * BIAS_PAD + 16 * BIAS_HEAD - 1 - (first + BIAS_RUN - 1)
            return rel[p:p + 8], bass.AP(a["rel_rev"].tensor, first, [[1, 8], [BIAS_HEAD, 8], [1, BIAS_RUN]])

        gb_base, gb_after = [0, 2, 4, 5], [0, 6, 12, 16]
        gb_need = {"out0L": (1, 2), "out0C": (1, 2), "fo0L": (3, 4), "fo0C": (3, 4), "out1L": (5, 5), "fo1L": (6, 6)}
        tm_name = {"out0L": "out0L", "out0C": "out0C", "fo0C": "fo0C", "out1L": "out1L"}
        n_y = {"fo0L": 0, "fo1L": LT}
        full_free = {"out0L": (at_f, n_groups[0]), "out0C": (at_f, n_groups[0]), "fo0L": (pre_lo, PRE["mix1"]),
                     "fo0C": (pre_lo, PRE["mix1"] + LT), "out1L": (at_f, n_groups[0] + n_groups[1]),
                     "fo1L": (pre_lo, PRE["ffn1L"] + LT)}
        posts_before = {"mix0": 0, "ffn0L": 6, "ffn0C": 6, "ffn1L": 16}

        def s_cols(layer, a):
            t = STEPS[layer][a][0]
            return (len(local_tiles(t)) + CT) * P

        block = ctx.enter_context(nc.Block())

        @block.sync
        def _(sync):
            for dst, src in ((ident[:], a["k_ident"]), (tri[:].rearrange("p a n -> p (a n)"), a["k_tri"]),
                             (mask_in[:, 0:2 * P], a["k_window"]), (mask_in[:, 2 * P:], a["k_near"]),
                             (cos[:], a["k_cos"]), (sin[:], a["k_sin"])):
                sync.dma_start(dst, src).then_inc(consts_in, 16)
            sync.dma_start(par_rows[0:96, 0, :], a["b_mod"].rearrange("l (r n) -> (l r) n", n=P)).then_inc(par_in, 16)
            at = 0
            for name in ("g_mix_pre", "g_mix_post", "g_ffn_pre", "g_ffn_post", "gla_norm_g"):
                src = a[name].rearrange("l (r n) -> (l r) n", n=P)
                n = src.shape[0]
                sync.dma_start(par_rows[at:at + n, 1, :], src).then_inc(par_in, 16)
                at += n
            for src in (a["c"].rearrange("b (r n) -> (b r) n", n=P), a["c_ctx"].rearrange("(r n) -> r n", n=P)):
                sync.dma_start(par_rows[at:at + KT, 1, :], src).then_inc(par_in, 16)
                at += KT
            sync.dma_start(sink[:], a["a_sink"].partition_broadcast(P)).then_inc(par_in, 16)
            sync.dma_start(x_res[:, 0:LT, :], a["x"][0].rearrange("(t p) d -> p t d", p=P)).then_inc(x_in, 16)
            sync.dma_start(x_res[:, LT:NT, :], a["ctx"][0].rearrange("(t p) d -> p t d", p=P)).then_inc(x_in, 16)
            for u, (kind, parts) in enumerate(units):
                n = ring_no[u]
                if kind == "acc":
                    if n >= ACC:
                        sync.wait_ge(w_acc, n - ACC + 1)
                    sync.dma_start(acc_slot(n), parts[0][3]).then_inc(acc_landed[n % ACC], 16)
                    continue
                if n >= RAW:
                    v = in_ring[0][n - RAW]
                    if units[v][0] == "direct":
                        sync.wait_ge(w_direct, kind_no[v] + 1)
                    else:
                        sync.wait_ge(w_hi_done, kind_no[v] + 1)
                        sync.wait_ge(*low_ready(kind_no[v]))
                for layout, at, width, src in parts:
                    dst = w_raw[:, n % RAW, :]
                    if layout == "fm":
                        dst = dst.rearrange("p (k n) -> p k n", k=KT)
                        dst = dst[:, :, at:at + width]
                    else:
                        dst = dst[:, at:at + width]
                    sync.dma_start(dst, src).then_inc(landed[n % RAW], 16)
            for t in L_TILES:
                sync.wait_ge(post_x, POST["fo1L"] + t + 1)
                sync.dma_start(out[0, t * P:(t + 1) * P, :], x_res[:, t, :]).then_inc(stored, 16)
            sync.wait_ge(stored, 16 * LT)

        @block.gpsimd
        def _(pool):
            pool.memset(half_neg[:], -0.5).then_inc(small_done, 1)
            pool.memset(one_col[:], 1.0).then_inc(small_done, 1)
            pool.wait_ge(small_done, 2)
            fed = [0]

            def feed(s):
                while fed[0] <= s:
                    if not by_dve[fed[0]]:
                        low_part(pool, fed[0])
                    fed[0] += 1

            def root(ssq, m, r, width, n_done, s_ssq, s_ms, s_rs, sums=1):
                pool.wait_ge(s_ssq, sums * (n_done + 1))
                pool.tensor_scalar(m, ssq, 1.0 / width, EPS, ALU.mult, ALU.add).then_inc(s_ms, 1)
                pool.wait_ge(s_ms, n_done + 1)
                pool.tensor_tensor(r, m, half_neg[:, 0:m.shape[1]], ALU.pow).then_inc(s_rs, 1)

            def pre(name, i):
                n = PRE[name] + i
                root(ssq_pre[:, n:n + 1], ms_pre[:, n:n + 1], rs_pre[:, n:n + 1], D, n, pre_ssq, pre_ms, pre_rs)

            def post(name, i):
                n = POST[name] + i
                root(ssq_post[:, n:n + 1], ms_post[:, n:n + 1], rs_post[:, n:n + 1], D, n,
                     post_ssq, post_ms, post_rs)

            for i in range(NT):
                pre("mix0", i)
            feed(sp("in0") + 14)
            for t in range(NT):
                root(gla_ssq[:, t, :], gla_ms[:, t, :], gla_rs[:, t, :], P, t, gl_ssq, gl_ms, gl_rs, 4)
            feed(sp("out0C") + RING - 1)
            for i in range(LT):
                post("out0L", i)
                feed(sp("out0C") + i + RING - 2)
            for i in range(LT):
                pre("ffn0L", i)
                feed(sp("out0C") + 4 + i + RING - 2)
            feed(sp(("fi0L", 0)) + RING - 1)
            for i in range(CT):
                post("out0C", i)
            for i in range(CT):
                pre("ffn0C", i)
            feed(sp("fi0C") + RING - 1)
            for j in range(LT + 1):
                if j < LT:
                    post("fo0L", j)
                if j:
                    pre("mix1", j - 1)
            for i in range(CT):
                post("fo0C", i)
            for i in range(CT):
                pre("mix1", LT + i)
            feed(sp("v1C") + 7)
            for i, (t, _, h) in enumerate(STEPS[1]):
                near = local_tiles(t)
                d0 = near[0] - t + 1
                run = rel[:, 7 - h, BIAS_RUN - 1 - 16 * d0:BIAS_RUN - 16 * d0]
                run = bass.AP(run.tensor, run.offset,
                              [list(run.ap[0]), [-8, 2 * len(near)], [-BIAS_ROW, 8], [-1, 8]])
                split = lambda x: x.rearrange("p (b r c) -> p b r c", r=8, c=8)
                pool.wait_ge(rel_in, 16 * (32 if i >= len(STEPS[1]) // 2 else 16))
                if i == 0:
                    pool.wait_ge(pre_tr, PRE["mix1"] + NT)
                if i >= 2:
                    pool.wait_ge(at_r, STEP0[1] + i - 1)
                pool.tensor_tensor(split(bias_m[:, i % 2, 0:len(near) * P]), run,
                                   split(near_b[:, t, d0 * P:(d0 + len(near)) * P]), ALU.add).then_inc(at_b, 1)
            feed(sp("out1L") + 7)
            feed(sp(("fi1L", 0)) + RING - 1)
            for i in range(LT):
                post("out1L", i)
            for i in range(LT):
                pre("ffn1L", i)
            feed(sp(("fo1L", 1)) + FH - 1)
            for i in range(LT):
                post("fo1L", i)

        @block.scalar
        def _(act):
            fed = [0]
            junk_written = []

            def square(src, ssq, done, value, into=junk):
                if junk_written:
                    act.wait_ge(*junk_written.pop())
                act.activation(into[:, 0:src.shape[1]], src, ACT.Square, accum_out=ssq).then_inc(done, 1)
                junk_written.append((done, value))

            def feed(s):
                while fed[0] <= min(s, n_kind["split"] - 1):
                    u = fed[0]
                    raw = unit_of_split[u]
                    width = sum(w for _, _, w, _ in units[raw][1]) * (KT if units[raw][1][0][0] == "fm" else 1)
                    act.wait_ge(landed[ring_no[raw] % RAW], landed_value[raw])
                    if u >= RING:
                        act.wait_ge(w_used, u - RING + 1)
                    act.activation(w_hi[:, u % RING, 0:width], w_raw[:, ring_no[raw] % RAW, 0:width],
                                   ACT.Copy).then_inc(w_hi_done, 1)
                    fed[0] += 1

            def pre_square(name, i, tiles, ready):
                n = PRE[name] + i
                act.wait_ge(*ready)
                square(x_res[:, tiles[i], :], ssq_pre[:, n:n + 1], pre_ssq, n + 1)

            def pre_high(name, i, tiles):
                n, t = PRE[name] + i, tiles[i]
                act.wait_ge(pre_full, n + 1)
                if name == "mix1" and t < LT:
                    for k in range(KT):
                        last = act.activation(grid_order(h_hi, k, t), full[:, k, :].rearrange(
                            "p (r b c) -> p r b c", b=8, c=8), ACT.Copy)
                else:
                    last = act.activation(h_hi[:, :, t * P:(t + 1) * P], full[:], ACT.Copy)
                last.then_inc(pre_hi, 1)

            def post_square(name, i, k_units=None):
                n = POST[name] + i
                if k_units is None:
                    act.wait_ge(post_y, n_y[name] + i + 1)
                    src = y_half[:, i, :]
                else:
                    wait_tm(act, tm_name[name], i, k_units)
                    src = ps(2 * i, 0, D)
                square(src, ssq_post[:, n:n + 1], post_ssq, n + 1)

            def gate_rows(b, n_lc):
                for lc in range(n_lc):
                    act.wait_ge(gb_ready, gb_base[b] + lc + 1)
                    if gb_after[b]:
                        act.wait_ge(post_n, gb_after[b])
                    act.activation(gate_b[:, lc, :], ps(4 + 2 * lc, 0, D), ACT.Copy).then_inc(gb_done, 1)

            def ffn_in(name, n_js, width, hooks=None):
                s, f0 = sp(name), FI[name]
                for j in range(n_js):
                    f = f0 + j
                    feed(s + 2 * j + RING - 1)
                    act.wait_ge(w_used, s + 2 * j + 1)
                    if f >= 2:
                        act.wait_ge(ff_full, f - 1)
                    act.activation(silu_g[:, f % 2, 0:width], ps(2 * (f % 2), 0, width), ACT.Silu)\
                        .then_inc(ff_silu, 1)
                    feed(s + 2 * j + 2 + RING - 2)
                    act.wait_ge(ff_full, f + 1)
                    act.activation(hid_hi[:, j * width:(j + 1) * width], hid_f[:, f % 2, 0:width], ACT.Copy)\
                        .then_inc(ff_hi, 1)
                    feed(s + 2 * j + 3 + RING - 2)
                    if hooks and j in hooks:
                        hooks[j]()

            def attention(layer):
                steps, a0, g0 = STEPS[layer], STEP0[layer], GROUP0[layer]
                prob = (prob0, prob1)[layer]

                def softmax(i):
                    a, n = a0 + i, s_cols(layer, i)
                    g, h = g0 + i // 8, steps[i][2]
                    act.wait_ge(at_m, a + 1)
                    if a >= 2:
                        act.wait_ge(at_t, a - 1)
                    act.activation(prob[:, i % 2, 0:n], ps(2 * (i % 2), 0, n), ACT.Exp, bias=negm[:, g % 2, h:h + 1],
                                   scale=SCALE if layer == 0 else 1.0,
                                   accum_out=rowsum[:, g % 2, h:h + 1]).then_inc(at_p, 1)

                def high(gi):
                    t, grp, _ = steps[8 * gi]
                    act.wait_ge(at_f, g0 + gi + 1)
                    for f in range(4):
                        dst, order = group_out(layer, t, grp, f)
                        last = act.activation(dst(h_hi), order(ps(6 + gi % 2, f * P, (f + 1) * P)), ACT.Copy)
                    last.then_inc(at_hi, 1)

                n_pairs = len(steps) // 2
                for p in range(n_pairs + 4):
                    if p < n_pairs:
                        softmax(2 * p)
                        softmax(2 * p + 1)
                    if layer == 1 and p == n_pairs // 2 - 1:
                        act.wait_ge(at_b, len(steps) // 2)
                        for part in range(16):
                            act.dma_start(*rel_load(1, part)).then_inc(rel_in, 16)
                    if p % 4 == 3 and p < n_pairs and layer == 0:
                        act.wait_ge(at_shift, p // 4 + 1)
                        act.activation(sm[:, 1, :], sm[:, 0, :], ACT.Exp).then_inc(at_sink, 1)
                    if p % 4 == 3 and p > 4:
                        high(p // 4 - 1)

            act.wait_ge(gw_zero, 1)
            act.dma_start(gw[0:RANK, 0:BQK], a["gla_gate_f_w"][0]).then_inc(gw_in, 16)
            act.dma_start(gw[RANK:2 * RANK, BQK:], a["gla_gate_b_w"][0]).then_inc(gw_in, 16)
            act.dma_start(gw[2 * RANK:, 0:BQK], a["gla_gate_f_b"]).then_inc(gw_in, 16)
            act.dma_start(gw[2 * RANK:, BQK:], a["gla_gate_b_b"]).then_inc(gw_in, 16)
            act.wait_ge(par_done, 2)
            act.activation(c_col[:], par_col[:, 68:84].rearrange("p (v k) -> p k v", v=2), ACT.Silu)\
                .then_inc(c_done, 1)
            act.wait_ge(x_in, 32)
            act.wait_ge(consts_in, 16 * 6)
            for i in range(NT):
                pre_square("mix0", i, range(NT), (x_in, 32))
            feed(sp("v0") + RING - 1)
            for i in range(NT):
                pre_high("mix0", i, range(NT))
            feed(sp("in0") + 1)
            for t in range(NT):
                wait_tm(act, "v0", t, KT)
                act.activation(b_v[:, t, :], ps(t, 0, BV), ACT.Copy).then_inc(v_act, 1)
            for i in range(15):
                s = sp("in0") + i
                feed(s + RING - 1)
                act.wait_ge(w_used, s + 1)
                bl, bc = 2 * (i % 2), 2 * (i % 2) + 1
                lat, con = ps(bl, 0, SEQ), ps(bc, 0, CTX)
                if i < 6:
                    dst = a_q[:, i] if i < 4 else a_k[:, i - 4]
                    act.activation(dst[:, SEQ:], con, ACT.Copy).then_inc(fe_act, 1)
                    continue
                if i < 8:
                    dst, fn, scale = b_q[:, i - 6], ACT.Copy, SCALE
                elif i < 10:
                    dst, fn, scale = b_k[:, i - 8], ACT.Copy, 1.0
                elif i < 14:
                    dst, fn, scale = b_o[:, i - 10], ACT.Silu, 1.0
                else:
                    dst, fn, scale = r_t[0:32], ACT.Copy, 1.0
                    lat, con = ps(bl, 0, SEQ, 96, P), ps(bc, 0, CTX, 96, P)
                act.activation(dst[:, 0:SEQ], lat, fn, scale=scale)
                act.activation(dst[:, SEQ:], con, fn, scale=scale).then_inc(fe_act, 1)
            attention(0)

            for t in range(NT):
                act.wait_ge(gl_z, t + 1)
                if t == 0:
                    act.wait_ge(at_lo, n_groups[0])
                act.activation(la[:, t, :], ps(t, 0, 512), ACT.Abs).then_inc(gl_abs, 1)
                act.wait_ge(gl_abs, t + 1)
                act.activation(la[:, t, :], la[:, t, :], ACT.Exp, scale=-1.0).then_inc(gl_exp, 1)
            for t in range(NT):
                act.wait_ge(gl_exp, t + 1)
                act.activation(la[:, t, :], la[:, t, :], ACT.Ln, bias=one_col[:]).then_inc(gl_ln, 1)
            for t in range(NT):
                act.wait_ge(gl_cum, t + 1)
                src = ps(6 + t % 2, 0, 512).rearrange("p (m n) -> p m n", m=4)
                act.activation(qg[:, :, t * P:(t + 1) * P], src, ACT.Exp, scale=1.0 / 16).then_inc(gl_eq, 1)
                act.activation(kg[:, :, t * P:(t + 1) * P], src, ACT.Exp, scale=-1.0 / 16).then_inc(gl_ek, 1)

            def gla_high(t):
                act.wait_ge(gl_full, t + 1)
                act.activation(h_hi[:, 4:8, t * P:(t + 1) * P],
                               b_q[:].rearrange("p a n -> p (a n)")[:, 0:512].rearrange("p (h n) -> p h n", h=4),
                               ACT.Copy).then_inc(gl_hi, 1)

            for t in range(NT):
                act.wait_ge(gl_o, t + 1)
                for h in range(4):
                    square(ps(4 + h % 2, (h // 2) * P, (h // 2 + 1) * P), gla_ssq[:, t, h:h + 1], gl_ssq, 4 * t + h + 1,
                           kg_t[:, 0])
                if t:
                    gla_high(t - 1)
            gla_high(NT - 1)

            gate_rows(0, 2)
            feed(sp("out0C") + RING - 1)
            for i in range(LT):
                post_square("out0L", i, KT)
                feed(sp("out0C") + i + RING - 2)
            for i in range(LT):
                pre_square("ffn0L", i, L_TILES, (post_x, POST["out0L"] + i + 1))
                feed(sp("out0C") + 4 + i + RING - 2)
            feed(sp(("fi0L", 0)) + RING - 1)
            for i in range(CT):
                post_square("out0C", i, KT)
            for i in range(CT):
                pre_square("ffn0C", i, C_TILES, (post_x, POST["out0C"] + i + 1))
            for i in range(LT):
                pre_high("ffn0L", i, L_TILES)
            ffn_in(("fi0L", 0), FH, SEQ,
                   {0: lambda: [pre_high("ffn0C", i, C_TILES) for i in range(CT)], 4: lambda: gate_rows(1, 2)})
            feed(sp(("fi0L", 1)) + RING - 1)
            ffn_in(("fi0L", 1), FH, SEQ)
            feed(sp("fi0C") + RING - 1)
            hooks = {j: (lambda i=j: (post_square("fo0L", i) if i < LT else None,
                                      pre_square("mix1", i - 1, L_TILES, (post_x, POST["fo0L"] + i)) if i else None))
                     for j in range(LT + 1)}
            hooks |= {6 + 2 * j: (lambda i=j: pre_high("mix1", i, L_TILES)) for j in range(LT)}
            ffn_in("fi0C", FT, CTX, hooks)
            feed(sp("fo0C") + FT - 1)
            for i in range(CT):
                post_square("fo0C", i, FT)
            for i in range(CT):
                pre_square("mix1", LT + i, range(NT), (post_x, POST["fo0C"] + i + 1))

            feed(sp("qk1") + RING - 1)
            for i in range(16):
                s = sp("qk1") + i
                feed(s + RING - 1)
                act.wait_ge(w_used, s + 1)
                bank = qk_bank(i)
                if i == 0:
                    act.dma_start(*rel_load(0)).then_inc(rel_in, 16)
                    for other in range(1, 16):
                        act.dma_start(*rel_load(0, other)).then_inc(rel_in, 16)
                if i < KT:
                    act.activation(c_q[:, i, :], ps(bank, 0, SEQ), ACT.Copy, scale=SCALE).then_inc(fe1_act, 1)
                    if i == 4:
                        for t in C_TILES:
                            pre_high("mix1", t, range(NT))
                else:
                    act.activation(c_k[:, i - KT, 0:SEQ], ps(bank, 0, SEQ), ACT.Copy)
                    act.activation(c_k[:, i - KT, SEQ:], ps(bank + 1, 0, CTX), ACT.Copy).then_inc(fe1_act, 1)
            gate_rows(2, 1)
            for name, tiles in (("v1L", L_TILES), ("v1C", C_TILES)):
                feed(sp(name) + KT + RING - 1)
                for i, t in enumerate(tiles):
                    wait_tm(act, name, i, KT)
                    act.activation(c_v[:, t, :], ps(2 * i, 0, D), ACT.Copy).then_inc(v_act, 1)
            attention(1)
            feed(sp("out1L") + 7)
            feed(sp(("fi1L", 0)) + RING - 1)
            for i in range(LT):
                post_square("out1L", i, KT)
            for i in range(LT):
                pre_square("ffn1L", i, L_TILES, (post_x, POST["out1L"] + i + 1))
            for i in range(LT):
                pre_high("ffn1L", i, L_TILES)
            ffn_in(("fi1L", 0), FH, SEQ, {4: lambda: gate_rows(3, 1)})
            feed(sp(("fi1L", 1)) + RING - 1)
            ffn_in(("fi1L", 1), FH, SEQ)
            feed(sp(("fo1L", 1)) + FH - 1)
            for i in range(LT):
                post_square("fo1L", i)

        @block.vector
        def _(dve):
            def pre_scale(name, i, tiles):
                n = PRE[name] + i
                dve.wait_ge(pre_rs, n + 1)
                if n >= 2:
                    dve.wait_ge(pre_tr, n - 1)
                dve.tensor_scalar(xs[:, n % 2, :], x_res[:, tiles[i], :], rs_pre[:, n:n + 1], None,
                                  ALU.mult).then_inc(pre_xs, 1)

            def pre_modulate(name, i, tiles, b, j):
                n = PRE[name] + i
                lc = int(tiles[i] >= LT)
                dve.wait_ge(pre_tr, n + 1)
                if n:
                    dve.wait_ge(pre_lo, n)
                n_post = posts_before.get(name, 10 if i < LT else 12)
                if n_post:
                    dve.wait_ge(post_x, n_post)
                dve.wait_ge(mod_der, 2 * j + 1 if j % 2 == 0 else 2 * j + 1)
                dve.wait_ge(mod_done, b + 1)
                for k in range(KT):
                    last = dve.tensor_scalar(full[:, k, :], ps(4 + 2 * (n % 2), k * P, (k + 1) * P),
                                             pre_a[:, j, lc, k:k + 1], mod_col[:, b, lc, k:k + 1], ALU.mult, ALU.add)
                last.then_inc(pre_full, 1)

            def pre_low(name, i, tiles):
                n, t = PRE[name] + i, tiles[i]
                dve.wait_ge(pre_hi, n + 1)
                if name == "mix1" and t < LT:
                    for k in range(KT):
                        last = dve.tensor_tensor(
                            grid_order(h_lo, k, t), full[:, k, :].rearrange("p (r b c) -> p r b c", b=8, c=8),
                            grid_order(h_hi, k, t).bitcast(F32), ALU.subtract)
                else:
                    cols = slice(t * P, (t + 1) * P)
                    last = dve.tensor_tensor(h_lo[:, :, cols], full[:], h_hi[:, :, cols].bitcast(F32), ALU.subtract)
                last.then_inc(pre_lo, 1)

            def pre_rest(name, tiles, b, j, scaled=0):
                for i in range(scaled, min(2, len(tiles))):
                    pre_scale(name, i, tiles)
                for i in range(len(tiles)):
                    pre_modulate(name, i, tiles, b, j)
                    if 2 <= i + 2 < len(tiles):
                        pre_scale(name, i + 2, tiles)
                    pre_low(name, i, tiles)

            def post_norm(name, i, t, k_units=None):
                n, lc = POST[name] + i, int(t >= LT)
                src = ps(2 * i, 0, D) if k_units else y_half[:, i, :]
                dve.wait_ge(post_rs, n + 1)
                dve.wait_ge(gb_done, gb_need[name][lc])
                if n:
                    dve.wait_ge(post_x, n)
                dve.wait_ge(*full_free[name])
                scaled = full[:].rearrange("p k n -> p (k n)")
                dve.scalar_tensor_tensor(scaled, src, rs_post[:, n:n + 1], gate_b[:, lc, :], ALU.mult,
                                         ALU.mult).then_inc(post_n, 1)
                dve.wait_ge(post_n, n + 1)
                dve.tensor_tensor(x_res[:, t, :], x_res[:, t, :], scaled, ALU.add).then_inc(post_x, 1)

            def take_half(name, k_units):
                for i in range(LT):
                    wait_tm(dve, name, i, k_units)
                    dve.tensor_copy(y_half[:, i, :], ps(2 * i, 0, D)).then_inc(half_done, 1)

            def add_half(name, short, k_units):
                for i in range(LT):
                    wait_tm(dve, name, i, k_units)
                    dve.wait_ge(half_done, LT * (1 + (short == "fo1L")))
                    dve.tensor_tensor(y_half[:, i, :], y_half[:, i, :], ps(2 * i, 0, D), ALU.add).then_inc(post_y, 1)

            def modulation_rows(b):
                dve.wait_ge(w_direct, KT * (b + 1))
                if b:
                    dve.wait_ge(mod_turned, b)
                dve.tensor_copy(gate_b[0:2, 0, :], ps(4, 0, D, 0, 2)).then_inc(mod_copied, 1)
                modulation(b, 6)

            acc_done = [0]

            def accumulate(s):
                while acc_done[0] < len(acc_unit) and acc_after[acc_done[0]] <= s + 1:
                    n = acc_done[0]
                    b, k = 2 + n // KT, n % KT
                    acc, w = (xs if b < 6 else mod_acc), acc_slot(n)
                    dve.wait_ge(acc_landed[n % ACC], landed_value[acc_unit[n]])
                    if k == 0 and b > 2:
                        dve.wait_ge(mod_turned, b)
                    elif k == 0:
                        dve.wait_ge(pre_tr, NT)
                    else:
                        dve.wait_ge(w_acc, n)
                    for v in range(2):
                        if k == 0:
                            last = dve.tensor_scalar(acc[:, v, :], w, c_col[:, k, v:v + 1], None, ALU.mult)
                        else:
                            last = dve.scalar_tensor_tensor(acc[:, v, :], w, c_col[:, k, v:v + 1], acc[:, v, :],
                                                            ALU.mult, ALU.add)
                    last.then_inc(w_acc, 1)
                    acc_done[0] += 1

            def modulation(b, bank=7):
                l, i = divmod(b, 6)
                dve.wait_ge(mod_turned, b + 1)
                bias = bias_col[:, b * KT:(b + 1) * KT]
                bias = bass.AP(bias.tensor, bias.offset, [list(bias.ap[0]), [0, 2], [1, KT]])
                dve.tensor_tensor(mod_col[:, b], ps(bank, 0, 2 * KT).rearrange("p (k v) -> p v k", v=2), bias,
                                  ALU.add).then_inc(mod_done, 1)
                if i in (0, 3):
                    return
                which = {1: 0, 2: 0, 4: 1, 5: 1}[i]
                gain = {1: 0, 2: 16, 4: 32, 5: 48}[i] + l * KT
                gain = par_col[:, gain:gain + KT]
                gain = bass.AP(gain.tensor, gain.offset, [list(gain.ap[0]), [0, 2], [1, KT]])
                dve.wait_ge(mod_done, b + 1)
                if i in (1, 4):
                    dve.scalar_tensor_tensor(pre_a[:, 2 * l + which], mod_col[:, b], 1.0, gain, ALU.add,
                                             ALU.mult).then_inc(mod_der, 1)
                else:
                    dve.tensor_tensor(gate_col[:, 2 * l + which], mod_col[:, b], gain, ALU.mult).then_inc(mod_der, 1)

            fed = [0]

            def feed(s):
                while fed[0] <= s:
                    if by_dve[fed[0]]:
                        low_part(dve, fed[0])
                    fed[0] += 1

            def ffn_in(name, n_js, width, hooks=None):
                s, f0 = sp(name), FI[name]
                for j in range(n_js):
                    f = f0 + j
                    dve.wait_ge(w_used, s + 2 * j + 2)
                    dve.wait_ge(ff_silu, f + 1)
                    if f >= 2:
                        dve.wait_ge(ff_lo, f - 1)
                    dve.tensor_tensor(hid_f[:, f % 2, 0:width], silu_g[:, f % 2, 0:width],
                                      ps(2 * (f % 2) + 1, 0, width), ALU.mult).then_inc(ff_full, 1)
                    if by_dve[s]:
                        feed(s + 2 * j + 1 + RING)
                    dve.wait_ge(ff_hi, f + 1)
                    dve.tensor_tensor(hid_lo[:, j * width:(j + 1) * width], hid_f[:, f % 2, 0:width],
                                      hid_hi[:, j * width:(j + 1) * width].bitcast(F32), ALU.subtract)\
                        .then_inc(ff_lo, 1)
                    if hooks and j in hooks:
                        hooks[j]()
                    if by_dve[s]:
                        feed(s + 2 * j + 2 + RING)
                    if name[0] == "fi0L":
                        accumulate(s + 2 * j + 3)

            def attention(layer):
                steps, a0, g0 = STEPS[layer], STEP0[layer], GROUP0[layer]
                prob_t = (prob0_t, prob1_t)[layer]

                def maximum(i, between):
                    a, n = a0 + i, s_cols(layer, i)
                    g, h = g0 + i // 8, steps[i][2]
                    dve.wait_ge(at_s, a + 1)
                    if a >= 2:
                        dve.wait_ge(at_m, a - 1)
                    raw = raw_max[:, a % 2:a % 2 + 1]
                    if layer == 0:
                        dve.tensor_reduce(raw, ps(2 * (i % 2), 0, n), AX, ALU.max).then_inc(at_r, 1)
                    else:
                        t = steps[i][0]
                        near = local_tiles(t)
                        m = len(near) * P
                        dve.tensor_reduce(ctx_max[:, a % 2:a % 2 + 1], ps(2 * (i % 2), m, n), AX, ALU.max)\
                            .then_inc(at_c, 1)
                        dve.wait_ge(at_b, i + 1)
                        dve.wait_ge(at_c, i + 1)
                        dve.tensor_tensor_reduce(ps(2 * (i % 2), 0, m), ps(2 * (i % 2), 0, m), bias_m[:, i % 2, 0:m],
                                                 1.0, ctx_max[:, a % 2:a % 2 + 1], ALU.add, ALU.max,
                                                 raw).then_inc(at_r, 1)
                    between()
                    dve.wait_ge(at_r, a + 1)
                    if layer == 0:
                        dve.tensor_scalar(negm[:, g % 2, h:h + 1], raw_max[:, a % 2:a % 2 + 1], -SCALE,
                                          nsink[:, h:h + 1], ALU.mult, ALU.min).then_inc(at_m, 1)
                    else:
                        dve.tensor_scalar(negm[:, g % 2, h:h + 1], raw_max[:, a % 2:a % 2 + 1], -1.0, None,
                                          ALU.mult).then_inc(at_m, 1)

                def evacuate(i):
                    a, n = a0 + i, s_cols(layer, i)
                    dve.wait_ge(at_t, a + 1)
                    if a >= 2:
                        dve.wait_ge(at_o, a - 1)
                    dve.tensor_copy(prob_t[:, i % 2, 0:n], ps(4, 0, n)).then_inc(at_e, 1)

                def group_end(gi):
                    g = g0 + gi
                    dve.wait_ge(at_o, a0 + 8 * gi + 8)
                    den = rowsum[:, g % 2, :]
                    if layer == 0:
                        dve.wait_ge(at_sink, g + 1)
                        dve.tensor_tensor(sm[:, 2, :], den, sm[:, 1, :], ALU.add).then_inc(at_den, 1)
                        dve.wait_ge(at_den, g + 1)
                        den = sm[:, 2, :]
                    if g:
                        dve.wait_ge(at_on, g)
                    dve.reciprocal(sm[:, 3, :], den).then_inc(at_rinv, 1)
                    dve.wait_ge(at_rinv, g + 1)
                    if g >= 2:
                        dve.wait_ge(at_f, g - 1)
                    dve.tensor_tensor(full[:, 4 * (g % 2):4 * (g % 2) + 4, :].rearrange(
                        "p a n -> p (a n)").rearrange("p (h d) -> p h d", h=8),
                        ps(6 + gi % 2, 0, 512).rearrange("p (h d) -> p h d", h=8), bcast(sm[:, 3, :], 64),
                        ALU.mult).then_inc(at_on, 1)

                def low(gi):
                    t, grp, _ = steps[8 * gi]
                    dve.wait_ge(at_hi, g0 + gi + 1)
                    for f in range(4):
                        dst, order = group_out(layer, t, grp, f)
                        last = dve.tensor_tensor(dst(h_lo), order(ps(6 + gi % 2, f * P, (f + 1) * P)),
                                                 dst(h_hi).bitcast(F32), ALU.subtract)
                    last.then_inc(at_lo, 1)

                def shift(gi):
                    g = g0 + gi
                    dve.wait_ge(at_m, a0 + 8 * gi + 8)
                    if g:
                        dve.wait_ge(at_sink, g)
                    dve.tensor_tensor(sm[:, 0, :], negm[:, g % 2, :], sink[:], ALU.add).then_inc(at_shift, 1)

                n_pairs = len(steps) // 2
                for p in range(n_pairs + 5):
                    earlier = (lambda: evacuate(2 * p - 2)) if 0 < p <= n_pairs else (lambda: None)
                    maximum(2 * p, earlier) if p < n_pairs else earlier()
                    if p < n_pairs:
                        maximum(2 * p + 1, lambda: None)
                    if p % 4 == 3 and p < n_pairs and layer == 0:
                        shift(p // 4)
                    if p % 4 == 2 and p > 4:
                        group_end(p // 4 - 1)
                    if p % 4 == 0 and p > 4:
                        low(p // 4 - 2)
                    if 0 < p <= n_pairs:
                        evacuate(2 * p - 1)

            dve.memset(r_t[32:33, :], 1.0)
            dve.memset(gw[:], 0.0).then_inc(gw_zero, 1)
            dve.wait_ge(consts_in, 16 * 6)
            dve.tensor_copy(ident_b[:], ident[:])
            dve.tensor_copy(window_b[:], mask_in[:, 0:2 * P])
            dve.tensor_copy(near_b[:].rearrange("p t n -> p (t n)"), mask_in[:, 2 * P:]).then_inc(par_done, 1)
            dve.wait_ge(par_in, 16 * 9)
            dve.tensor_scalar(nsink[:], sink[:], -1.0, None, ALU.mult)
            dve.wait_ge(par_turned, 2)
            dve.tensor_copy(bias_col[:], ps(6, 0, 96))
            dve.tensor_copy(par_col[:], ps(7, 0, 84)).then_inc(par_done, 1)
            dve.wait_ge(par_done, 2)
            modulation_rows(0)
            modulation_rows(1)
            pre_rest("mix0", range(NT), 0, 0)
            accumulate(sp("v0") + KT - 1)
            wait_tm(dve, "v0", NT - 1, KT)
            for t in range(NT):
                dve.tensor_copy(a_v[:, t, :], ps(6, t * P, (t + 1) * P)).then_inc(v_dve, 1)
            for i in range(15):
                s = sp("in0") + i
                if i < 6:
                    dst = (a_q[:, i] if i < 4 else a_k[:, i - 4])[:, 0:SEQ]
                    lat = ps(2 * (i % 2), 0, SEQ)
                    dve.wait_ge(w_used, s + 1)
                    if i:
                        dve.wait_ge(rope_done, i)
                    dve.tensor_tensor(rope_t[:, 0], lat, cos[:], ALU.mult)
                    dve.stream_shuffle(rope_t[:, 1], lat, [(q + 16) % 32 for q in range(32)]).then_inc(fe_dve, 1)
                    dve.wait_ge(fe_dve, i + 1)
                    dve.tensor_tensor(rope_t[:, 1], rope_t[:, 1], sin[:], ALU.mult).then_inc(rope_m, 1)
                    dve.wait_ge(rope_m, i + 1)
                    dve.tensor_tensor(dst, rope_t[:, 0], rope_t[:, 1], ALU.add).then_inc(rope_done, 1)
                elif 10 <= i < 14:
                    dve.wait_ge(fe_act, i + 1)
                    dve.tensor_scalar(b_o[:, i - 10], b_o[:, i - 10], par_col[:, 64 + i - 10:65 + i - 10], None,
                                      ALU.mult).then_inc(bo_done, 1)
                if i in (0, 6, 10):
                    modulation({0: 2, 6: 3, 10: 4}[i])
                accumulate(s + 1)
            attention(0)
            modulation(5)

            for t in range(NT):
                dve.wait_ge(gl_ln, t + 1)
                dve.scalar_tensor_tensor(la[:, t, :], ps(t, 0, 512), 0.0, la[:, t, :], ALU.min,
                                         ALU.subtract).then_inc(gl_la, 1)
            for t in range(NT):
                cols = slice(t * P, (t + 1) * P)
                dve.wait_ge(gl_eq, t + 1)
                dve.tensor_copy(decay[:, 0:2, 2 * t:2 * t + 2], qg[:, 0:2, t * P + CH - 1:(t + 1) * P:CH])
                dve.tensor_copy(decay[:, 2:4, 2 * t:2 * t + 2], qg[:, 2:4, t * P:(t + 1) * P:CH]).then_inc(gl_dec, 1)
                dve.wait_ge(gl_dec, t + 1)
                for d in range(2):
                    last = dve.tensor_tensor(qg[:, 2 * d:2 * d + 2, cols], qg[:, 2 * d:2 * d + 2, cols],
                                             b_q[:, :, cols], ALU.mult)
                last.then_inc(gl_q, 1)
                dve.wait_ge(gl_ek, t + 1)
                for d in range(2):
                    last = dve.tensor_tensor(kg[:, 2 * d:2 * d + 2, cols], kg[:, 2 * d:2 * d + 2, cols],
                                             b_k[:, :, cols], ALU.mult)
                last.then_inc(gl_k, 1)
            for t in range(NT):
                dve.wait_ge(gl_kt, t + 1)
                if t == 0:
                    dve.wait_ge(gl_cum, NT)
                dve.tensor_copy(kg_t[:, t, :], ps(t % 2, 0, 512)).then_inc(gl_ktc, 1)
            dve.wait_ge(gl_dec, NT)
            for i in range(2 * NT - 1):
                dve.wait_ge(gl_ds, i + 1)
                if i:
                    dve.wait_ge(gl_s, 2 * i)
                for d in range(2):
                    m = slice(2 * d, 2 * d + 2)
                    ds = ps(2 + 2 * d + i % 2, 0, 256).rearrange("p (m n) -> p m n", m=2)
                    if i == 0:
                        last = dve.tensor_copy(state[:, 0, m], ds)
                    else:
                        last = dve.tensor_tensor(state[:, i, m], state[:, i - 1, m], ds, ALU.add)
                last.then_inc(gl_u, 1)
                dve.wait_ge(gl_u, i + 1)
                for d, chunk in enumerate((f_order[i], b_order[i])):
                    dve.tensor_tensor(state[:, i, 2 * d:2 * d + 2], state[:, i, 2 * d:2 * d + 2],
                                      bcast(decay[:, 2 * d:2 * d + 2, chunk], P), ALU.mult).then_inc(gl_s, 1)
            fg = b_q[:].rearrange("p a n -> p (a n)")[:, 0:512]
            on = b_k[:].rearrange("p a n -> p (a n)")[:, 0:512]

            def gla_mask(t):
                dve.wait_ge(gl_att, t + 1)
                if t:
                    dve.wait_ge(gl_o, t)
                for d in range(2):
                    m = tri[:, d]
                    m = bass.AP(m.tensor, m.offset, [list(m.ap[0]), [0, 2], [1, P]])
                    for b in range(2):
                        last = dve.tensor_tensor(
                            att_m[:, d].rearrange("p (a b n) -> p b a n", a=2, b=2)[:, b],
                            ps(2 * d + b, 0, 256).rearrange("p (h n) -> p h n", h=2), m, ALU.mult)
                last.then_inc(gl_msk, 1)

            gla_mask(0)
            for t in range(NT):
                dve.wait_ge(gl_rs, t + 1)
                if t:
                    dve.wait_ge(gl_f, t)
                for b in range(2):
                    last = dve.tensor_tensor(on.rearrange("p (a b n) -> p b a n", a=2, b=2)[:, b],
                                             ps(4 + b, 0, 256).rearrange("p (h n) -> p h n", h=2),
                                             bcast(gla_rs[:, t, b:4:2], P), ALU.mult)
                last.then_inc(gl_on, 1)
                if t + 1 < NT:
                    gla_mask(t + 1)
                dve.wait_ge(gl_f, t + 1)
                cols = slice(t * P, (t + 1) * P)
                if t:
                    dve.wait_ge(gl_lo, t)
                dve.tensor_tensor(fg.rearrange("p (h n) -> p h n", h=4),
                                  ps(6 + t % 2, 0, 512).rearrange("p (h n) -> p h n", h=4), b_o[:, :, cols],
                                  ALU.mult).then_inc(gl_full, 1)
                dve.wait_ge(gl_hi, t + 1)
                dve.tensor_tensor(h_lo[:, 4:8, cols], fg.rearrange("p (h n) -> p h n", h=4),
                                  h_hi[:, 4:8, cols].bitcast(F32), ALU.subtract).then_inc(gl_lo, 1)

            for i in range(LT):
                post_norm("out0L", i, i, KT)
            pre_scale("ffn0L", 0, L_TILES)
            pre_scale("ffn0L", 1, L_TILES)
            for i in range(CT):
                post_norm("out0C", i, LT + i, KT)
            pre_rest("ffn0L", L_TILES, 3, 1, scaled=2)
            for i in range(CT):
                pre_scale("ffn0C", i, C_TILES)
            ffn_in(("fi0L", 0), FH, SEQ, {0: lambda: pre_rest("ffn0C", C_TILES, 3, 1, scaled=2),
                                          5: lambda: modulation(6), 9: lambda: modulation(7)})
            accumulate(sp(("fo0L", 0)) + FH - 1)
            take_half(("fo0L", 0), FH)
            ffn_in(("fi0L", 1), FH, SEQ, {0: lambda: modulation(8), 5: lambda: modulation(9),
                                          9: lambda: modulation(10)})
            accumulate(sp(("fo0L", 1)) + FH - 1)
            feed(sp("fi0C") + RING - 1)
            add_half(("fo0L", 1), "fo0L", FH)
            feed(sp("fi0C") + RING)
            mix1 = range(NT)
            hooks = {j: (lambda i=j: post_norm("fo0L", i, i)) for j in range(LT)}
            hooks[0] = lambda: (modulation(11), post_norm("fo0L", 0, 0))
            hooks |= {4: lambda: pre_scale("mix1", 0, mix1), 5: lambda: pre_scale("mix1", 1, mix1)}
            for i in range(LT):
                hooks[6 + 2 * i] = lambda i=i: pre_modulate("mix1", i, mix1, 6, 2)
                hooks[7 + 2 * i] = lambda i=i: (pre_scale("mix1", i + 2, mix1) if i + 2 < LT else None,
                                                pre_low("mix1", i, mix1))
            ffn_in("fi0C", FT, CTX, hooks)
            feed(sp("fo0C") + FT - 1)
            for i in range(CT):
                post_norm("fo0C", i, LT + i, FT)
            for i in range(LT, NT):
                pre_scale("mix1", i, mix1)
            for i in range(LT, NT):
                pre_modulate("mix1", i, mix1, 6, 2)
                pre_low("mix1", i, mix1)
            feed(sp("v1C") + KT - 1)
            attention(1)
            for i in range(LT):
                post_norm("out1L", i, i, KT)
            pre_rest("ffn1L", L_TILES, 9, 3)
            ffn_in(("fi1L", 0), FH, SEQ)
            take_half(("fo1L", 0), FH)
            ffn_in(("fi1L", 1), FH, SEQ)
            add_half(("fo1L", 1), "fo1L", FH)
            for i in range(LT):
                post_norm("fo1L", i, i)

        @block.tensor
        def _(pe):
            readers = {}

            def claim(*banks):
                for b in banks:
                    for s, v in readers.pop(b, ()):
                        pe.wait_ge(s, v)

            def read_by(banks, *who):
                for b in banks:
                    readers[b] = who

            def split_ready(s):
                pe.wait_ge(*low_ready(s))

            def product3(s, sta, mov, outs, first, last, done=None):
                order = [("hi", "hi"), ("hi", "lo"), ("lo", "hi")]
                for n, (x, y) in enumerate(order):
                    for o in outs:
                        mm = pe.matmul(o[0], sta(x, o), mov(y, o), start=first and n == 0, stop=last and n == 2)
                return mm

            def fm_unit(s, outs):
                split_ready(s)
                w = {"hi": w_hi[:, s % RING], "lo": w_lo[:, s % RING]}
                h = {"hi": h_hi, "lo": h_lo}
                for k in range(KT):
                    mm = product3(s, lambda x, o: w[x][:, k * P:(k + 1) * P],
                                  lambda y, o: h[y][:, k, o[1]:o[1] + o[2]], outs, k == 0, k == KT - 1)
                mm.then_inc(w_used, 1)

            def tm_product(name, n_units, act, tiles, where, ready=None):
                s0 = sp(name)
                for k in range(n_units):
                    s = s0 + k
                    if ready:
                        ready(k)
                    split_ready(s)
                    w = {"hi": w_hi[:, s % RING], "lo": w_lo[:, s % RING]}
                    for i, t in enumerate(tiles):
                        for x, y in (("hi", "hi"), ("hi", "lo"), ("lo", "hi")):
                            for o, c, n in where(i):
                                mm = pe.matmul(o, act(x, k, t), w[y][:, c:c + n],
                                               start=k == 0 and (x, y) == ("hi", "hi") and first_in_bank(name, i, c),
                                               stop=k == n_units - 1 and x == "lo", skip_group_check=True)
                        if k == n_units - 1 and i < len(tiles) - 1:
                            mm.then_inc(tm_done, 1)
                    mm.then_inc(w_used, 1)

            def first_in_bank(name, i, c):
                return not (name == "v0" and c == 0 and i not in (0, 4))

            def h_act(x, k, t):
                return (h_hi if x == "hi" else h_lo)[:, k, t * P:(t + 1) * P]

            def two_halves(i):
                return [(ps(2 * i + n, 0, 512), 512 * n, 512) for n in range(2)]

            def modulation_rows(b):
                claim(4, 5)
                u0 = start[("mod", b)]
                for k in range(KT):
                    pe.wait_ge(landed[ring_no[u0 + k] % RAW], landed_value[u0 + k])
                    for n in range(2):
                        mm = pe.matmul(ps(4 + n, 0, 512, 0, 2), c_col[:, k, :],
                                       w_raw[:, ring_no[u0 + k] % RAW, n * 512:(n + 1) * 512], start=k == 0, stop=k == KT - 1)
                    mm.then_inc(w_direct, 1)
                read_by((4, 5), (mod_copied, b + 1))
                claim(6)
                pe.wait_ge(mod_copied, b + 1)
                for k in range(KT):
                    mm = pe.transpose(ps(6, 2 * k, 2 * k + 2), gate_b[0:2, 0, k * P:(k + 1) * P], ident[0:2, 0:2])
                mm.then_inc(mod_turned, 1)
                read_by((6,), (mod_done, b + 1))

            def modulation(b):
                acc = xs if b < 6 else mod_acc
                claim(7)
                pe.wait_ge(w_acc, KT * (b - 1))
                for k in range(KT):
                    for v in range(2):
                        mm = pe.matmul(ps(7, 2 * k + v, 2 * k + v + 1), acc[:, v, k * P:(k + 1) * P], one_col[:],
                                       start=True, stop=True)
                mm.then_inc(mod_turned, 1)
                read_by((7,), (mod_done, b + 1))

            def pre_turn(name, tiles):
                for i in tiles:
                    n = PRE[name] + i
                    b = 4 + 2 * (n % 2)
                    claim(b, b + 1)
                    pe.wait_ge(pre_xs, n + 1)
                    for k in range(KT):
                        mm = pe.transpose(ps(b, k * P, (k + 1) * P), xs[:, n % 2, k * P:(k + 1) * P], ident[:])
                    mm.then_inc(pre_tr, 1)
                    read_by((b, b + 1), (pre_full, n + 1))

            def gate_rows(j, n_lc):
                pe.wait_ge(mod_der, 2 * j + 2)
                for lc in range(n_lc):
                    claim(4 + 2 * lc, 5 + 2 * lc)
                    for k in range(KT):
                        col = gate_col[:, j, lc, k:k + 1]
                        mm = pe.matmul(ps(4 + 2 * lc, k * P, (k + 1) * P),
                                       bass.AP(col.tensor, col.offset, [list(col.ap[0]), [0, P]]), ident[:],
                                       start=True, stop=True)
                    mm.then_inc(gb_ready, 1)
                    read_by((4 + 2 * lc, 5 + 2 * lc), (gb_done, gb_base[j] + lc + 1))

            def ffn_in(name, n_js, col0, width, hooks=None):
                s, f0 = sp(name), FI[name]
                for j in range(n_js):
                    f = f0 + j
                    for up in range(2):
                        bank = 2 * (f % 2) + up
                        claim(bank)
                        fm_unit(s + 2 * j + up, [(ps(bank, 0, width), col0, width)])
                        read_by((bank,), (ff_full, f + 1) if up else (ff_silu, f + 1))
                    if hooks and j in hooks:
                        hooks[j]()

            def ffn_out(name, fi, n_units, tiles, width, base):
                f0 = FI[fi]
                hid = {"hi": hid_hi, "lo": hid_lo}
                tm_product(name, n_units,
                           lambda x, k, t: hid[x][:, k * width + (t - base) * P:k * width + (t - base + 1) * P],
                           tiles, two_halves, ready=lambda k: pe.wait_ge(ff_lo, f0 + k + 1))

            def attention(layer):
                steps, a0, g0 = STEPS[layer], STEP0[layer], GROUP0[layer]
                prob, prob_t = ((prob0, prob0_t), (prob1, prob1_t))[layer]

                def scores(pair, between):
                    todo = []
                    claim(0, 1, 2, 3)
                    for i in (2 * pair, 2 * pair + 1):
                        t, grp, h = steps[i]
                        sb_ = 2 * (i % 2)
                        head = 8 * grp + h
                        rows = slice(64 * (h % 2), 64 * (h % 2) + 64)
                        if layer == 0:
                            q, kk = a_q[rows, h // 2, t * P:(t + 1) * P], a_k[rows, h // 4]
                        else:
                            q, kk = c_q[rows, head // 2, t * P:(t + 1) * P], c_k[rows, head // 2]
                        near, n, parts = local_tiles(t), 0, []
                        if near:
                            n = len(near) * P
                            parts.append((ps(sb_, 0, n), q, kk[:, near[0] * P:near[0] * P + n], True))
                        left, at = CTX, 0
                        while left:
                            m = min(left, 512 - n % 512)
                            parts.append((ps(sb_, n, n + m), q, kk[:, SEQ + at:SEQ + at + m], n % 512 == 0))
                            n, at, left = n + m, at + m, left - m
                        todo.append(parts)
                        read_by((sb_, sb_ + 1), (at_p, a0 + i + 1))
                    for n, both in enumerate(zip(*todo)):
                        for o, q, kk, first in both:
                            mm = pe.matmul(o, q, kk, start=first, stop=layer == 1 or not near,
                                           skip_group_check=True)
                            if (layer == 1 or not near) and n == len(todo[0]) - 1:
                                mm.then_inc(at_s, 1)
                    for i in (2 * pair, 2 * pair + 1):
                        t, _, h = steps[i]
                        sb_ = 2 * (i % 2)
                        n = len(near) * P
                        if near and layer == 0:
                            for at, u in enumerate(near):
                                if u != t:
                                    side = int(u > t)
                                    mm = pe.matmul(ps(sb_, at * P, (at + 1) * P), ident_b[:],
                                                   window_b[:, side * P:(side + 1) * P], start=False, stop=True,
                                                   skip_group_check=True)
                            mm.then_inc(at_s, 1)
                        if i % 2 == 0:
                            between()

                def turn(i):
                    a = a0 + i
                    pe.wait_ge(at_p, a + 1)
                    claim(4, 5)
                    for j in range(s_cols(layer, i) // P):
                        mm = pe.transpose(ps(4, j * P, (j + 1) * P), prob[:, i % 2, j * P:(j + 1) * P], ident[:])
                    mm.then_inc(at_t, 1)
                    read_by((4, 5), (at_e, a + 1))

                def values(i):
                    t, grp, h = steps[i]
                    bank = 6 + i // 8 % 2
                    if h == 0:
                        claim(bank)
                    pe.wait_ge(at_e, a0 + i + 1)
                    keys = local_tiles(t) + C_TILES
                    for j, u in enumerate(keys):
                        v = a_v[:, u, 64 * (h // 4):64 * (h // 4) + 64] if layer == 0 else \
                            c_v[:, u, (8 * grp + h) * 64:(8 * grp + h + 1) * 64]
                        mm = pe.matmul(ps(bank, h * 64, h * 64 + 64), prob_t[:, i % 2, j * P:(j + 1) * P], v,
                                       start=h == 0 and j == 0, stop=j == len(keys) - 1, skip_group_check=True)
                    mm.then_inc(at_o, 1)
                    if h == 7:
                        read_by((bank,), (at_on, g0 + i // 8 + 1))

                def turn_group(gi):
                    g = g0 + gi
                    bank = 6 + gi % 2
                    pe.wait_ge(at_on, g + 1)
                    claim(bank)
                    for f in range(4):
                        mm = pe.transpose(ps(bank, f * P, (f + 1) * P), full[:, 4 * (g % 2) + f, :], ident[:])
                    mm.then_inc(at_f, 1)
                    read_by((bank,), (at_lo, g + 1))

                n_pairs = len(steps) // 2
                for p in range(n_pairs + 4):
                    earlier = (lambda: turn(2 * p - 2)) if 0 < p <= n_pairs else (lambda: None)
                    scores(p, earlier) if p < n_pairs else earlier()
                    if 1 < p <= n_pairs + 1:
                        values(2 * p - 3)
                    if p % 4 == 3 and p > 4:
                        turn_group(p // 4 - 1)
                    if 0 < p <= n_pairs:
                        turn(2 * p - 1)
                        values(2 * p - 2)

            pe.wait_ge(par_in, 16 * 9)
            pe.wait_ge(consts_in, 16 * 6)
            pe.transpose(ps(6, 0, 96), par_rows[0:96, 0, :], ident[0:96, 0:96]).then_inc(par_turned, 1)
            pe.transpose(ps(7, 0, 84), par_rows[0:84, 1, :], ident[0:84, 0:84]).then_inc(par_turned, 1)
            read_by((6, 7), (par_done, 2))
            pe.wait_ge(c_done, 1)
            modulation_rows(0)
            modulation_rows(1)
            pre_turn("mix0", range(NT))
            pe.wait_ge(pre_lo, NT)
            claim(*range(8))
            tm_product("v0", KT, h_act, range(NT),
                       lambda i: [(ps(6, i * P, (i + 1) * P), 0, AKV), (ps(i, 0, BV), AKV, BV)])
            for t in range(NT):
                read_by((t,), (v_act, t + 1))
            read_by((6, 7), (v_dve, NT))
            for i in range(15):
                bl = 2 * (i % 2)
                claim(bl, bl + 1)
                fm_unit(sp("in0") + i, [(ps(bl, 0, SEQ), 0, SEQ), (ps(bl + 1, 0, CTX), SEQ, CTX)])
                read_by((bl, bl + 1), (fe_act, i + 1), *([(fe_dve, i + 1)] if i < 6 else []))
                if i in (0, 6, 10):
                    modulation({0: 2, 6: 3, 10: 4}[i])
            pe.wait_ge(rope_done, 6)
            pe.wait_ge(fe_act, 15)
            claim(*range(8))
            attention(0)
            modulation(5)

            pe.wait_ge(gw_in, 64)
            claim(*range(8))
            for t in range(NT):
                pe.matmul(ps(t, 0, 512), r_t[:, t * P:(t + 1) * P], gw[:], start=True, stop=True).then_inc(gl_z, 1)
                read_by((t,), (gl_la, t + 1))
            for t in range(NT):
                claim(6 + t % 2)
                pe.wait_ge(gl_la, t + 1)
                for m in range(4):
                    mm = pe.matmul(ps(6 + t % 2, m * P, (m + 1) * P), la[:, t, m * P:(m + 1) * P], tri[:, m // 2],
                                   start=True, stop=True)
                mm.then_inc(gl_cum, 1)
                read_by((6 + t % 2,), (gl_ek, t + 1))
            for t in range(NT):
                claim(t % 2)
                pe.wait_ge(gl_k, t + 1)
                for m in range(4):
                    mm = pe.transpose(ps(t % 2, m * P, (m + 1) * P), kg[:, m, t * P:(t + 1) * P], ident[:])
                mm.then_inc(gl_kt, 1)
                read_by((t % 2,), (gl_ktc, t + 1))
            pe.wait_ge(gl_ktc, NT)
            for i in range(2 * NT - 1):
                claim(2 + i % 2, 4 + i % 2)
                for m in range(4):
                    bank = 2 + 2 * (m // 2) + i % 2
                    chunk = (f_order, b_order)[m // 2][i]
                    t, rows = chunk // 2, slice(64 * (chunk % 2), 64 * (chunk % 2) + 64)
                    for hh in range(2):
                        head = 2 * (m % 2) + hh
                        mm = pe.matmul(ps(bank, (m % 2) * P, (m % 2 + 1) * P, 64 * hh, 64 * hh + 64),
                                       kg_t[rows, t, m * P + 64 * hh:m * P + 64 * hh + 64],
                                       b_v[rows, t, head * P:(head + 1) * P], start=True, stop=True)
                mm.then_inc(gl_ds, 1)
                read_by((2 + i % 2, 4 + i % 2), (gl_u, i + 1))
            pe.wait_ge(gl_q, NT)

            def gla_scores(t):
                claim(0, 1, 2, 3)
                cols = slice(t * P, (t + 1) * P)
                for d in range(2):
                    for h in range(4):
                        m, rows = 2 * d + h // 2, slice(64 * (h % 2), 64 * (h % 2) + 64)
                        mm = pe.matmul(ps(2 * d + h % 2, (h // 2) * P, (h // 2 + 1) * P), kg[rows, m, cols],
                                       qg[rows, m, cols], start=True, stop=True)
                mm.then_inc(gl_att, 1)
                read_by((0, 1, 2, 3), (gl_msk, t + 1))

            def gla_turn(t):
                bank = 6 + t % 2
                claim(bank)
                pe.wait_ge(gl_on, t + 1)
                on = b_k[:].rearrange("p a n -> p (a n)")
                for h in range(4):
                    mm = pe.transpose(ps(bank, h * P, (h + 1) * P), on[:, h * P:(h + 1) * P], ident[:])
                mm.then_inc(gl_f, 1)
                read_by((bank,), (gl_full, t + 1))

            gla_scores(0)
            pe.wait_ge(gl_s, 2 * (2 * NT - 1))
            for t in range(NT):
                claim(4, 5)
                pe.wait_ge(gl_msk, t + 1)
                for d in range(2):
                    for h in range(4):
                        pe.matmul(ps(4 + h % 2, (h // 2) * P, (h // 2 + 1) * P), att_m[:, d, h * P:(h + 1) * P],
                                  b_v[:, t, h * P:(h + 1) * P], start=d == 0 and h < 2, stop=False,
                                  skip_group_check=True)
                for d in range(2):
                    for half in range(2):
                        chunk = 2 * t + half
                        i = (f_order, b_order)[d].index(chunk)
                        for h in range(4) if i else ():
                            m, rows = 2 * d + h // 2, slice(64 * (h % 2), 64 * (h % 2) + 64)
                            mm = pe.matmul(ps(4 + h % 2, (h // 2) * P, (h // 2 + 1) * P, 64 * half, 64 * half + 64),
                                           qg[rows, m, chunk * CH:(chunk + 1) * CH], state[rows, i - 1, m, :],
                                           start=False, stop=d == 1, skip_group_check=True)
                mm.then_inc(gl_o, 1)
                read_by((4, 5), (gl_on, t + 1))
                if t + 1 < NT:
                    gla_scores(t + 1)
                gla_turn(t)

            gate_rows(0, 2)
            claim(*range(8))
            pe.wait_ge(gl_lo, NT)
            pe.wait_ge(at_lo, NT)
            tm_product("out0L", KT, h_act, L_TILES, two_halves)
            for i in range(LT):
                read_by((2 * i, 2 * i + 1), (post_n, POST["out0L"] + i + 1))
            claim(0, 1, 2, 3)
            tm_product("out0C", KT, h_act, C_TILES, two_halves)
            for i in range(CT):
                read_by((2 * i, 2 * i + 1), (post_n, POST["out0C"] + i + 1))
            pre_turn("ffn0L", range(LT))
            pe.wait_ge(pre_lo, PRE["ffn0L"] + LT)
            ffn_in(("fi0L", 0), FH, 0, SEQ, {0: lambda: pre_turn("ffn0C", range(CT)), 4: lambda: gate_rows(1, 2),
                    5: lambda: modulation(6), 9: lambda: modulation(7)})
            claim(*range(8))
            ffn_out(("fo0L", 0), ("fi0L", 0), FH, L_TILES, SEQ, 0)
            for i in range(LT):
                read_by((2 * i, 2 * i + 1), (half_done, i + 1))
            ffn_in(("fi0L", 1), FH, 0, SEQ, {0: lambda: modulation(8), 5: lambda: modulation(9),
                                             9: lambda: modulation(10)})
            claim(*range(8))
            ffn_out(("fo0L", 1), ("fi0L", 1), FH, L_TILES, SEQ, 0)
            for i in range(LT):
                read_by((2 * i, 2 * i + 1), (post_y, i + 1))
            hooks = {0: lambda: modulation(11)}
            hooks |= {5 + 2 * i: (lambda i=i: pre_turn("mix1", [i])) for i in range(LT)}
            ffn_in("fi0C", FT, SEQ, CTX, hooks)
            claim(0, 1, 2, 3)
            ffn_out("fo0C", "fi0C", FT, C_TILES, CTX, LT)
            for i in range(CT):
                read_by((2 * i, 2 * i + 1), (post_n, POST["fo0C"] + i + 1))

            pe.wait_ge(pre_lo, PRE["mix1"] + LT)
            for i in range(16):
                bank = qk_bank(i)
                if i < KT:
                    claim(bank)
                    outs = [(ps(bank, 0, SEQ), 0, SEQ)]
                else:
                    claim(bank, bank + 1)
                    pe.wait_ge(pre_lo, PRE["mix1"] + NT)
                    outs = [(ps(bank, 0, SEQ), 0, SEQ), (ps(bank + 1, 0, CTX), SEQ, CTX)]
                fm_unit(sp("qk1") + i, outs)
                read_by((bank,) if i < KT else (bank, bank + 1), (fe1_act, i + 1))
                if i == 3:
                    pre_turn("mix1", C_TILES)
            gate_rows(2, 1)
            claim(*range(8))
            tm_product("v1L", KT, h_act, L_TILES, two_halves)
            for i in range(LT):
                read_by((2 * i, 2 * i + 1), (v_act, NT + i + 1))
            claim(0, 1, 2, 3)
            tm_product("v1C", KT, h_act, C_TILES, two_halves)
            for i in range(CT):
                read_by((2 * i, 2 * i + 1), (v_act, NT + LT + i + 1))
            pe.wait_ge(fe1_act, 16)
            claim(*range(8))
            attention(1)
            claim(*range(8))
            pe.wait_ge(at_lo, n_groups[0] + n_groups[1])
            tm_product("out1L", KT, h_act, L_TILES, two_halves)
            for i in range(LT):
                read_by((2 * i, 2 * i + 1), (post_n, POST["out1L"] + i + 1))
            pre_turn("ffn1L", range(LT))
            pe.wait_ge(pre_lo, PRE["ffn1L"] + LT)
            ffn_in(("fi1L", 0), FH, 0, SEQ, {4: lambda: gate_rows(3, 1)})
            claim(*range(8))
            ffn_out(("fo1L", 0), ("fi1L", 0), FH, L_TILES, SEQ, 0)
            for i in range(LT):
                read_by((2 * i, 2 * i + 1), (half_done, LT + i + 1))
            ffn_in(("fi1L", 1), FH, 0, SEQ)
            claim(*range(8))
            ffn_out(("fo1L", 1), ("fi1L", 1), FH, L_TILES, SEQ, 0)


INPUTS = ["x", "c", "ctx", "c_ctx", "w_mod", "b_mod", "g_mix_pre", "g_mix_post", "g_ffn_pre", "g_ffn_post", "w_ffn_in",
          "w_ffn_out", "ab_w_in", "ab_w_out", "a_sink", "gla_gate_f_w", "gla_gate_f_b", "gla_gate_b_w",
          "gla_gate_b_b", "gla_norm_g", "na_w_in", "na_w_out"]


def kernel(**inputs):
    import concourse.bacc as bacc
    from concourse.bass_utils import run_bass_kernel_spmd

    nc = bacc.Bacc("TRN2", target_bir_lowering=False, num_devices=1, dynamic_dma_scratch_size=1024)
    arrays = {name: np.ascontiguousarray(inputs[name]) for name in INPUTS}
    arrays["rel_rev"] = np.ascontiguousarray(np.pad(np.asarray(inputs["na_rel_bias"]).reshape(-1), BIAS_PAD)[::-1])
    arrays |= constants()
    handles = {name: nc.dram_tensor(f"in_{name}", v.shape, mybir.dt.from_np(v.dtype), kind="ExternalInput").ap()
               for name, v in arrays.items()}
    out = nc.dram_tensor("out_y", (1, SEQ, D), F32, kind="ExternalOutput").ap()
    build(nc, handles, out)
    r = run_bass_kernel_spmd(nc, [{f"in_{name}": v for name, v in arrays.items()}], core_ids=[0])
    return r.results[0]["out_y"]
```

```python
from contextlib import ExitStack

import numpy as np

import concourse.bass as bass
from concourse import mybir

F32, F32R, BF16 = mybir.dt.float32, mybir.dt.float32r, mybir.dt.bfloat16
ALU, ACT = mybir.AluOpType, mybir.ActivationFunctionType
AX = mybir.AxisListType.X

P = 128
D = 1024
KT = D // P
SEQ, CTX = 512, 256
LT, CT = SEQ // P, CTX // P
NT = LT + CT
TOK = SEQ + CTX
DFF = 2816
FT = DFF // P
FH = FT // 2
AQ, AKV, BQK, BV, RANK = 512, 128, 256, 512, 16
C_AQ, C_AK, C_AV = 0, AQ, AQ + AKV
C_BQ = C_AV + AKV
C_BK = C_BQ + BQK
C_BV = C_BK + BQK
C_BO = C_BV + BV
AB_IN = C_BO + BV + 2 * RANK
CH = 64
GRID = 64
EPS = 1e-6
NEG = -1e30
SCALE = 0.125
RAW, RING, ACC = 3, 3, 2
BIAS_ROW = 31
BIAS_HEAD = 15 * BIAS_ROW
BIAS_PAD = 16
BIAS_RUN = 7 * BIAS_ROW + 48
L_TILES, C_TILES = list(range(LT)), list(range(LT, NT))
UNIT = 1024


def constants():
    nf = 16
    inv = (10000.0 ** (-np.arange(nf, dtype=np.float32) / nf)).astype(np.float32)
    t = np.arange(SEQ)
    ang = [(t // GRID).astype(np.float32)[None] * inv[:, None], (t % GRID).astype(np.float32)[None] * inv[:, None]]
    cos, sin = np.zeros((P, SEQ), np.float32), np.zeros((P, SEQ), np.float32)
    for p in range(P):
        a = ang[(p % 64) // 32][p % 16]
        cos[p] = np.cos(a)
        sin[p] = np.sin(a) * (-1.0 if p % 32 < 16 else 1.0)
    q, k = np.arange(P)[:, None], np.arange(P)[None]
    window = np.concatenate([np.where(k >= q, 0.0, NEG), np.where(k <= q, 0.0, NEG)], 1).astype(np.float32)
    col = lambda i: 8 * (i // 64) + i % 8
    near = np.full((P, LT, 3 * P), NEG, np.float32)
    for tile in range(LT):
        qc = 16 * tile + col(np.arange(P))
        cs = np.clip(qc - 8, 0, GRID - 16)[:, None]
        for d in range(3):
            kc = (16 * (tile + d - 1) + col(np.arange(P)))[None]
            near[:, tile, d * P:(d + 1) * P] = np.where((kc >= cs) & (kc < cs + 16), 0.0, NEG)
    same = (q // CH) == (k // CH)
    tri = np.stack([same & (q <= k), same & (q >= k)], 1).astype(np.float32)
    return {"k_ident": np.eye(P, dtype=np.float32), "k_cos": cos, "k_sin": sin, "k_window": window,
            "k_near": near.reshape(P, LT * 3 * P), "k_tri": tri.reshape(P, 2 * P)}


def weight_units(a):
    units = []
    start = {}
    w_mod = [(block, k) for block in range(1, 12) for k in range(KT)]

    def begin(name):
        start[name] = len(units)

    def modulations(n):
        for block, k in w_mod[:n]:
            l, i = divmod(block, 6)
            units.append(("acc", [("tm", 0, D, a["w_mod"][l, k * P:(k + 1) * P, i * D:(i + 1) * D])]))
        del w_mod[:n]

    def fm(w, parts):
        src = w.rearrange("(k p) n -> p k n", p=P)
        units.append(("split", [("fm", at, width, src[:, :, c:c + width]) for at, c, width in parts]))

    def tm(w, k, parts):
        units.append(("split", [("tm", at, width, w[k * P:(k + 1) * P, c:c + width]) for at, c, width in parts]))

    def ffn_in(name, l, js, n_mod=0):
        begin(name)
        for n, j in enumerate(js):
            fm(a["w_ffn_in"][l], [(0, j * P, P)])
            modulations(n_mod if n > 1 else 0)
            fm(a["w_ffn_in"][l], [(0, DFF + j * P, P)])
            modulations(n_mod if n else 0)

    def rows(name, w, ks, n_mod=0):
        begin(name)
        for n, k in enumerate(ks):
            tm(w, k, [(0, 0, D)])
            modulations(int(n < n_mod))

    for k in range(KT):
        units.append(("direct", [("tm", 0, D, a["w_mod"][0, k * P:(k + 1) * P, 0:D])]))
        modulations(1)
    w = a["ab_w_in"][0]
    begin("v0")
    for k in range(KT):
        tm(w, k, [(0, C_AV, AKV), (AKV, C_BV, BV)])
        modulations(int(k >= 2) + int(k >= 6))
    begin("in0")
    parts = [[(0, C_AQ + j * P, P)] for j in range(4)]
    parts += [[(0, C_AK + 64 * j, 64), (64, C_AK + 64 * j, 64)] for j in range(2)]
    parts += [[(0, c + j * P, P)] for c, n in ((C_BQ, 2), (C_BK, 2), (C_BO, 4)) for j in range(n)]
    parts += [[(0, AB_IN - P, P)]]
    for i, part in enumerate(parts):
        fm(w, part)
        modulations(1 if i < 6 else 2)
    rows("out0L", a["ab_w_out"][0], range(KT))
    rows("out0C", a["ab_w_out"][0], range(KT))
    for half in range(2):
        ffn_in(("fi0L", half), 0, range(FH * half, FH * half + FH), 1)
        rows(("fo0L", half), a["w_ffn_out"][0], range(FH * half, FH * half + FH), 5)
    ffn_in("fi0C", 0, range(FT))
    rows("fo0C", a["w_ffn_out"][0], range(FT))
    w = a["na_w_in"][0]
    begin("qk1")
    for j in range(16):
        fm(w, [(0, j * P, P)])
    begin("v1L")
    for k in range(KT):
        tm(w, k, [(0, 2 * D, D)])
    begin("v1C")
    for k in range(KT):
        tm(w, k, [(0, 2 * D, D)])
    rows("out1L", a["na_w_out"][0], range(KT))
    for half in range(2):
        ffn_in(("fi1L", half), 1, range(FH * half, FH * half + FH))
        rows(("fo1L", half), a["w_ffn_out"][1], range(FH * half, FH * half + FH))
    return units, start


def attention_steps(layer):
    if layer == 0:
        return [(t, 0, h) for t in range(NT) for h in range(8)]
    return [(t, g, h) for g in range(2) for t in range(LT) for h in range(8)]


def local_tiles(t):
    return [u for u in (t - 1, t, t + 1) if 0 <= u < LT] if t < LT else []


def build(nc, a, out):
    units, start = weight_units(a)
    kind_no, n_kind = [], {"split": 0, "direct": 0, "acc": 0}
    for kind, _ in units:
        kind_no.append(n_kind[kind])
        n_kind[kind] += 1
    acc_unit = [u for u, x in enumerate(units) if x[0] == "acc"]
    acc_after = [sum(x[0] == "split" for x in units[:u]) for u in acc_unit]
    ring_no, in_ring, landed_value, count = [], ([], []), [], {}
    for u, (kind, parts) in enumerate(units):
        acc = kind == "acc"
        n = len(in_ring[acc])
        slot = (acc, n % (ACC if acc else RAW))
        count[slot] = count.get(slot, 0) + 16 * len(parts)
        ring_no.append(n)
        in_ring[acc].append(u)
        landed_value.append(count[slot])
    unit_of_split = [u for u, x in enumerate(units) if x[0] == "split"]

    def sp(name):
        return kind_no[start[name]]

    by_dve = [False] * n_kind["split"]
    for name, n in (("fi0C", 2 * FT), ("fo0C", FT), ("v1C", KT)):
        for u in range(sp(name), sp(name) + n):
            by_dve[u] = True
    low_no = [sum(x == by_dve[u] for x in by_dve[:u]) for u in range(len(by_dve))]

    with ExitStack() as ctx:
        def sb(name, shape, dt=F32, scope=ctx):
            return scope.enter_context(nc.sbuf_tensor(name, shape, dt))

        x_res = sb("x_res", [P, NT, D])
        h_hi = sb("h_hi", [P, KT, TOK], F32R)
        h_lo = sb("h_lo", [P, KT, TOK], F32R)
        w_raw = sb("w_raw", [P, RAW, UNIT])
        w_hi = sb("w_hi", [P, RING, UNIT], F32R)
        w_lo = sb("w_lo", [P, RING, UNIT], F32R)
        with ExitStack() as early:
            state = sb("state", [P, 11, 4, P], scope=early)
        with ExitStack() as early:
            sb("before", [P, D], scope=early)
            bias_m = sb("bias_m", [P, 2, 3 * P], scope=early)
            rel_last = sb("rel_last", [P, 8, BIAS_RUN], scope=early)
        gate_b = sb("gate_b", [P, 2, D])
        xs = sb("xs", [P, 2, D])
        full = sb("full", [P, KT, P])
        junk = sb("junk", [P, D], BF16)
        ident = sb("ident", [P, P])
        ident_b = sb("ident_b", [P, P], BF16)
        window_b = sb("window_b", [P, 2 * P], BF16)
        near_b = sb("near_b", [P, LT, 3 * P], BF16)
        tri = sb("tri", [P, 2, P])
        bias_col = sb("bias_col", [P, 96])
        par_col = sb("par_col", [P, 84])
        c_col = sb("c_col", [P, KT, 2])
        mod_col = sb("mod_col", [P, 12, 2, KT])
        pre_a = sb("pre_a", [P, 4, 2, KT])
        gate_col = sb("gate_col", [P, 4, 2, KT])
        half_neg = sb("half_neg", [P, 8])
        one_col = sb("one_col", [P, 1])
        sink = sb("sink", [P, 8])
        nsink = sb("nsink", [P, 8])
        negm = sb("negm", [P, 2, 8])
        rowsum = sb("rowsum", [P, 2, 8])
        sm = sb("sm", [P, 4, 8])
        raw_max = sb("raw_max", [P, 2])
        ctx_max = sb("ctx_max", [P, 2])
        ssq_pre, ms_pre, rs_pre = (sb(n, [P, 24]) for n in ("ssq_pre", "ms_pre", "rs_pre"))
        ssq_post, ms_post, rs_post = (sb(n, [P, 24]) for n in ("ssq_post", "ms_post", "rs_post"))
        gla_ssq, gla_ms, gla_rs = (sb(n, [P, NT, 4]) for n in ("gla_ssq", "gla_ms", "gla_rs"))
        decay = sb("decay", [P, 4, 2 * NT])

        with ExitStack() as s0:
            par_rows = sb("par_rows", [P, 2, P], scope=s0)
            mask_in = sb("mask_in", [P, 2 * P + LT * 3 * P], scope=s0)
            sb("fence0", [P, 64], scope=s0)
        with ExitStack() as s1:
            b_q = sb("b_q", [P, 2, TOK], scope=s1)
            b_k = sb("b_k", [P, 2, TOK], scope=s1)
            b_v = sb("b_v", [P, NT, BV], scope=s1)
            b_o = sb("b_o", [P, 4, TOK], scope=s1)
            r_t = sb("r_t", [33, TOK], scope=s1)
            gw = sb("gw", [33, 2 * BQK], scope=s1)
            with ExitStack() as s2:
                cos = sb("cos", [P, SEQ], scope=s2)
                sin = sb("sin", [P, SEQ], scope=s2)
                rope_t = sb("rope_t", [P, 2, SEQ], scope=s2)
                a_q = sb("a_q", [P, 4, TOK], scope=s2)
                a_k = sb("a_k", [P, 2, TOK], scope=s2)
                a_v = sb("a_v", [P, NT, AKV], scope=s2)
                prob0 = sb("prob0", [P, 2, 5 * P], scope=s2)
                prob0_t = sb("prob0_t", [P, 2, 5 * P], scope=s2)
            with ExitStack() as s2:
                with ExitStack() as s3:
                    la = sb("la", [P, NT, 2 * BQK], scope=s3)
                kg_t = sb("kg_t", [P, NT, 2 * BQK], scope=s2)
                qg = sb("qg", [P, 4, TOK], scope=s2)
                kg = sb("kg", [P, 4, TOK], scope=s2)
                att_m = sb("att_m", [P, 2, 4 * P], scope=s2)
        with ExitStack() as s1:
            hid_hi = sb("hid_hi", [P, FH * SEQ], F32R, scope=s1)
            hid_lo = sb("hid_lo", [P, FH * SEQ], F32R, scope=s1)
            y_half = sb("y_half", [P, LT, D], scope=s1)
            silu_g = sb("silu_g", [P, 2, SEQ], scope=s1)
            hid_f = sb("hid_f", [P, 2, SEQ], scope=s1)
            mod_acc = sb("mod_acc", [P, 2, D], scope=s1)
            mod_raw = sb("mod_raw", [P, ACC, UNIT], scope=s1)
        with ExitStack() as s1:
            c_q = sb("c_q", [P, KT, SEQ], scope=s1)
            c_k = sb("c_k", [P, KT, TOK], scope=s1)
            c_v = sb("c_v", [P, NT, D], scope=s1)
            rel = sb("rel", [P, 8, BIAS_RUN], scope=s1)
            prob1 = sb("prob1", [P, 2, 5 * P], scope=s1)
            prob1_t = sb("prob1_t", [P, 2, 5 * P], scope=s1)

        PS = ctx.enter_context(nc.psum_tensor("ps", [P, 8, 512], F32))

        def ps(bank, lo, hi, p0=0, p1=P):
            return PS[p0:p1].rearrange("p b n -> p (b n)")[:, bank * 512 + lo:bank * 512 + hi]

        def sem(name):
            return ctx.enter_context(nc.semaphore(name))

        landed = [sem(f"w_landed{i}") for i in range(RAW)]
        acc_landed = [sem(f"acc_landed{i}") for i in range(ACC)]
        (consts_in, par_in, x_in, gw_zero, gw_in, rel_in, stored) = map(sem, (
            "consts_in", "par_in", "x_in", "gw_zero", "gw_in", "rel_in", "stored"))
        gl_av = sem("gl_av")
        ident_in, masks_done = sem("ident_in"), sem("masks_done")
        w_lo_dve, w_acc, pre_half = sem("w_lo_dve"), sem("w_acc"), sem("pre_half")
        (w_hi_done, w_lo_done, w_used, w_direct, tm_done) = map(sem, (
            "w_hi_done", "w_lo_done", "w_used", "w_direct", "tm_done"))
        (small_done, par_turned, par_done, c_done) = map(sem, ("small_done", "par_turned", "par_done", "c_done"))
        (mod_copied, mod_turned, mod_done, mod_der) = map(sem, ("mod_copied", "mod_turned", "mod_done", "mod_der"))
        (gb_ready, gb_done) = map(sem, ("gb_ready", "gb_done"))
        (pre_ssq, pre_ms, pre_rs, pre_xs, pre_tr, pre_full, pre_hi, pre_lo) = map(sem, (
            "pre_ssq", "pre_ms", "pre_rs", "pre_xs", "pre_tr", "pre_full", "pre_hi", "pre_lo"))
        (post_y, post_ssq, post_ms, post_rs, post_n, post_x) = map(sem, (
            "post_y", "post_ssq", "post_ms", "post_rs", "post_n", "post_x"))
        (v_act, v_dve, fe_act, fe_dve, rope_m, rope_done, bo_done, fe1_act) = map(sem, (
            "v_act", "v_dve", "fe_act", "fe_dve", "rope_m", "rope_done", "bo_done", "fe1_act"))
        (ff_silu, ff_full, ff_hi, ff_lo, half_done) = map(sem, ("ff_silu", "ff_full", "ff_hi", "ff_lo", "half_done"))
        at_c, at_b = sem("at_c"), sem("at_b")
        (at_s, at_r, at_m, at_p, at_t, at_e, at_o) = map(sem, (
            "at_s", "at_r", "at_m", "at_p", "at_t", "at_e", "at_o"))
        (at_shift, at_sink, at_den, at_rinv, at_on, at_f, at_hi, at_lo) = map(sem, (
            "at_shift", "at_sink", "at_den", "at_rinv", "at_on", "at_f", "at_hi", "at_lo"))
        (gl_z, gl_abs, gl_exp, gl_ln, gl_la, gl_cum, gl_eq, gl_ek, gl_dec, gl_q, gl_k, gl_kt, gl_ktc) = map(sem, (
            "gl_z", "gl_abs", "gl_exp", "gl_ln", "gl_la", "gl_cum", "gl_eq", "gl_ek", "gl_dec", "gl_q", "gl_k",
            "gl_kt", "gl_ktc"))
        (gl_ds, gl_u, gl_s, gl_att, gl_msk, gl_o, gl_ssq, gl_ms, gl_rs, gl_on, gl_f, gl_full, gl_hi, gl_lo) = map(
            sem, ("gl_ds", "gl_u", "gl_s", "gl_att", "gl_msk", "gl_o", "gl_ssq", "gl_ms", "gl_rs", "gl_on", "gl_f",
                  "gl_full", "gl_hi", "gl_lo"))

        TM = [("v0", 6), ("out0L", 4), ("out0C", 2), (("fo0L", 0), 4), (("fo0L", 1), 4), ("fo0C", 2), ("v1L", 4),
              ("v1C", 2), ("out1L", 4), (("fo1L", 0), 4), (("fo1L", 1), 4)]
        tm_base, n = {}, 0
        for name, tiles in TM:
            tm_base[name] = (n, tiles)
            n += tiles - 1
        PRE = {"mix0": 0, "ffn0L": 6, "ffn0C": 10, "mix1": 12, "ffn1L": 18}
        POST = {"out0L": 0, "out0C": 4, "fo0L": 6, "fo0C": 10, "out1L": 12, "fo1L": 16}
        FI = {("fi0L", 0): 0, ("fi0L", 1): FH, "fi0C": 2 * FH, ("fi1L", 0): 4 * FH, ("fi1L", 1): 5 * FH}
        n_groups = {0: NT, 1: 2 * LT}
        STEPS = {0: attention_steps(0), 1: attention_steps(1)}
        STEP0 = {0: 0, 1: len(STEPS[0])}
        GROUP0 = {0: 0, 1: n_groups[0]}
        f_order = [8, 9, 10, 11, 0, 1, 2, 3, 4, 5, 6, 7]
        b_order = [11, 10, 9, 8, 7, 6, 5, 4, 3, 2, 1, 0]

        def wait_tm(eng, name, i, k_units):
            base, tiles = tm_base[name]
            if i == tiles - 1:
                eng.wait_ge(w_used, sp(name) + k_units)
            else:
                eng.wait_ge(tm_done, base + i + 1)

        def in0_bank(i):
            return 4 if i == 14 else 2 * (i % 2)

        def qk_bank(i):
            return 6 + i if i < 2 else 2 * (i % 2)

        def low_ready(s):
            return (w_lo_dve if by_dve[s] else w_lo_done), low_no[s] + 1

        def acc_place(b):
            return gate_b if b == 1 else xs if b < 6 else mod_acc

        def acc_slot(n):
            if n < 5 * KT:
                return (prob0, prob0_t)[n % ACC][:].rearrange("p a n -> p (a n)")[:, 0:UNIT]
            return mod_raw[:, n % ACC, :]

        def low_part(eng, u):
            raw = unit_of_split[u]
            width = sum(w for _, _, w, _ in units[raw][1]) * (KT if units[raw][1][0][0] == "fm" else 1)
            eng.wait_ge(w_hi_done, u + 1)
            if u >= RING:
                eng.wait_ge(w_used, u - RING + 1)
            eng.tensor_tensor(w_lo[:, u % RING, 0:width], w_raw[:, ring_no[raw] % RAW, 0:width],
                              w_hi[:, u % RING, 0:width].bitcast(F32), ALU.subtract).then_inc(low_ready(u)[0], 1)

        def bcast(ap, n):
            return bass.AP(ap.tensor, ap.offset, [list(x) for x in ap.ap] + [[0, n]])

        def group_out(layer, t, g, f):
            if layer == 0:
                return lambda h: h[:, 4 * g + f, t * P:(t + 1) * P], lambda x: x
            return (lambda h: h[:, 4 * g + f, 0:SEQ].rearrange("p (r b c) -> p b r c", b=8, c=8)[:, 2 * t:2 * t + 2],
                    lambda x: x.rearrange("p (b r c) -> p b r c", b=2, c=8))

        def tile_of(h, name, t):
            if name == "mix1" and t < LT:
                return h[:, :, 0:SEQ].rearrange("p k (b n) -> p k b n", b=8)[:, :, :, 16 * t:16 * t + 16]
            return h[:, :, t * P:(t + 1) * P]

        def full_tile(name, t):
            x = full[:]
            return x.rearrange("p k (b n) -> p k b n", b=8) if name == "mix1" and t < LT else x

        def turned(name, t, k, n):
            dst, src = full[:, k, :], ps(pre_bank(name, n), k * P, (k + 1) * P)
            if name == "mix1" and t < LT:
                return (dst.rearrange("p (b r c) -> p r b c", b=8, c=8), src.rearrange("p (r b c) -> p r b c", b=8, c=8))
            return dst, src

        def rel_load(g, part=0):
            b, r = divmod(part, 8)
            p = 64 * b + 8 * r
            first = BIAS_PAD + (8 * g + 7) * BIAS_HEAD + (7 - r) * BIAS_ROW - 1 - 8 * b
            first = 2 * BIAS_PAD + 16 * BIAS_HEAD - 1 - (first + BIAS_RUN - 1)
            return (rel, rel_last)[g][p:p + 8], bass.AP(a["rel_rev"].tensor, first, [[1, 8], [BIAS_HEAD, 8], [1, BIAS_RUN]])

        gb_base, gb_after = [0, 2, 4, 5], [0, 6, 12, 16]
        gb_need = {"out0L": (1, 2), "out0C": (1, 2), "fo0L": (3, 4), "fo0C": (3, 4), "out1L": (5, 5), "fo1L": (6, 6)}
        tm_name = {"out0L": "out0L", "out0C": "out0C", "fo0C": "fo0C", "out1L": "out1L"}
        n_y = {"fo0L": 0, "fo1L": LT}
        full_free = {"out0L": (at_f, n_groups[0]), "out0C": (pre_lo, PRE["ffn0C"]), "fo0L": (pre_lo, PRE["mix1"]),
                     "fo0C": (pre_lo, PRE["mix1"] + LT)}

        def post_place(name, i):
            return x_res[:, LT + i % 2, :] if name in ("out1L", "fo1L") else full[:].rearrange("p k n -> p (k n)")

        def post_add(eng, name, i, t):
            eng.wait_ge(post_n, POST[name] + i + 1)
            eng.tensor_tensor(x_res[:, t, :], x_res[:, t, :], post_place(name, i), ALU.add).then_inc(post_x, 1)

        posts_before = {"mix0": 0, "ffn0L": 4, "ffn0C": 6, "ffn1L": 0}
        PRE_MOD = {"mix0": (0, 0), "ffn0L": (3, 1), "ffn0C": (3, 1), "mix1": (6, 2), "ffn1L": (9, 3)}

        def pre_bank(name, n):
            return {"mix0": 2, "ffn0L": 0}.get(name, 4) + 2 * (n % 2)

        def tm_bank(name, i):
            return {"out0L": (4, 6, 0, 2), "out0C": (4, 6), "v1C": (4, 6)}.get(name, (0, 2, 4, 6))[i]

        def free_full(eng, name, i):
            if PRE[name] + i:
                eng.wait_ge(pre_lo, PRE[name] + i)
            n_post = posts_before.get(name, 10 if i < LT else 12)
            if n_post:
                eng.wait_ge(post_x, n_post)
            if name == "ffn1L":
                eng.wait_ge(at_f, n_groups[0] + n_groups[1])

        def s_cols(layer, a):
            t = STEPS[layer][a][0]
            return (len(local_tiles(t)) + CT) * P

        block = ctx.enter_context(nc.Block())

        @block.sync
        def _(sync):
            sync.dma_start(ident[:], a["k_ident"]).then_inc(ident_in, 16)
            sync.dma_start(par_rows[0:96, 0, :], a["b_mod"].rearrange("l (r n) -> (l r) n", n=P)).then_inc(par_in, 16)
            at = 0
            for name in ("g_mix_pre", "g_mix_post", "g_ffn_pre", "g_ffn_post", "gla_norm_g"):
                src = a[name].rearrange("l (r n) -> (l r) n", n=P)
                n = src.shape[0]
                sync.dma_start(par_rows[at:at + n, 1, :], src).then_inc(par_in, 16)
                at += n
            for src in (a["c"].rearrange("b (r n) -> (b r) n", n=P), a["c_ctx"].rearrange("(r n) -> r n", n=P)):
                sync.dma_start(par_rows[at:at + KT, 1, :], src).then_inc(par_in, 16)
                at += KT
            sync.dma_start(sink[:], a["a_sink"].partition_broadcast(P)).then_inc(par_in, 16)
            for u, (kind, parts) in enumerate(units):
                n = ring_no[u]
                if u == start["v0"]:
                    for dst, src in ((mask_in[:, 0:2 * P], a["k_window"]), (mask_in[:, 2 * P:], a["k_near"]),
                                     (tri[:].rearrange("p a n -> p (a n)"), a["k_tri"]),
                                     (cos[:], a["k_cos"]), (sin[:], a["k_sin"])):
                        sync.dma_start(dst, src).then_inc(consts_in, 16)
                if kind == "acc":
                    if n >= ACC:
                        sync.wait_ge(w_acc, n - ACC + 1)
                    sync.dma_start(acc_slot(n), parts[0][3]).then_inc(acc_landed[n % ACC], 16)
                    continue
                if n >= RAW:
                    v = in_ring[0][n - RAW]
                    if units[v][0] == "direct":
                        sync.wait_ge(w_direct, kind_no[v] + 1)
                    else:
                        sync.wait_ge(w_hi_done, kind_no[v] + 1)
                        sync.wait_ge(*low_ready(kind_no[v]))
                for layout, at, width, src in parts:
                    dst = w_raw[:, n % RAW, :]
                    if layout == "fm":
                        dst = dst.rearrange("p (k n) -> p k n", k=KT)
                        dst = dst[:, :, at:at + width]
                    else:
                        dst = dst[:, at:at + width]
                    sync.dma_start(dst, src).then_inc(landed[n % RAW], 16)
            for t in L_TILES:
                sync.wait_ge(post_x, POST["fo1L"] + t + 1)
                sync.dma_start(out[0, t * P:(t + 1) * P, :], x_res[:, t, :]).then_inc(stored, 16)
            sync.wait_ge(stored, 16 * LT)

        @block.gpsimd
        def _(pool):
            pool.memset(half_neg[:], -0.5).then_inc(small_done, 1)
            pool.memset(one_col[:], 1.0).then_inc(small_done, 1)
            pool.wait_ge(small_done, 2)
            fed = [0]

            def feed(s):
                while fed[0] <= s:
                    if not by_dve[fed[0]]:
                        low_part(pool, fed[0])
                    fed[0] += 1

            def root(ssq, m, r, width, n_done, s_ssq, s_ms, s_rs, sums=1):
                pool.wait_ge(s_ssq, sums * (n_done + 1))
                pool.tensor_scalar(m, ssq, 1.0 / width, EPS, ALU.mult, ALU.add).then_inc(s_ms, 1)
                pool.wait_ge(s_ms, n_done + 1)
                pool.tensor_tensor(r, m, half_neg[:, 0:m.shape[1]], ALU.pow).then_inc(s_rs, 1)

            def pre(name, i):
                n = PRE[name] + i
                root(ssq_pre[:, n:n + 1], ms_pre[:, n:n + 1], rs_pre[:, n:n + 1], D, n, pre_ssq, pre_ms, pre_rs)

            def post(name, i):
                n = POST[name] + i
                root(ssq_post[:, n:n + 1], ms_post[:, n:n + 1], rs_post[:, n:n + 1], D, n,
                     post_ssq, post_ms, post_rs)

            for i in range(NT):
                pre("mix0", i)
            feed(sp("in0") + 14)
            for t in range(NT):
                root(gla_ssq[:, t, :], gla_ms[:, t, :], gla_rs[:, t, :], P, t, gl_ssq, gl_ms, gl_rs, 4)
            feed(sp("out0C") + RING - 2)
            for i in range(LT):
                post("out0L", i)
                feed(sp("out0C") + i + RING - 2)
            for i in range(LT):
                pre("ffn0L", i)
                if i < 3:
                    feed(sp("out0C") + 4 + i + RING - 2)
            feed(sp(("fi0L", 0)) + RING - 1)
            for i in range(CT):
                post("out0C", i)
            for i in range(CT):
                pre("ffn0C", i)
            feed(sp("fi0C") + RING - 1)
            for j in range(LT + 1):
                if j < LT:
                    post("fo0L", j)
                    post_add(pool, "fo0L", j, j)
                if j:
                    pre("mix1", j - 1)
            feed(sp("qk1") + 1)
            for i in range(CT):
                post("fo0C", i)
            for i in range(CT):
                pre("mix1", LT + i)
            feed(sp("v1C") + KT - 1)
            for i, (t, g, h) in enumerate(STEPS[1]):
                if i % 4 == 0 and 0 < i <= 4 * RING:
                    feed(sp("out1L") + i // 4 - 1)
                near = local_tiles(t)
                d0 = near[0] - t + 1
                run = (rel, rel_last)[g][:, 7 - h, BIAS_RUN - 1 - 16 * d0:BIAS_RUN - 16 * d0]
                run = bass.AP(run.tensor, run.offset,
                              [list(run.ap[0]), [-8, 2 * len(near)], [-BIAS_ROW, 8], [-1, 8]])
                split = lambda x: x.rearrange("p (b r c) -> p b r c", r=8, c=8)
                pool.wait_ge(rel_in, 16 * 32)
                if i == 0:
                    pool.wait_ge(pre_tr, PRE["mix1"] + NT)
                if i >= 2:
                    pool.wait_ge(at_r, STEP0[1] + i - 1)
                pool.tensor_tensor(split(bias_m[:, i % 2, 0:len(near) * P]), run,
                                   split(near_b[:, t, d0 * P:(d0 + len(near)) * P]), ALU.add).then_inc(at_b, 1)
            feed(sp("out1L") + 7)
            feed(sp(("fi1L", 0)) + RING - 2)
            for i in range(LT + 2):
                if i < LT:
                    post("out1L", i)
                if 0 < i <= LT:
                    pre("ffn1L", i - 1)
            feed(sp(("fo1L", 1)) + FH - 1)
            for i in range(LT):
                post("fo1L", i)

        @block.scalar
        def _(act):
            fed = [0]
            junk_written = []

            def square(src, ssq, done, value, into=junk):
                if junk_written:
                    act.wait_ge(*junk_written.pop())
                act.activation(into[:, 0:src.shape[1]], src, ACT.Square, accum_out=ssq).then_inc(done, 1)
                junk_written.append((done, value))

            def feed(s):
                while fed[0] <= min(s, n_kind["split"] - 1):
                    u = fed[0]
                    raw = unit_of_split[u]
                    width = sum(w for _, _, w, _ in units[raw][1]) * (KT if units[raw][1][0][0] == "fm" else 1)
                    act.wait_ge(landed[ring_no[raw] % RAW], landed_value[raw])
                    if u >= RING:
                        act.wait_ge(w_used, u - RING + 1)
                    act.activation(w_hi[:, u % RING, 0:width], w_raw[:, ring_no[raw] % RAW, 0:width],
                                   ACT.Copy).then_inc(w_hi_done, 1)
                    fed[0] += 1

            def pre_square(name, i, tiles, ready):
                n = PRE[name] + i
                act.wait_ge(*ready)
                square(x_res[:, tiles[i], :], ssq_pre[:, n:n + 1], pre_ssq, n + 1)

            def pre_high(name, i, tiles):
                n, t = PRE[name] + i, tiles[i]
                lc, (b, j) = int(t >= LT), PRE_MOD[name]
                act.wait_ge(pre_tr, n + 1)
                free_full(act, name, i)
                act.wait_ge(mod_der, 2 * j + 1)
                act.wait_ge(mod_done, b + 1)
                for k in range(KT // 2):
                    last = act.activation(*turned(name, t, k, n), ACT.Identity, bias=mod_col[:, b, lc, k:k + 1], scale=pre_a[:, j, lc, k:k + 1])
                last.then_inc(pre_half, 1)
                act.wait_ge(pre_half, n + 1)
                act.wait_ge(pre_full, n + 1)
                act.activation(tile_of(h_hi, name, t), full_tile(name, t), ACT.Copy).then_inc(pre_hi, 1)

            def post_square(name, i, k_units=None):
                n = POST[name] + i
                if k_units is None:
                    act.wait_ge(post_y, n_y[name] + i + 1)
                    src = y_half[:, i, :]
                else:
                    wait_tm(act, tm_name[name], i, k_units)
                    src = ps(tm_bank(name, i), 0, D)
                square(src, ssq_post[:, n:n + 1], post_ssq, n + 1)

            def gate_rows(b, n_lc):
                for lc in range(n_lc):
                    act.wait_ge(gb_ready, gb_base[b] + lc + 1)
                    if gb_after[b]:
                        act.wait_ge(post_n, gb_after[b])
                    act.activation(gate_b[:, lc, :], ps(4 + 2 * lc, 0, D), ACT.Copy).then_inc(gb_done, 1)

            def ffn_in(name, n_js, width, hooks=None):
                s, f0 = sp(name), FI[name]
                for j in range(n_js):
                    f = f0 + j
                    feed(s + 2 * j + RING - 1)
                    act.wait_ge(w_used, s + 2 * j + 1)
                    if f >= 2:
                        act.wait_ge(ff_full, f - 1)
                    act.activation(silu_g[:, f % 2, 0:width], ps(2 * (f % 2), 0, width), ACT.Silu)\
                        .then_inc(ff_silu, 1)
                    feed(s + 2 * j + RING)
                    act.wait_ge(ff_full, f + 1)
                    act.activation(hid_hi[:, j * width:(j + 1) * width], hid_f[:, f % 2, 0:width], ACT.Copy)\
                        .then_inc(ff_hi, 1)
                    feed(s + 2 * j + RING + 1)
                    if hooks and j in hooks:
                        hooks[j]()

            def attention(layer, meanwhile):
                steps, a0, g0 = STEPS[layer], STEP0[layer], GROUP0[layer]
                prob = (prob0, prob1)[layer]

                def softmax(i):
                    a, n = a0 + i, s_cols(layer, i)
                    g, h = g0 + i // 8, steps[i][2]
                    act.wait_ge(at_m, a + 1)
                    if a >= 2:
                        act.wait_ge(at_t, a - 1)
                    act.activation(prob[:, i % 2, 0:n], ps(2 * (i % 2), 0, n), ACT.Exp, bias=negm[:, g % 2, h:h + 1],
                                   scale=SCALE if layer == 0 else 1.0,
                                   accum_out=rowsum[:, g % 2, h:h + 1]).then_inc(at_p, 1)

                def high(gi):
                    t, grp, _ = steps[8 * gi]
                    act.wait_ge(at_f, g0 + gi + 1)
                    for f in range(4):
                        dst, order = group_out(layer, t, grp, f)
                        last = act.activation(dst(h_hi), order(ps(6 + gi % 2, f * P, (f + 1) * P)), ACT.Copy)
                    last.then_inc(at_hi, 1)

                n_pairs = len(steps) // 2
                for p in range(n_pairs + 4):
                    if p < n_pairs:
                        softmax(2 * p)
                        softmax(2 * p + 1)
                    if p == 0:
                        meanwhile()
                    if p % 4 == 3 and p < n_pairs and layer == 0:
                        act.wait_ge(at_shift, p // 4 + 1)
                        act.activation(sm[:, 1, :], sm[:, 0, :], ACT.Exp).then_inc(at_sink, 1)
                    if p % 4 == 3 and p > 4:
                        high(p // 4 - 1)

            act.dma_start(x_res[:, 0:LT, :], a["x"][0].rearrange("(t p) d -> p t d", p=P)).then_inc(x_in, 16)
            act.dma_start(x_res[:, LT:NT, :], a["ctx"][0].rearrange("(t p) d -> p t d", p=P)).then_inc(x_in, 16)
            act.wait_ge(gw_zero, 1)
            act.dma_start(gw[0:RANK, 0:BQK], a["gla_gate_f_w"][0]).then_inc(gw_in, 16)
            act.dma_start(gw[RANK:2 * RANK, BQK:], a["gla_gate_b_w"][0]).then_inc(gw_in, 16)
            act.dma_start(gw[2 * RANK:, 0:BQK], a["gla_gate_f_b"]).then_inc(gw_in, 16)
            act.dma_start(gw[2 * RANK:, BQK:], a["gla_gate_b_b"]).then_inc(gw_in, 16)
            act.wait_ge(par_done, 1)
            act.activation(c_col[:], par_col[:, 68:84].rearrange("p (v k) -> p k v", v=2), ACT.Silu)\
                .then_inc(c_done, 1)
            for i in range(NT):
                pre_square("mix0", i, range(NT), (x_in, 32))
            act.wait_ge(w_direct, KT)
            act.activation(full[0:2], ps(0, 0, D, 0, 2).rearrange("p (k n) -> p k n", k=KT), ACT.Copy)\
                .then_inc(mod_copied, 1)
            for i in range(NT):
                pre_high("mix0", i, range(NT))
                if i < RING:
                    feed(sp("v0") + i)
            feed(sp("in0") + 1)
            for t in range(NT):
                wait_tm(act, "v0", t, KT)
                act.activation(b_v[:, t, :], ps(t, 0, BV), ACT.Copy).then_inc(v_act, 1)
            def in0_unit(i):
                s = sp("in0") + i
                feed(s + RING - 2)
                act.wait_ge(w_used, s + 1)
                bl = in0_bank(i)
                bc = bl + 1
                lat, con = ps(bl, 0, SEQ), ps(bc, 0, CTX)
                if i == 6:
                    act.wait_ge(masks_done, 1)
                if i < 6:
                    dst = a_q[:, i] if i < 4 else a_k[:, i - 4]
                    act.activation(dst[:, SEQ:], con, ACT.Copy).then_inc(fe_act, 1)
                    return
                if i < 8:
                    dst, fn, scale = b_q[:, i - 6], ACT.Copy, SCALE
                elif i < 10:
                    dst, fn, scale = b_k[:, i - 8], ACT.Copy, 1.0
                elif i < 14:
                    dst, fn, scale = b_o[:, i - 10], ACT.Silu, 1.0
                else:
                    dst, fn, scale = r_t[0:32], ACT.Copy, 1.0
                    lat, con = ps(bl, 0, SEQ, 96, P), ps(bc, 0, CTX, 96, P)
                act.activation(dst[:, 0:SEQ], lat, fn, scale=scale)
                act.activation(dst[:, SEQ:], con, fn, scale=scale).then_inc(fe_act, 1)

            for i in range(14):
                in0_unit(i)
            feed(sp("in0") + 14)
            attention(0, lambda: in0_unit(14))

            for t in range(NT):
                act.wait_ge(gl_z, t + 1)
                if t == 0:
                    act.wait_ge(at_lo, n_groups[0])
                act.activation(la[:, t, :], ps(t, 0, 512), ACT.Abs).then_inc(gl_abs, 1)
                act.wait_ge(gl_abs, t + 1)
                act.activation(la[:, t, :], la[:, t, :], ACT.Exp, scale=-1.0).then_inc(gl_exp, 1)
            for t in range(NT):
                act.wait_ge(gl_exp, t + 1)
                act.activation(la[:, t, :], la[:, t, :], ACT.Ln, bias=one_col[:]).then_inc(gl_ln, 1)
            for t in range(NT):
                act.wait_ge(gl_cum, t + 1)
                src = ps(6 + t % 2, 0, 512).rearrange("p (m n) -> p m n", m=4)
                act.activation(qg[:, :, t * P:(t + 1) * P], src, ACT.Exp, scale=1.0 / 16).then_inc(gl_eq, 1)
                act.activation(kg[:, :, t * P:(t + 1) * P], src, ACT.Exp, scale=-1.0 / 16).then_inc(gl_ek, 1)

            def gla_high(t):
                act.wait_ge(gl_full, t + 1)
                act.activation(h_hi[:, 4:8, t * P:(t + 1) * P],
                               b_q[:].rearrange("p a n -> p (a n)")[:, 0:512].rearrange("p (h n) -> p h n", h=4),
                               ACT.Copy).then_inc(gl_hi, 1)

            for t in range(NT):
                act.wait_ge(gl_o, t + 1)
                for h in range(4):
                    square(ps(4 + 2 * (t % 2) + h % 2, (h // 2) * P, (h // 2 + 1) * P), gla_ssq[:, t, h:h + 1], gl_ssq, 4 * t + h + 1,
                           kg_t[:, 0])
                if t:
                    gla_high(t - 1)
            gla_high(NT - 1)

            gate_rows(0, 2)
            feed(sp("out0C") + RING - 2)
            for i in range(LT):
                post_square("out0L", i, KT)
                feed(sp("out0C") + i + RING - 2)
            for i in range(LT):
                pre_square("ffn0L", i, L_TILES, (post_x, POST["out0L"] + i + 1))
                if i < 3:
                    feed(sp("out0C") + 4 + i + RING - 2)
            for i in range(LT):
                pre_high("ffn0L", i, L_TILES)
                if i < RING:
                    feed(sp(("fi0L", 0)) + i)
            for i in range(CT):
                post_square("out0C", i, KT)
            for i in range(CT):
                pre_square("ffn0C", i, C_TILES, (post_x, POST["out0C"] + i + 1))
            ffn_in(("fi0L", 0), FH, SEQ,
                   {3: lambda: [pre_high("ffn0C", i, C_TILES) for i in range(CT)], 4: lambda: gate_rows(1, 2)})
            feed(sp(("fi0L", 1)) + RING - 1)
            ffn_in(("fi0L", 1), FH, SEQ)
            feed(sp("fi0C") + RING - 1)
            hooks = {j: (lambda i=j: (post_square("fo0L", i) if i < LT else None,
                                      pre_square("mix1", i - 1, L_TILES, (post_x, POST["fo0L"] + i)) if i else None))
                     for j in range(LT + 1)}
            hooks |= {6 + 2 * j: (lambda i=j: pre_high("mix1", i, L_TILES)) for j in range(LT)}
            ffn_in("fi0C", FT, CTX, hooks)
            feed(sp("qk1") + 1)
            for i in range(CT):
                post_square("fo0C", i, FT)
            for i in range(CT):
                pre_square("mix1", LT + i, range(NT), (post_x, POST["fo0C"] + i + 1))

            feed(sp("qk1") + RING - 1)
            for i in range(16):
                s = sp("qk1") + i
                feed(s + RING - 1)
                act.wait_ge(w_used, s + 1)
                bank = qk_bank(i)
                if i == 0:
                    for part in range(16):
                        act.dma_start(*rel_load(0, part)).then_inc(rel_in, 16)
                if i == KT:
                    act.wait_ge(pre_tr, PRE["mix1"] + NT)
                    for part in range(16):
                        act.dma_start(*rel_load(1, part)).then_inc(rel_in, 16)
                if i < KT:
                    act.activation(c_q[:, i, :], ps(bank, 0, SEQ), ACT.Copy, scale=SCALE).then_inc(fe1_act, 1)
                    if i == 4:
                        for t in C_TILES:
                            pre_high("mix1", t, range(NT))
                else:
                    act.activation(c_k[:, i - KT, 0:SEQ], ps(bank, 0, SEQ), ACT.Copy)
                    act.activation(c_k[:, i - KT, SEQ:], ps(bank + 1, 0, CTX), ACT.Copy).then_inc(fe1_act, 1)
            gate_rows(2, 1)
            def layer1_values(name, tiles):
                for i, t in enumerate(tiles):
                    wait_tm(act, name, i, KT)
                    act.activation(c_v[:, t, :], ps(tm_bank(name, i), 0, D), ACT.Copy).then_inc(v_act, 1)
                feed(sp(name) + KT + RING - 1)

            feed(sp("v1C") + 1)
            layer1_values("v1L", L_TILES)
            feed(sp("v1C") + 7)
            attention(1, lambda: layer1_values("v1C", C_TILES))
            feed(sp("out1L") + 7)
            feed(sp(("fi1L", 0)) + RING - 2)
            for i in range(LT + 3):
                if i < LT:
                    post_square("out1L", i, KT)
                if 0 < i <= LT:
                    pre_square("ffn1L", i - 1, L_TILES, (post_x, POST["out1L"] + i))
                if i > 2:
                    pre_high("ffn1L", i - 3, L_TILES)
            ffn_in(("fi1L", 0), FH, SEQ, {4: lambda: gate_rows(3, 1)})
            feed(sp(("fi1L", 1)) + RING - 1)
            ffn_in(("fi1L", 1), FH, SEQ)
            feed(sp(("fo1L", 1)) + FH - 1)
            for i in range(LT):
                post_square("fo1L", i)

        @block.vector
        def _(dve):
            def pre_scale(name, i, tiles):
                n = PRE[name] + i
                dve.wait_ge(pre_rs, n + 1)
                if n >= 2:
                    dve.wait_ge(pre_tr, n - 1)
                dve.tensor_scalar(xs[:, n % 2, :], x_res[:, tiles[i], :], rs_pre[:, n:n + 1], None,
                                  ALU.mult).then_inc(pre_xs, 1)

            def pre_modulate(name, i, tiles):
                n, lc, (b, j) = PRE[name] + i, int(tiles[i] >= LT), PRE_MOD[name]
                dve.wait_ge(pre_tr, n + 1)
                free_full(dve, name, i)
                dve.wait_ge(mod_der, 2 * j + 1)
                dve.wait_ge(mod_done, b + 1)
                for k in range(KT // 2, KT):
                    last = dve.tensor_scalar(*turned(name, tiles[i], k, n), pre_a[:, j, lc, k:k + 1], mod_col[:, b, lc, k:k + 1], ALU.mult, ALU.add)
                last.then_inc(pre_full, 1)

            def pre_low(name, i, tiles):
                n, t = PRE[name] + i, tiles[i]
                dve.wait_ge(pre_hi, n + 1)
                dve.tensor_tensor(tile_of(h_lo, name, t), full_tile(name, t), tile_of(h_hi, name, t).bitcast(F32),
                                  ALU.subtract).then_inc(pre_lo, 1)

            def pre_rest(name, tiles, scaled=0):
                for i in range(scaled, min(2, len(tiles))):
                    pre_scale(name, i, tiles)
                for i in range(len(tiles)):
                    pre_modulate(name, i, tiles)
                    if 2 <= i + 2 < len(tiles):
                        pre_scale(name, i + 2, tiles)
                    pre_low(name, i, tiles)

            def post_norm(name, i, t, k_units=None):
                n, lc = POST[name] + i, int(t >= LT)
                src = ps(tm_bank(name, i), 0, D) if k_units else y_half[:, i, :]
                dve.wait_ge(post_rs, n + 1)
                dve.wait_ge(gb_done, gb_need[name][lc])
                if n:
                    dve.wait_ge(post_x, n)
                if name in full_free:
                    dve.wait_ge(*full_free[name])
                dve.scalar_tensor_tensor(post_place(name, i), src, rs_post[:, n:n + 1], gate_b[:, lc, :], ALU.mult,
                                         ALU.mult).then_inc(post_n, 1)
                if name != "fo0L":
                    post_add(dve, name, i, t)

            def take_half(name, k_units):
                for i in range(LT):
                    wait_tm(dve, name, i, k_units)
                    dve.tensor_copy(y_half[:, i, :], ps(2 * i, 0, D)).then_inc(half_done, 1)

            def add_half(name, short, k_units):
                for i in range(LT):
                    wait_tm(dve, name, i, k_units)
                    dve.wait_ge(half_done, LT * (1 + (short == "fo1L")))
                    dve.tensor_tensor(y_half[:, i, :], y_half[:, i, :], ps(2 * i, 0, D), ALU.add).then_inc(post_y, 1)

            acc_done = [0]

            def accumulate(s):
                while acc_done[0] < len(acc_unit) and acc_after[acc_done[0]] <= s + 1:
                    n = acc_done[0]
                    b, k = 1 + n // KT, n % KT
                    acc, w = acc_place(b), acc_slot(n)
                    dve.wait_ge(acc_landed[n % ACC], landed_value[acc_unit[n]])
                    if k:
                        dve.wait_ge(w_acc, n)
                    elif b > 1:
                        dve.wait_ge(mod_turned, b)
                    if k == 0 and b == 2:
                        dve.wait_ge(pre_tr, NT)
                    for v in range(2):
                        if k == 0:
                            last = dve.tensor_scalar(acc[:, v, :], w, c_col[:, k, v:v + 1], None, ALU.mult)
                        else:
                            last = dve.scalar_tensor_tensor(acc[:, v, :], w, c_col[:, k, v:v + 1], acc[:, v, :],
                                                            ALU.mult, ALU.add)
                    last.then_inc(w_acc, 1)
                    acc_done[0] += 1

            def modulation(b, bank=7):
                l, i = divmod(b, 6)
                dve.wait_ge(mod_turned, b + 1)
                bias = bias_col[:, b * KT:(b + 1) * KT]
                bias = bass.AP(bias.tensor, bias.offset, [list(bias.ap[0]), [0, 2], [1, KT]])
                dve.tensor_tensor(mod_col[:, b], ps(bank, 0, 2 * KT).rearrange("p (k v) -> p v k", v=2), bias,
                                  ALU.add).then_inc(mod_done, 1)
                if i in (0, 3):
                    return
                which = {1: 0, 2: 0, 4: 1, 5: 1}[i]
                gain = {1: 0, 2: 16, 4: 32, 5: 48}[i] + l * KT
                gain = par_col[:, gain:gain + KT]
                gain = bass.AP(gain.tensor, gain.offset, [list(gain.ap[0]), [0, 2], [1, KT]])
                dve.wait_ge(mod_done, b + 1)
                if i in (1, 4):
                    dve.scalar_tensor_tensor(pre_a[:, 2 * l + which], mod_col[:, b], 1.0, gain, ALU.add,
                                             ALU.mult).then_inc(mod_der, 1)
                else:
                    dve.tensor_tensor(gate_col[:, 2 * l + which], mod_col[:, b], gain, ALU.mult).then_inc(mod_der, 1)

            fed = [0]

            def feed(s):
                while fed[0] <= s:
                    if by_dve[fed[0]]:
                        low_part(dve, fed[0])
                    fed[0] += 1

            def ffn_in(name, n_js, width, hooks=None):
                s, f0 = sp(name), FI[name]
                for j in range(n_js):
                    f = f0 + j
                    dve.wait_ge(w_used, s + 2 * j + 2)
                    dve.wait_ge(ff_silu, f + 1)
                    if f >= 2:
                        dve.wait_ge(ff_lo, f - 1)
                    dve.tensor_tensor(hid_f[:, f % 2, 0:width], silu_g[:, f % 2, 0:width],
                                      ps(2 * (f % 2) + 1, 0, width), ALU.mult).then_inc(ff_full, 1)
                    if by_dve[s]:
                        feed(s + 2 * j + 1 + RING)
                    dve.wait_ge(ff_hi, f + 1)
                    dve.tensor_tensor(hid_lo[:, j * width:(j + 1) * width], hid_f[:, f % 2, 0:width],
                                      hid_hi[:, j * width:(j + 1) * width].bitcast(F32), ALU.subtract)\
                        .then_inc(ff_lo, 1)
                    if hooks and j in hooks:
                        hooks[j]()
                    if by_dve[s]:
                        feed(s + 2 * j + 2 + RING)
                    if name[0] == "fi0L":
                        accumulate(s + 2 * j + 3)

            def attention(layer):
                steps, a0, g0 = STEPS[layer], STEP0[layer], GROUP0[layer]
                prob_t = (prob0_t, prob1_t)[layer]

                def maximum(i, between):
                    a, n = a0 + i, s_cols(layer, i)
                    g, h = g0 + i // 8, steps[i][2]
                    dve.wait_ge(at_s, a + 1)
                    if a >= 2:
                        dve.wait_ge(at_m, a - 1)
                    raw = raw_max[:, a % 2:a % 2 + 1]
                    if layer == 0:
                        dve.tensor_reduce(raw, ps(2 * (i % 2), 0, n), AX, ALU.max).then_inc(at_r, 1)
                    else:
                        t = steps[i][0]
                        near = local_tiles(t)
                        m = len(near) * P
                        dve.tensor_reduce(ctx_max[:, a % 2:a % 2 + 1], ps(2 * (i % 2), m, n), AX, ALU.max)\
                            .then_inc(at_c, 1)
                        dve.wait_ge(at_b, i + 1)
                        dve.wait_ge(at_c, i + 1)
                        dve.tensor_tensor_reduce(ps(2 * (i % 2), 0, m), ps(2 * (i % 2), 0, m), bias_m[:, i % 2, 0:m],
                                                 1.0, ctx_max[:, a % 2:a % 2 + 1], ALU.add, ALU.max,
                                                 raw).then_inc(at_r, 1)
                    between()
                    dve.wait_ge(at_r, a + 1)
                    if layer == 0:
                        dve.tensor_scalar(negm[:, g % 2, h:h + 1], raw_max[:, a % 2:a % 2 + 1], -SCALE,
                                          nsink[:, h:h + 1], ALU.mult, ALU.min).then_inc(at_m, 1)
                    else:
                        dve.tensor_scalar(negm[:, g % 2, h:h + 1], raw_max[:, a % 2:a % 2 + 1], -1.0, None,
                                          ALU.mult).then_inc(at_m, 1)

                def evacuate(i):
                    a, n = a0 + i, s_cols(layer, i)
                    dve.wait_ge(at_t, a + 1)
                    if a >= 2:
                        dve.wait_ge(at_o, a - 1)
                    dve.tensor_copy(prob_t[:, i % 2, 0:n], ps(4, 0, n)).then_inc(at_e, 1)

                def group_end(gi):
                    g = g0 + gi
                    dve.wait_ge(at_o, a0 + 8 * gi + 8)
                    den = rowsum[:, g % 2, :]
                    if layer == 0:
                        dve.wait_ge(at_sink, g + 1)
                        dve.tensor_tensor(sm[:, 2, :], den, sm[:, 1, :], ALU.add).then_inc(at_den, 1)
                        dve.wait_ge(at_den, g + 1)
                        den = sm[:, 2, :]
                    if g:
                        dve.wait_ge(at_on, g)
                    dve.reciprocal(sm[:, 3, :], den).then_inc(at_rinv, 1)
                    dve.wait_ge(at_rinv, g + 1)
                    if g >= 2:
                        dve.wait_ge(at_f, g - 1)
                    dve.tensor_tensor(full[:, 4 * (g % 2):4 * (g % 2) + 4, :].rearrange(
                        "p a n -> p (a n)").rearrange("p (h d) -> p h d", h=8),
                        ps(6 + gi % 2, 0, 512).rearrange("p (h d) -> p h d", h=8), bcast(sm[:, 3, :], 64),
                        ALU.mult).then_inc(at_on, 1)

                def low(gi):
                    t, grp, _ = steps[8 * gi]
                    dve.wait_ge(at_hi, g0 + gi + 1)
                    for f in range(4):
                        dst, order = group_out(layer, t, grp, f)
                        last = dve.tensor_tensor(dst(h_lo), order(ps(6 + gi % 2, f * P, (f + 1) * P)),
                                                 dst(h_hi).bitcast(F32), ALU.subtract)
                    last.then_inc(at_lo, 1)

                def shift(gi):
                    g = g0 + gi
                    dve.wait_ge(at_m, a0 + 8 * gi + 8)
                    if g:
                        dve.wait_ge(at_sink, g)
                    dve.tensor_tensor(sm[:, 0, :], negm[:, g % 2, :], sink[:], ALU.add).then_inc(at_shift, 1)

                n_pairs = len(steps) // 2
                for p in range(n_pairs + 5):
                    earlier = (lambda: evacuate(2 * p - 2)) if 0 < p <= n_pairs else (lambda: None)
                    maximum(2 * p, earlier) if p < n_pairs else earlier()
                    if p < n_pairs:
                        maximum(2 * p + 1, lambda: None)
                    if p % 4 == 3 and p < n_pairs and layer == 0:
                        shift(p // 4)
                    if p % 4 == 2 and p > 4:
                        group_end(p // 4 - 1)
                    if p % 4 == 0 and p > 4:
                        low(p // 4 - 2)
                    if 0 < p <= n_pairs:
                        evacuate(2 * p - 1)

            dve.memset(r_t[32:33, :], 1.0)
            dve.memset(gw[:], 0.0).then_inc(gw_zero, 1)
            dve.wait_ge(ident_in, 16)
            dve.tensor_copy(ident_b[:], ident[:])
            dve.wait_ge(par_in, 16 * 9)
            dve.tensor_scalar(nsink[:], sink[:], -1.0, None, ALU.mult)
            dve.wait_ge(par_turned, 2)
            dve.tensor_copy(bias_col[:], ps(6, 0, 96))
            dve.tensor_copy(par_col[:], ps(7, 0, 84)).then_inc(par_done, 1)
            dve.wait_ge(par_done, 1)
            pre_scale("mix0", 0, range(NT))
            pre_scale("mix0", 1, range(NT))
            accumulate(-1)
            modulation(0, 6)
            modulation(1)
            pre_rest("mix0", range(NT), scaled=2)
            dve.wait_ge(consts_in, 16 * 5)
            dve.tensor_copy(window_b[:], mask_in[:, 0:2 * P])
            dve.tensor_copy(near_b[:].rearrange("p t n -> p (t n)"), mask_in[:, 2 * P:]).then_inc(masks_done, 1)
            accumulate(sp("v0") + KT - 1)
            wait_tm(dve, "v0", NT - 1, KT)
            for t in range(NT):
                dve.tensor_copy(a_v[:, t, :], ps(6, t * P, (t + 1) * P)).then_inc(v_dve, 1)
            for i in range(15):
                s = sp("in0") + i
                if i < 6:
                    dst = (a_q[:, i] if i < 4 else a_k[:, i - 4])[:, 0:SEQ]
                    lat = ps(2 * (i % 2), 0, SEQ)
                    dve.wait_ge(w_used, s + 1)
                    if i:
                        dve.wait_ge(rope_done, i)
                    dve.tensor_tensor(rope_t[:, 0], lat, cos[:], ALU.mult)
                    dve.stream_shuffle(rope_t[:, 1], lat, [(q + 16) % 32 for q in range(32)]).then_inc(fe_dve, 1)
                    dve.wait_ge(fe_dve, i + 1)
                    dve.tensor_tensor(rope_t[:, 1], rope_t[:, 1], sin[:], ALU.mult).then_inc(rope_m, 1)
                    dve.wait_ge(rope_m, i + 1)
                    dve.tensor_tensor(dst, rope_t[:, 0], rope_t[:, 1], ALU.add).then_inc(rope_done, 1)
                elif 10 <= i < 14:
                    dve.wait_ge(fe_act, i + 1)
                    dve.tensor_scalar(b_o[:, i - 10], b_o[:, i - 10], par_col[:, 64 + i - 10:65 + i - 10], None,
                                      ALU.mult).then_inc(bo_done, 1)
                if i in (0, 6, 10):
                    modulation({0: 2, 6: 3, 10: 4}[i])
                accumulate(s + 1)
            attention(0)

            for t in range(NT):
                dve.wait_ge(gl_ln, t + 1)
                dve.scalar_tensor_tensor(la[:, t, :], ps(t, 0, 512), 0.0, la[:, t, :], ALU.min,
                                         ALU.subtract).then_inc(gl_la, 1)
            modulation(5)
            for t in range(NT):
                cols = slice(t * P, (t + 1) * P)
                dve.wait_ge(gl_eq, t + 1)
                dve.tensor_copy(decay[:, 0:2, 2 * t:2 * t + 2], qg[:, 0:2, t * P + CH - 1:(t + 1) * P:CH])
                dve.tensor_copy(decay[:, 2:4, 2 * t:2 * t + 2], qg[:, 2:4, t * P:(t + 1) * P:CH]).then_inc(gl_dec, 1)
                dve.wait_ge(gl_dec, t + 1)
                for d in range(2):
                    last = dve.tensor_tensor(qg[:, 2 * d:2 * d + 2, cols], qg[:, 2 * d:2 * d + 2, cols],
                                             b_q[:, :, cols], ALU.mult)
                last.then_inc(gl_q, 1)
                dve.wait_ge(gl_ek, t + 1)
                for d in range(2):
                    last = dve.tensor_tensor(kg[:, 2 * d:2 * d + 2, cols], kg[:, 2 * d:2 * d + 2, cols],
                                             b_k[:, :, cols], ALU.mult)
                last.then_inc(gl_k, 1)
            for t in range(NT):
                dve.wait_ge(gl_kt, t + 1)
                if t == 0:
                    dve.wait_ge(gl_cum, NT)
                dve.tensor_copy(kg_t[:, t, :], ps(t % 2, 0, 512)).then_inc(gl_ktc, 1)
            dve.wait_ge(gl_dec, NT)
            for i in range(2 * NT - 1):
                dve.wait_ge(gl_ds, i + 1)
                if i:
                    dve.wait_ge(gl_s, 2 * i)
                for d in range(2):
                    m = slice(2 * d, 2 * d + 2)
                    ds = ps(2 + 2 * d + i % 2, 0, 256).rearrange("p (m n) -> p m n", m=2)
                    if i == 0:
                        last = dve.tensor_copy(state[:, 0, m], ds)
                    else:
                        last = dve.tensor_tensor(state[:, i, m], state[:, i - 1, m], ds, ALU.add)
                last.then_inc(gl_u, 1)
                dve.wait_ge(gl_u, i + 1)
                for d, chunk in enumerate((f_order[i], b_order[i])):
                    dve.tensor_tensor(state[:, i, 2 * d:2 * d + 2], state[:, i, 2 * d:2 * d + 2],
                                      bcast(decay[:, 2 * d:2 * d + 2, chunk], P), ALU.mult).then_inc(gl_s, 1)
            fg = b_q[:].rearrange("p a n -> p (a n)")[:, 0:512]
            on = b_k[:].rearrange("p a n -> p (a n)")[:, 0:512]

            def gla_mask(t):
                dve.wait_ge(gl_att, t + 1)
                if t:
                    dve.wait_ge(gl_av, t)
                for d in range(2):
                    m = tri[:, d]
                    m = bass.AP(m.tensor, m.offset, [list(m.ap[0]), [0, 2], [1, P]])
                    for b in range(2):
                        last = dve.tensor_tensor(
                            att_m[:, d].rearrange("p (a b n) -> p b a n", a=2, b=2)[:, b],
                            ps(2 * d + b, 0, 256).rearrange("p (h n) -> p h n", h=2), m, ALU.mult)
                last.then_inc(gl_msk, 1)

            def gla_gate(t):
                dve.wait_ge(gl_f, t + 1)
                cols = slice(t * P, (t + 1) * P)
                if t:
                    dve.wait_ge(gl_lo, t)
                dve.tensor_tensor(fg.rearrange("p (h n) -> p h n", h=4),
                                  ps(4 + 2 * (t % 2), 0, 512).rearrange("p (h n) -> p h n", h=4), b_o[:, :, cols],
                                  ALU.mult).then_inc(gl_full, 1)
                dve.wait_ge(gl_hi, t + 1)
                dve.tensor_tensor(h_lo[:, 4:8, cols], fg.rearrange("p (h n) -> p h n", h=4),
                                  h_hi[:, 4:8, cols].bitcast(F32), ALU.subtract).then_inc(gl_lo, 1)

            gla_mask(0)
            for t in range(NT):
                if t + 1 < NT:
                    gla_mask(t + 1)
                dve.wait_ge(gl_rs, t + 1)
                if t:
                    dve.wait_ge(gl_f, t)
                for b in range(2):
                    last = dve.tensor_tensor(on.rearrange("p (a b n) -> p b a n", a=2, b=2)[:, b],
                                             ps(4 + 2 * (t % 2) + b, 0, 256).rearrange("p (h n) -> p h n", h=2),
                                             bcast(gla_rs[:, t, b:4:2], P), ALU.mult)
                last.then_inc(gl_on, 1)
                if t:
                    gla_gate(t - 1)
            gla_gate(NT - 1)

            for i in range(LT):
                post_norm("out0L", i, i, KT)
            pre_rest("ffn0L", L_TILES)
            for i in range(CT):
                post_norm("out0C", i, LT + i, KT)
            for i in range(CT):
                pre_scale("ffn0C", i, C_TILES)
            ffn_in(("fi0L", 0), FH, SEQ, {3: lambda: pre_rest("ffn0C", C_TILES, scaled=2),
                                          5: lambda: modulation(6), 9: lambda: modulation(7)})
            accumulate(sp(("fo0L", 0)) + FH - 1)
            take_half(("fo0L", 0), FH)
            ffn_in(("fi0L", 1), FH, SEQ, {0: lambda: modulation(8), 5: lambda: modulation(9),
                                          9: lambda: modulation(10)})
            accumulate(sp(("fo0L", 1)) + FH - 1)
            feed(sp("fi0C") + RING - 1)
            add_half(("fo0L", 1), "fo0L", FH)
            feed(sp("fi0C") + RING)
            mix1 = range(NT)
            hooks = {j: (lambda i=j: post_norm("fo0L", i, i)) for j in range(LT)}
            hooks[0] = lambda: (modulation(11), post_norm("fo0L", 0, 0))
            hooks |= {4: lambda: pre_scale("mix1", 0, mix1), 5: lambda: pre_scale("mix1", 1, mix1)}
            for i in range(LT):
                hooks[6 + 2 * i] = lambda i=i: pre_modulate("mix1", i, mix1)
                hooks[7 + 2 * i] = lambda i=i: (pre_scale("mix1", i + 2, mix1) if i + 2 < LT else None,
                                                pre_low("mix1", i, mix1))
            ffn_in("fi0C", FT, CTX, hooks)
            feed(sp("fo0C") + FT - 1)
            for i in range(CT):
                post_norm("fo0C", i, LT + i, FT)
            for i in range(LT, NT):
                pre_scale("mix1", i, mix1)
            for i in range(LT, NT):
                pre_modulate("mix1", i, mix1)
                pre_low("mix1", i, mix1)
            feed(sp("v1C") + KT - 1)
            attention(1)
            for i in range(LT + 3):
                if i < LT:
                    post_norm("out1L", i, i, KT)
                if i > 3:
                    pre_low("ffn1L", i - 4, L_TILES)
                if 0 < i <= LT:
                    pre_scale("ffn1L", i - 1, L_TILES)
                if i > 2:
                    pre_modulate("ffn1L", i - 3, L_TILES)
            pre_low("ffn1L", LT - 1, L_TILES)
            ffn_in(("fi1L", 0), FH, SEQ)
            take_half(("fo1L", 0), FH)
            ffn_in(("fi1L", 1), FH, SEQ)
            add_half(("fo1L", 1), "fo1L", FH)
            for i in range(LT):
                post_norm("fo1L", i, i)

        @block.tensor
        def _(pe):
            readers = {}

            def claim(*banks):
                for b in banks:
                    for s, v in readers.pop(b, ()):
                        pe.wait_ge(s, v)

            def read_by(banks, *who):
                for b in banks:
                    readers[b] = who

            def split_ready(s):
                pe.wait_ge(*low_ready(s))

            def product3(s, sta, mov, outs, first, last, done=None):
                order = [("hi", "hi"), ("hi", "lo"), ("lo", "hi")]
                for n, (x, y) in enumerate(order):
                    for o in outs:
                        mm = pe.matmul(o[0], sta(x, o), mov(y, o), start=first and n == 0, stop=last and n == 2)
                return mm

            def fm_unit(s, outs, done=True):
                split_ready(s)
                w = {"hi": w_hi[:, s % RING], "lo": w_lo[:, s % RING]}
                h = {"hi": h_hi, "lo": h_lo}
                for k in range(KT):
                    mm = product3(s, lambda x, o: w[x][:, k * P:(k + 1) * P],
                                  lambda y, o: h[y][:, k, o[1]:o[1] + o[2]], outs, k == 0, k == KT - 1)
                if done:
                    mm.then_inc(w_used, 1)

            def tm_product(name, n_units, act, tiles, where, ready=None, lead=0, before=None, after=None):
                s0 = sp(name)

                def one(k, i, t):
                    s = s0 + k
                    w = {"hi": w_hi[:, s % RING], "lo": w_lo[:, s % RING]}
                    for x, y in (("hi", "hi"), ("hi", "lo"), ("lo", "hi")):
                        for o, c, n in where(i):
                            mm = pe.matmul(o, act(x, k, t), w[y][:, c:c + n],
                                           start=k == 0 and (x, y) == ("hi", "hi") and first_in_bank(name, i, c),
                                           stop=k == n_units - 1 and x == "lo", skip_group_check=True)
                    if i == len(tiles) - 1:
                        mm.then_inc(w_used, 1)
                    elif k == n_units - 1:
                        mm.then_inc(tm_done, 1)

                for i, t in enumerate(tiles) if lead else ():
                    before(i)
                    for k in range(lead):
                        if i == 0:
                            split_ready(s0 + k)
                        one(k, i, t)
                for k in range(lead, n_units):
                    if ready:
                        ready(k)
                    split_ready(s0 + k)
                    for i, t in enumerate(tiles):
                        if k == 0 and before:
                            before(i)
                        one(k, i, t)
                    if after:
                        after(k)

            def first_in_bank(name, i, c):
                return not (name == "v0" and c == 0 and i not in (0, 4))

            def h_act(x, k, t):
                return (h_hi if x == "hi" else h_lo)[:, k, t * P:(t + 1) * P]

            def two_halves(name):
                return lambda i: [(ps(tm_bank(name, i) + n, 0, 512), 512 * n, 512) for n in range(2)]

            def modulation_rows():
                claim(0, 1)
                for k in range(KT):
                    pe.wait_ge(landed[ring_no[2 * k] % RAW], landed_value[2 * k])
                    for n in range(2):
                        mm = pe.matmul(ps(n, 0, 512, 0, 2), c_col[:, k, :],
                                       w_raw[:, ring_no[2 * k] % RAW, n * 512:(n + 1) * 512], start=k == 0,
                                       stop=k == KT - 1)
                    mm.then_inc(w_direct, 1)
                read_by((0, 1), (mod_copied, 1))

            def turn_rows():
                claim(6)
                pe.wait_ge(mod_copied, 1)
                for k in range(KT):
                    mm = pe.transpose(ps(6, 2 * k, 2 * k + 2), full[0:2, k, :], ident[0:2, 0:2])
                mm.then_inc(mod_turned, 1)
                read_by((6,), (mod_done, 1))

            def modulation(b):
                acc = acc_place(b)
                claim(7)
                pe.wait_ge(w_acc, KT * b)
                for k in range(KT):
                    for v in range(2):
                        mm = pe.matmul(ps(7, 2 * k + v, 2 * k + v + 1), acc[:, v, k * P:(k + 1) * P], one_col[:],
                                       start=True, stop=True)
                mm.then_inc(mod_turned, 1)
                read_by((7,), (mod_done, b + 1))

            def pre_turn(name, tiles):
                for i in tiles:
                    n = PRE[name] + i
                    b = pre_bank(name, n)
                    claim(b, b + 1)
                    pe.wait_ge(pre_xs, n + 1)
                    for k in range(KT):
                        mm = pe.transpose(ps(b, k * P, (k + 1) * P), xs[:, n % 2, k * P:(k + 1) * P], ident[:])
                    mm.then_inc(pre_tr, 1)
                    read_by((b, b + 1), (pre_full, n + 1), (pre_half, n + 1))

            def gate_rows(j, n_lc):
                pe.wait_ge(mod_der, 2 * j + 2)
                for lc in range(n_lc):
                    claim(4 + 2 * lc, 5 + 2 * lc)
                    for k in range(KT):
                        col = gate_col[:, j, lc, k:k + 1]
                        mm = pe.matmul(ps(4 + 2 * lc, k * P, (k + 1) * P),
                                       bass.AP(col.tensor, col.offset, [list(col.ap[0]), [0, P]]), ident[:],
                                       start=True, stop=True)
                    mm.then_inc(gb_ready, 1)
                    read_by((4 + 2 * lc, 5 + 2 * lc), (gb_done, gb_base[j] + lc + 1))

            def ffn_in(name, n_js, col0, width, hooks=None, halves=None):
                s, f0 = sp(name), FI[name]
                for j in range(n_js):
                    f = f0 + j
                    if j == 0 and halves:
                        for half in range(2):
                            pe.wait_ge(pre_lo, PRE[halves] + (half + 1) * LT // 2)
                            for up in range(2):
                                bank = 2 * (f % 2) + up
                                if half == 0:
                                    claim(bank)
                                at, n = half * width // 2, width // 2
                                fm_unit(s + up, [(ps(bank, at, at + n), col0 + at, n)], half == 1)
                                read_by((bank,), (ff_full, f + 1) if up else (ff_silu, f + 1))
                        continue
                    for up in range(2):
                        bank = 2 * (f % 2) + up
                        claim(bank)
                        fm_unit(s + 2 * j + up, [(ps(bank, 0, width), col0, width)])
                        read_by((bank,), (ff_full, f + 1) if up else (ff_silu, f + 1))
                    if hooks and j in hooks:
                        hooks[j]()

            def ffn_out(name, fi, n_units, tiles, width, base):
                f0 = FI[fi]
                hid = {"hi": hid_hi, "lo": hid_lo}
                tm_product(name, n_units,
                           lambda x, k, t: hid[x][:, k * width + (t - base) * P:k * width + (t - base + 1) * P],
                           tiles, two_halves(name), ready=lambda k: pe.wait_ge(ff_lo, f0 + k + 1))

            def attention(layer, start):
                steps, a0, g0 = STEPS[layer], STEP0[layer], GROUP0[layer]
                prob, prob_t = ((prob0, prob0_t), (prob1, prob1_t))[layer]

                def scores(i):
                    t, grp, h = steps[i]
                    sb_ = 2 * (i % 2)
                    claim(sb_, sb_ + 1)
                    head = 8 * grp + h
                    rows = slice(64 * (h % 2), 64 * (h % 2) + 64)
                    if layer == 0:
                        q, kk = a_q[rows, h // 2, t * P:(t + 1) * P], a_k[rows, h // 4]
                    else:
                        q, kk = c_q[rows, head // 2, t * P:(t + 1) * P], c_k[rows, head // 2]
                    near, n = local_tiles(t), 0
                    if near:
                        n = len(near) * P
                        pe.matmul(ps(sb_, 0, n), q, kk[:, near[0] * P:near[0] * P + n], start=True, stop=False,
                                  skip_group_check=True)
                    if layer == 0:
                        for at, u in enumerate(near):
                            if u != t:
                                side = int(u > t)
                                pe.matmul(ps(sb_, at * P, (at + 1) * P), ident_b[:],
                                          window_b[:, side * P:(side + 1) * P], start=False, stop=False,
                                          skip_group_check=True)
                    left, at = CTX, 0
                    while left:
                        m = min(left, 512 - n % 512)
                        mm = pe.matmul(ps(sb_, n, n + m), q, kk[:, SEQ + at:SEQ + at + m],
                                       start=n % 512 == 0, stop=left == m, skip_group_check=True)
                        n, at, left = n + m, at + m, left - m
                    mm.then_inc(at_s, 1)
                    read_by((sb_, sb_ + 1), (at_p, a0 + i + 1))

                def turn(i):
                    a = a0 + i
                    pe.wait_ge(at_p, a + 1)
                    claim(4, 5)
                    for j in range(s_cols(layer, i) // P):
                        mm = pe.transpose(ps(4, j * P, (j + 1) * P), prob[:, i % 2, j * P:(j + 1) * P], ident[:])
                    mm.then_inc(at_t, 1)
                    read_by((4, 5), (at_e, a + 1))

                def values(i):
                    t, grp, h = steps[i]
                    bank = 6 + i // 8 % 2
                    if h == 0:
                        claim(bank)
                    pe.wait_ge(at_e, a0 + i + 1)
                    keys = local_tiles(t) + C_TILES
                    for j, u in enumerate(keys):
                        v = a_v[:, u, 64 * (h // 4):64 * (h // 4) + 64] if layer == 0 else \
                            c_v[:, u, (8 * grp + h) * 64:(8 * grp + h + 1) * 64]
                        mm = pe.matmul(ps(bank, h * 64, h * 64 + 64), prob_t[:, i % 2, j * P:(j + 1) * P], v,
                                       start=h == 0 and j == 0, stop=j == len(keys) - 1, skip_group_check=True)
                    mm.then_inc(at_o, 1)
                    if h == 7:
                        read_by((bank,), (at_on, g0 + i // 8 + 1))

                def turn_group(gi):
                    g = g0 + gi
                    bank = 6 + gi % 2
                    pe.wait_ge(at_on, g + 1)
                    claim(bank)
                    for f in range(4):
                        mm = pe.transpose(ps(bank, f * P, (f + 1) * P), full[:, 4 * (g % 2) + f, :], ident[:])
                    mm.then_inc(at_f, 1)
                    read_by((bank,), (at_lo, g + 1))

                n_pairs = len(steps) // 2
                start(lambda: (scores(0), scores(1)))
                for p in range(1, n_pairs + 4):
                    if p < n_pairs:
                        scores(2 * p)
                    if p <= n_pairs:
                        turn(2 * p - 2)
                    if p < n_pairs:
                        scores(2 * p + 1)
                    if 1 < p <= n_pairs + 1:
                        values(2 * p - 3)
                    if p % 4 == 3 and p > 4:
                        turn_group(p // 4 - 1)
                    if p <= n_pairs:
                        turn(2 * p - 1)
                        values(2 * p - 2)

            pe.wait_ge(par_in, 16 * 9)
            pe.wait_ge(ident_in, 16)
            pe.transpose(ps(6, 0, 96), par_rows[0:96, 0, :], ident[0:96, 0:96]).then_inc(par_turned, 1)
            pe.transpose(ps(7, 0, 84), par_rows[0:84, 1, :], ident[0:84, 0:84]).then_inc(par_turned, 1)
            read_by((6, 7), (par_done, 1))
            pe.wait_ge(c_done, 1)
            modulation_rows()
            pre_turn("mix0", [0, 1])
            turn_rows()
            modulation(1)

            def next_tile(i):
                if i + 2 < NT:
                    pre_turn("mix0", [i + 2])
                pe.wait_ge(pre_lo, i + 1)
                claim(*(i, 6, 7) if i == 0 else (i,))

            tm_product("v0", KT, h_act, range(NT),
                       lambda i: [(ps(6, i * P, (i + 1) * P), 0, AKV), (ps(i, 0, BV), AKV, BV)], lead=RING,
                       before=next_tile)
            for t in range(NT):
                read_by((t,), (v_act, t + 1))
            read_by((6, 7), (v_dve, NT))
            def in0_unit(i):
                bl = in0_bank(i)
                claim(bl, bl + 1)
                fm_unit(sp("in0") + i, [(ps(bl, 0, SEQ), 0, SEQ), (ps(bl + 1, 0, CTX), SEQ, CTX)])
                read_by((bl, bl + 1), (fe_act, i + 1), *([(fe_dve, i + 1)] if i < 6 else []))

            for i in range(14):
                in0_unit(i)
                if i in (0, 6, 10):
                    modulation({0: 2, 6: 3, 10: 4}[i])
            pe.wait_ge(rope_done, 6)
            pe.wait_ge(masks_done, 1)
            attention(0, lambda first: (first(), in0_unit(14)))

            pe.wait_ge(gw_in, 64)
            claim(*range(8))
            for t in range(NT):
                pe.matmul(ps(t, 0, 512), r_t[:, t * P:(t + 1) * P], gw[:], start=True, stop=True).then_inc(gl_z, 1)
                read_by((t,), (gl_la, t + 1))
            modulation(5)
            for t in range(NT):
                claim(6 + t % 2)
                pe.wait_ge(gl_la, t + 1)
                for m in range(4):
                    mm = pe.matmul(ps(6 + t % 2, m * P, (m + 1) * P), la[:, t, m * P:(m + 1) * P], tri[:, m // 2],
                                   start=True, stop=True)
                mm.then_inc(gl_cum, 1)
                read_by((6 + t % 2,), (gl_ek, t + 1))
            for t in range(NT):
                claim(t % 2)
                pe.wait_ge(gl_k, t + 1)
                for m in range(4):
                    mm = pe.transpose(ps(t % 2, m * P, (m + 1) * P), kg[:, m, t * P:(t + 1) * P], ident[:])
                mm.then_inc(gl_kt, 1)
                read_by((t % 2,), (gl_ktc, t + 1))
            pe.wait_ge(gl_ktc, NT)
            for i in range(2 * NT - 1):
                claim(2 + i % 2, 4 + i % 2)
                for m in range(4):
                    bank = 2 + 2 * (m // 2) + i % 2
                    chunk = (f_order, b_order)[m // 2][i]
                    t, rows = chunk // 2, slice(64 * (chunk % 2), 64 * (chunk % 2) + 64)
                    for hh in range(2):
                        head = 2 * (m % 2) + hh
                        mm = pe.matmul(ps(bank, (m % 2) * P, (m % 2 + 1) * P, 64 * hh, 64 * hh + 64),
                                       kg_t[rows, t, m * P + 64 * hh:m * P + 64 * hh + 64],
                                       b_v[rows, t, head * P:(head + 1) * P], start=True, stop=True)
                mm.then_inc(gl_ds, 1)
                read_by((2 + i % 2, 4 + i % 2), (gl_u, i + 1))
            pe.wait_ge(gl_q, NT)

            def gla_scores(t):
                claim(0, 1, 2, 3)
                cols = slice(t * P, (t + 1) * P)
                for d in range(2):
                    for h in range(4):
                        m, rows = 2 * d + h // 2, slice(64 * (h % 2), 64 * (h % 2) + 64)
                        mm = pe.matmul(ps(2 * d + h % 2, (h // 2) * P, (h // 2 + 1) * P), kg[rows, m, cols],
                                       qg[rows, m, cols], start=True, stop=True)
                mm.then_inc(gl_att, 1)
                read_by((0, 1, 2, 3), (gl_msk, t + 1))

            def gla_turn(t):
                bank = 4 + 2 * (t % 2)
                pe.wait_ge(gl_on, t + 1)
                claim(bank)
                on = b_k[:].rearrange("p a n -> p (a n)")
                for h in range(4):
                    mm = pe.transpose(ps(bank, h * P, (h + 1) * P), on[:, h * P:(h + 1) * P], ident[:])
                mm.then_inc(gl_f, 1)
                read_by((bank,), (gl_full, t + 1))

            gla_scores(0)
            pe.wait_ge(gl_s, 2 * (2 * NT - 1))
            for t in range(NT):
                ob = 4 + 2 * (t % 2)
                pe.wait_ge(gl_msk, t + 1)
                if t + 1 < NT:
                    gla_scores(t + 1)
                claim(ob, ob + 1)
                for d in range(2):
                    for h in range(4):
                        mm = pe.matmul(ps(ob + h % 2, (h // 2) * P, (h // 2 + 1) * P),
                                       att_m[:, d, h * P:(h + 1) * P], b_v[:, t, h * P:(h + 1) * P],
                                       start=d == 0 and h < 2, stop=False, skip_group_check=True)
                mm.then_inc(gl_av, 1)
                for d in range(2):
                    for half in range(2):
                        chunk = 2 * t + half
                        i = (f_order, b_order)[d].index(chunk)
                        for h in range(4) if i else ():
                            m, rows = 2 * d + h // 2, slice(64 * (h % 2), 64 * (h % 2) + 64)
                            mm = pe.matmul(ps(ob + h % 2, (h // 2) * P, (h // 2 + 1) * P, 64 * half, 64 * half + 64),
                                           qg[rows, m, chunk * CH:(chunk + 1) * CH], state[rows, i - 1, m, :],
                                           start=False, stop=d == 1, skip_group_check=True)
                mm.then_inc(gl_o, 1)
                read_by((ob, ob + 1), (gl_on, t + 1))
                if t:
                    gla_turn(t - 1)
            gla_turn(NT - 1)

            gate_rows(0, 2)
            claim(*range(8))
            pe.wait_ge(gl_lo, NT)
            pe.wait_ge(at_lo, NT)
            tm_product("out0L", KT, h_act, L_TILES, two_halves("out0L"))
            for i in range(LT):
                b = tm_bank("out0L", i)
                read_by((b, b + 1), (post_n, POST["out0L"] + i + 1))
            tm_product("out0C", KT, h_act, C_TILES, two_halves("out0C"), before=lambda i: claim(4 + 2 * i, 5 + 2 * i),
                       after=lambda k: pre_turn("ffn0L", [k - 4]) if k >= 4 else None)
            for i in range(CT):
                read_by((4 + 2 * i, 5 + 2 * i), (post_n, POST["out0C"] + i + 1))
            ffn_in(("fi0L", 0), FH, 0, SEQ, {3: lambda: pre_turn("ffn0C", range(CT)), 4: lambda: gate_rows(1, 2),
                    5: lambda: modulation(6), 9: lambda: modulation(7)}, "ffn0L")
            claim(*range(8))
            ffn_out(("fo0L", 0), ("fi0L", 0), FH, L_TILES, SEQ, 0)
            for i in range(LT):
                read_by((2 * i, 2 * i + 1), (half_done, i + 1))
            ffn_in(("fi0L", 1), FH, 0, SEQ, {0: lambda: modulation(8), 5: lambda: modulation(9),
                                             9: lambda: modulation(10)})
            claim(*range(8))
            ffn_out(("fo0L", 1), ("fi0L", 1), FH, L_TILES, SEQ, 0)
            for i in range(LT):
                read_by((2 * i, 2 * i + 1), (post_y, i + 1))
            hooks = {0: lambda: modulation(11)}
            hooks |= {5 + 2 * i: (lambda i=i: pre_turn("mix1", [i])) for i in range(LT)}
            ffn_in("fi0C", FT, SEQ, CTX, hooks)
            claim(0, 1, 2, 3)
            ffn_out("fo0C", "fi0C", FT, C_TILES, CTX, LT)
            for i in range(CT):
                read_by((2 * i, 2 * i + 1), (post_n, POST["fo0C"] + i + 1))

            pe.wait_ge(pre_lo, PRE["mix1"] + LT)
            for i in range(16):
                bank = qk_bank(i)
                if i < KT:
                    claim(bank)
                    outs = [(ps(bank, 0, SEQ), 0, SEQ)]
                else:
                    claim(bank, bank + 1)
                    pe.wait_ge(pre_lo, PRE["mix1"] + NT)
                    outs = [(ps(bank, 0, SEQ), 0, SEQ), (ps(bank + 1, 0, CTX), SEQ, CTX)]
                fm_unit(sp("qk1") + i, outs)
                read_by((bank,) if i < KT else (bank, bank + 1), (fe1_act, i + 1))
                if i == 3:
                    pre_turn("mix1", C_TILES)
            gate_rows(2, 1)
            claim(*range(8))
            tm_product("v1L", KT, h_act, L_TILES, two_halves("v1L"))
            for i in range(LT):
                read_by((2 * i, 2 * i + 1), (v_act, NT + i + 1))
            pe.wait_ge(fe1_act, 16)

            def context_values(first_scores):
                claim(4, 5, 6, 7)
                tm_product("v1C", KT, h_act, C_TILES, two_halves("v1C"),
                           after=lambda k: first_scores() if k == 5 else None)
                for i in range(CT):
                    read_by((4 + 2 * i, 5 + 2 * i), (v_act, NT + LT + i + 1))

            attention(1, context_values)
            claim(*range(8))
            pe.wait_ge(at_lo, n_groups[0] + n_groups[1])
            tm_product("out1L", KT, h_act, L_TILES, two_halves("out1L"))
            for i in range(LT):
                read_by((2 * i, 2 * i + 1), (post_n, POST["out1L"] + i + 1))
            pre_turn("ffn1L", range(LT))
            ffn_in(("fi1L", 0), FH, 0, SEQ, {4: lambda: gate_rows(3, 1)}, "ffn1L")
            claim(*range(8))
            ffn_out(("fo1L", 0), ("fi1L", 0), FH, L_TILES, SEQ, 0)
            for i in range(LT):
                read_by((2 * i, 2 * i + 1), (half_done, LT + i + 1))
            ffn_in(("fi1L", 1), FH, 0, SEQ)
            claim(*range(8))
            ffn_out(("fo1L", 1), ("fi1L", 1), FH, L_TILES, SEQ, 0)


INPUTS = ["x", "c", "ctx", "c_ctx", "w_mod", "b_mod", "g_mix_pre", "g_mix_post", "g_ffn_pre", "g_ffn_post", "w_ffn_in",
          "w_ffn_out", "ab_w_in", "ab_w_out", "a_sink", "gla_gate_f_w", "gla_gate_f_b", "gla_gate_b_w",
          "gla_gate_b_b", "gla_norm_g", "na_w_in", "na_w_out"]


def kernel(**inputs):
    import concourse.bacc as bacc
    from concourse.bass_utils import run_bass_kernel_spmd

    nc = bacc.Bacc("TRN2", target_bir_lowering=False, num_devices=1, dynamic_dma_scratch_size=1024)
    arrays = {name: np.ascontiguousarray(inputs[name]) for name in INPUTS}
    arrays["rel_rev"] = np.ascontiguousarray(np.pad(np.asarray(inputs["na_rel_bias"]).reshape(-1), BIAS_PAD)[::-1])
    arrays |= constants()
    handles = {name: nc.dram_tensor(f"in_{name}", v.shape, mybir.dt.from_np(v.dtype), kind="ExternalInput").ap()
               for name, v in arrays.items()}
    out = nc.dram_tensor("out_y", (1, SEQ, D), F32, kind="ExternalOutput").ap()
    build(nc, handles, out)
    r = run_bass_kernel_spmd(nc, [{f"in_{name}": v for name, v in arrays.items()}], core_ids=[0])
    return r.results[0]["out_y"]
```
